# Optimizing a Trainium2 kernel written in Bass

```python
import math
import jax, jax.numpy as jnp
from jax import lax
import numpy as np

D_MODEL = 1024
BATCH = 1
SEQ = 2048
DEPTH = 1

CHUNK = 64
N_MIXERS = 3
PLE_DIM = 256
D_FF = 4 * D_MODEL
NORM_EPS = 1e-6
SSM_GROUP = 16
SSM_GROUPS = D_MODEL // SSM_GROUP
SSM_STATE = 64
DT_MIN = 1e-3
DT_MAX = 1e-1
CONV_WIDTH = 3
FOX_HEAD_DIM = 64
FOX_HEADS = D_MODEL // FOX_HEAD_DIM
Q_BLOCK = 128

N_SSM_LAYERS = len(range(0, DEPTH, N_MIXERS))
N_CONV_LAYERS = len(range(1, DEPTH, N_MIXERS))
N_FOX_LAYERS = len(range(2, DEPTH, N_MIXERS))


def rmsnorm(x, gain):
    xf = x.astype(jnp.float32)
    out = xf * lax.rsqrt(jnp.mean(xf * xf, axis=-1, keepdims=True) + NORM_EPS) * gain.astype(jnp.float32)
    return out.astype(x.dtype)

def s5_mixer(u, lam_re, lam_im, log_dt, b_re, b_im, c_re, c_im, d_skip, w_glu):
    f32 = jnp.float32
    bsz, seqlen, _ = u.shape
    uf = u.astype(f32)
    ug = uf.reshape(bsz, seqlen, SSM_GROUPS, SSM_GROUP)
    lr = lam_re.astype(f32)
    li = lam_im.astype(f32)
    dt = jnp.exp(log_dt.astype(f32))[:, None]
    mag = jnp.exp(lr * dt)
    ab_re = mag * jnp.cos(li * dt)
    ab_im = mag * jnp.sin(li * dt)
    nr = ab_re - 1.0
    ni = ab_im
    den = lr * lr + li * li
    coef_re = (nr * lr + ni * li) / den
    coef_im = (ni * lr - nr * li) / den
    br = b_re.astype(f32)
    bi = b_im.astype(f32)
    bb_re = coef_re[..., None] * br - coef_im[..., None] * bi
    bb_im = coef_re[..., None] * bi + coef_im[..., None] * br
    bu_re = jnp.einsum('blgh,gph->blgp', ug, bb_re)
    bu_im = jnp.einsum('blgh,gph->blgp', ug, bb_im)
    a_re = jnp.broadcast_to(ab_re, (1, seqlen, SSM_GROUPS, SSM_STATE))
    a_im = jnp.broadcast_to(ab_im, (1, seqlen, SSM_GROUPS, SSM_STATE))

    def combine(left, right):
        a1r, a1i, b1r, b1i = left
        a2r, a2i, b2r, b2i = right
        return (a2r * a1r - a2i * a1i,
                a2r * a1i + a2i * a1r,
                a2r * b1r - a2i * b1i + b2r,
                a2r * b1i + a2i * b1r + b2i)

    _, _, xs_re, xs_im = lax.associative_scan(combine, (a_re, a_im, bu_re, bu_im), axis=1)
    y = (jnp.einsum('blgp,ghp->blgh', xs_re, c_re.astype(f32))
         - jnp.einsum('blgp,ghp->blgh', xs_im, c_im.astype(f32)))
    y = y.reshape(bsz, seqlen, D_MODEL) + d_skip.astype(f32) * uf
    y = jax.nn.gelu(y).astype(u.dtype)
    a, g = jnp.split(y @ w_glu, 2, axis=-1)
    return a * jax.nn.sigmoid(g)

def short_conv_mixer(h, w_in, conv_w, w_out):
    b_gate, c_gate, v = jnp.split(h @ w_in, 3, axis=-1)
    z = c_gate * v
    rhs = conv_w[:, None, :].astype(z.dtype)
    conv = lax.conv_general_dilated(
        z, rhs, window_strides=(1,), padding=[(CONV_WIDTH - 1, 0)],
        dimension_numbers=('NWC', 'WIO', 'NWC'), feature_group_count=D_MODEL)
    return (b_gate * conv) @ w_out

def fox_mixer(h, w_in, b_f, w_out):
    f32 = jnp.float32
    bsz, seqlen, _ = h.shape
    proj = h @ w_in
    q, k, v, f_logit = jnp.split(proj, [D_MODEL, 2 * D_MODEL, 3 * D_MODEL], axis=-1)
    q = q.reshape(bsz, seqlen, FOX_HEADS, FOX_HEAD_DIM)
    k = k.reshape(bsz, seqlen, FOX_HEADS, FOX_HEAD_DIM)
    v = v.reshape(bsz, seqlen, FOX_HEADS, FOX_HEAD_DIM)
    log_f = jax.nn.log_sigmoid(f_logit.astype(f32) + b_f.astype(f32))
    cum = jnp.cumsum(log_f, axis=1).transpose(0, 2, 1)
    scale = FOX_HEAD_DIM ** -0.5
    outs = []
    for blk in range(seqlen // Q_BLOCK):
        q0 = blk * Q_BLOCK
        kv_len = q0 + Q_BLOCK
        s = jnp.einsum('bqhd,bkhd->bhqk', q[:, q0:kv_len], k[:, :kv_len]).astype(f32) * scale
        decay = cum[:, :, q0:kv_len, None] - cum[:, :, None, :kv_len]
        causal = (q0 + jnp.arange(Q_BLOCK))[:, None] >= jnp.arange(kv_len)[None, :]
        s = jnp.where(causal, s + decay, -jnp.inf)
        pr = jax.nn.softmax(s, axis=-1).astype(v.dtype)
        outs.append(jnp.einsum('bhqk,bkhd->bqhd', pr, v[:, :kv_len]))
    o = jnp.concatenate(outs, axis=1).reshape(bsz, seqlen, D_MODEL)
    return o @ w_out

def sqrelu_mlp(h, w1, w2):
    a = jax.nn.relu(h @ w1)
    return (a * a) @ w2

def first_inputs(seed: int = 0) -> dict:
    key = jax.random.key(seed)
    ks = jax.random.split(key, 26)
    f32 = jnp.float32
    nrm = lambda k, shape, s: jax.random.normal(k, shape, f32) * s
    gain = lambda k, shape: 1.0 + 0.05 * jax.random.normal(k, shape, f32)
    ns, nc, nf = N_SSM_LAYERS, N_CONV_LAYERS, N_FOX_LAYERS
    G, P, H = SSM_GROUPS, SSM_STATE, SSM_GROUP
    lam_im_init = jnp.broadcast_to(jnp.arange(P, dtype=f32) * math.pi, (ns, G, P))
    return {
        "x": nrm(ks[0], (BATCH, SEQ, D_MODEL), 1.0),
        "p": nrm(ks[1], (DEPTH, BATCH, SEQ, PLE_DIM), 1.0),
        "norm_mix": gain(ks[2], (DEPTH, D_MODEL)),
        "norm_ffn": gain(ks[3], (DEPTH, D_MODEL)),
        "norm_ple": gain(ks[4], (DEPTH, D_MODEL)),
        "norm_final": gain(ks[5], (D_MODEL,)),
        "ssm_lam_re": -0.5 + 0.01 * jax.random.normal(ks[6], (ns, G, P), f32),
        "ssm_lam_im": lam_im_init + 0.01 * jax.random.normal(ks[7], (ns, G, P), f32),
        "ssm_log_dt": jax.random.uniform(ks[8], (ns, G), f32, math.log(DT_MIN), math.log(DT_MAX)),
        "ssm_b_re": nrm(ks[9], (ns, G, P, H), (2 * H) ** -0.5),
        "ssm_b_im": nrm(ks[10], (ns, G, P, H), (2 * H) ** -0.5),
        "ssm_c_re": nrm(ks[11], (ns, G, H, P), (2 * P) ** -0.5),
        "ssm_c_im": nrm(ks[12], (ns, G, H, P), (2 * P) ** -0.5),
        "ssm_d": nrm(ks[13], (ns, D_MODEL), 1.0),
        "ssm_w_glu": nrm(ks[14], (ns, D_MODEL, 2 * D_MODEL), D_MODEL ** -0.5),
        "conv_w_in": nrm(ks[15], (nc, D_MODEL, 3 * D_MODEL), D_MODEL ** -0.5),
        "conv_w": nrm(ks[16], (nc, CONV_WIDTH, D_MODEL), CONV_WIDTH ** -0.5),
        "conv_w_out": nrm(ks[17], (nc, D_MODEL, D_MODEL), D_MODEL ** -0.5),
        "fox_w_in": nrm(ks[18], (nf, D_MODEL, 3 * D_MODEL + FOX_HEADS), D_MODEL ** -0.5),
        "fox_b_f": 3.0 + 0.5 * jax.random.normal(ks[19], (nf, FOX_HEADS), f32),
        "fox_w_out": nrm(ks[20], (nf, D_MODEL, D_MODEL), D_MODEL ** -0.5),
        "mlp_w1": nrm(ks[21], (DEPTH, D_MODEL, D_FF), D_MODEL ** -0.5),
        "mlp_w2": nrm(ks[22], (DEPTH, D_FF, D_MODEL), D_FF ** -0.5),
        "ple_w": nrm(ks[23], (DEPTH, PLE_DIM, D_MODEL), PLE_DIM ** -0.5),
        "ple_gate_w": nrm(ks[24], (DEPTH, D_MODEL, D_MODEL), D_MODEL ** -0.5),
    }

def first_block(x, p, norm_mix, norm_ffn, norm_ple, norm_final,
              ssm_lam_re, ssm_lam_im, ssm_log_dt, ssm_b_re, ssm_b_im, ssm_c_re, ssm_c_im,
              ssm_d, ssm_w_glu, conv_w_in, conv_w, conv_w_out, fox_w_in, fox_b_f, fox_w_out,
              mlp_w1, mlp_w2, ple_w, ple_gate_w):
    for i in range(DEPTH):
        kind, slot = i % N_MIXERS, i // N_MIXERS
        h = rmsnorm(x, norm_mix[i])
        if kind == 0:
            mix = s5_mixer(h, ssm_lam_re[slot], ssm_lam_im[slot], ssm_log_dt[slot],
                           ssm_b_re[slot], ssm_b_im[slot], ssm_c_re[slot], ssm_c_im[slot],
                           ssm_d[slot], ssm_w_glu[slot])
        elif kind == 1:
            mix = short_conv_mixer(h, conv_w_in[slot], conv_w[slot], conv_w_out[slot])
        else:
            mix = fox_mixer(h, fox_w_in[slot], fox_b_f[slot], fox_w_out[slot])
        x = x + mix
        x = x + sqrelu_mlp(rmsnorm(x, norm_ffn[i]), mlp_w1[i], mlp_w2[i])
        gate = jax.nn.sigmoid(rmsnorm(x, norm_ple[i]) @ ple_gate_w[i])
        x = x + (p[i] @ ple_w[i]) * gate
    return rmsnorm(x, norm_final)


D_MIX = D_MODEL
EPS = 1e-6
NEG = -1e30

ATT_HEAD_DIM = 64
D_ATT = D_MIX // 4
ATT_HEADS = D_ATT // ATT_HEAD_DIM
ATT_LEFT_CHUNKS = 8
ATT_BAND = (ATT_LEFT_CHUNKS + 1) * CHUNK
MAX_REL = 128
N_REL = 2 * MAX_REL + 1

D_ML = D_MIX // 2
ML_HEADS = 4
ML_HEAD_DIM = D_ML // ML_HEADS
ML_CONV = 4

D_CONV = D_MIX - D_ATT - D_ML
CONV_WIDTH_2 = 31

IN_SIZES = (D_ATT, D_ATT, D_ATT, D_ATT,
            D_ML, D_ML, D_ML, D_ML, D_ML,
            ML_HEADS, ML_HEADS,
            D_CONV, D_CONV, D_CONV)
D_IN = 4 * D_ATT + 5 * D_ML + 2 * ML_HEADS + 3 * D_CONV


def split_columns(h):
    parts = []
    off = 0
    for s in IN_SIZES:
        parts.append(h[..., off:off + s])
        off += s
    return parts

def rms_norm(x, g):
    xf = x.astype(jnp.float32)
    y = xf * lax.rsqrt(jnp.mean(xf * xf, axis=-1, keepdims=True) + EPS)
    return (y * g.astype(jnp.float32)).astype(x.dtype)

def layer_norm(x, g, b):
    xf = x.astype(jnp.float32)
    mu = jnp.mean(xf, axis=-1, keepdims=True)
    xc = xf - mu
    y = xc * lax.rsqrt(jnp.mean(xc * xc, axis=-1, keepdims=True) + EPS)
    return (y * g.astype(jnp.float32) + b.astype(jnp.float32)).astype(x.dtype)

def causal_depthwise_conv(x, w, b):
    width, ch = w.shape
    xp = jnp.pad(x, ((0, 0), (width - 1, 0), (0, 0)))
    out = lax.conv_general_dilated(
        xp, w[:, None, :].astype(x.dtype), window_strides=(1,), padding='VALID',
        dimension_numbers=('NWC', 'WIO', 'NWC'), feature_group_count=ch)
    return out + b.astype(x.dtype)

def chunk_band_attention(q, k, v, q_g, k_g, rel_bias):
    B, S, H, Dh = q.shape
    n_chunks = S // CHUNK
    pad = ATT_LEFT_CHUNKS * CHUNK
    q = rms_norm(q, q_g)
    k = rms_norm(k, k_g)
    kp = jnp.pad(k, ((0, 0), (pad, 0), (0, 0), (0, 0)))
    vp = jnp.pad(v, ((0, 0), (pad, 0), (0, 0), (0, 0)))
    rel = jnp.arange(CHUNK)[:, None] - jnp.arange(ATT_BAND)[None, :] + pad
    rel_idx = jnp.clip(rel, -MAX_REL, MAX_REL) + MAX_REL
    bias = rel_bias[:, rel_idx].astype(jnp.float32)
    scale = Dh ** -0.5
    qc = q.reshape(B, n_chunks, CHUNK, H, Dh).transpose(1, 0, 3, 2, 4)

    def one_chunk(args):
        c, qb = args
        start = c * CHUNK
        kb = lax.dynamic_slice_in_dim(kp, start, ATT_BAND, axis=1)
        vb = lax.dynamic_slice_in_dim(vp, start, ATT_BAND, axis=1)
        s = jnp.einsum('bhqd,bkhd->bhqk', qb, kb,
                       preferred_element_type=jnp.float32) * scale + bias
        key_pos = start - pad + jnp.arange(ATT_BAND)
        s = jnp.where(key_pos[None, None, None, :] >= 0, s, NEG)
        p = jax.nn.softmax(s, axis=-1).astype(vb.dtype)
        return jnp.einsum('bhqk,bkhd->bqhd', p, vb)

    out = lax.map(one_chunk, (jnp.arange(n_chunks), qc))
    return out.transpose(1, 0, 2, 3, 4).reshape(B, S, H * Dh)

def mlstm_chunkwise(q, k, v, i_pre, f_pre):
    B, S, H, D = q.shape
    n_chunks = S // CHUNK
    f32 = jnp.float32

    def chunks4(a):
        return a.astype(f32).reshape(B, n_chunks, CHUNK, H, D).transpose(1, 0, 3, 2, 4)

    def chunks3(a):
        return a.astype(f32).reshape(B, n_chunks, CHUNK, H).transpose(1, 0, 3, 2)

    qc = chunks4(q)
    kc = chunks4(k) * (D ** -0.5)
    vc = chunks4(v)
    ic = chunks3(i_pre)
    lfc = chunks3(jax.nn.log_sigmoid(f_pre.astype(f32)))
    causal = jnp.tril(jnp.ones((CHUNK, CHUNK), dtype=bool))

    def step(carry, xs):
        C, n, m = carry
        qb, kb, vb, ib, lfb = xs
        b = jnp.cumsum(lfb, axis=-1)
        log_d = b[..., :, None] - b[..., None, :] + ib[..., None, :]
        log_d = jnp.where(causal, log_d, NEG)
        inter = b + m[..., None]
        m_t = jnp.maximum(jnp.max(log_d, axis=-1), inter)
        d_mat = jnp.exp(log_d - m_t[..., None])
        inter_w = jnp.exp(inter - m_t)
        s = jnp.einsum('bhtd,bhsd->bhts', qb, kb) * d_mat
        num = (jnp.einsum('bhts,bhsd->bhtd', s, vb)
               + inter_w[..., None] * jnp.einsum('bhvk,bhtk->bhtv', C, qb))
        den = jnp.sum(s, axis=-1) + inter_w * jnp.einsum('bhk,bhtk->bht', n, qb)
        h = num / jnp.maximum(jnp.abs(den), jnp.exp(-m_t))[..., None]
        b_last = b[..., -1]
        w_log = b_last[..., None] - b + ib
        m_new = jnp.maximum(b_last + m, jnp.max(w_log, axis=-1))
        decay = jnp.exp(b_last + m - m_new)
        w = jnp.exp(w_log - m_new[..., None])
        C_new = decay[..., None, None] * C + jnp.einsum('bhs,bhsv,bhsk->bhvk', w, vb, kb)
        n_new = decay[..., None] * n + jnp.einsum('bhs,bhsk->bhk', w, kb)
        return (C_new, n_new, m_new), h

    init = (jnp.zeros((B, H, D, D), f32), jnp.zeros((B, H, D), f32), jnp.zeros((B, H), f32))
    _, hs = lax.scan(step, init, (qc, kc, vc, ic, lfc))
    return hs.transpose(1, 0, 3, 2, 4).reshape(B, S, H, D)

def second_inputs(seed: int = 0) -> dict:
    key = jax.random.key(seed)
    ks = jax.random.split(key, 17)
    f32 = jnp.float32
    nrm = lambda k, shape: jax.random.normal(k, shape, f32)
    return {
        "x": nrm(ks[0], (BATCH, SEQ, D_MODEL)),
        "norm_g": 1.0 + 0.02 * nrm(ks[1], (DEPTH, D_MODEL)),
        "w_in": nrm(ks[2], (DEPTH, D_MODEL, D_IN)) * D_MODEL ** -0.5,
        "att_q_g": 1.0 + 0.02 * nrm(ks[3], (DEPTH, ATT_HEAD_DIM)),
        "att_k_g": 1.0 + 0.02 * nrm(ks[4], (DEPTH, ATT_HEAD_DIM)),
        "att_rel_bias": 0.1 * nrm(ks[5], (DEPTH, ATT_HEADS, N_REL)),
        "ml_qk_conv_w": nrm(ks[6], (DEPTH, ML_CONV, 2 * D_ML)) * ML_CONV ** -0.5,
        "ml_qk_conv_b": 0.02 * nrm(ks[7], (DEPTH, 2 * D_ML)),
        "ml_b_i": 0.1 * nrm(ks[8], (DEPTH, ML_HEADS)),
        "ml_b_f": jnp.linspace(3.0, 6.0, ML_HEADS, dtype=f32)[None, :]
                  + 0.1 * nrm(ks[9], (DEPTH, ML_HEADS)),
        "ml_out_g": 1.0 + 0.02 * nrm(ks[10], (DEPTH, D_ML)),
        "cv_dw_w": nrm(ks[11], (DEPTH, CONV_WIDTH_2, D_CONV)) * CONV_WIDTH_2 ** -0.5,
        "cv_dw_b": 0.02 * nrm(ks[12], (DEPTH, D_CONV)),
        "cv_ln_g": 1.0 + 0.02 * nrm(ks[13], (DEPTH, D_CONV)),
        "cv_ln_b": 0.02 * nrm(ks[14], (DEPTH, D_CONV)),
        "w_out": nrm(ks[15], (DEPTH, D_MIX, D_MODEL)) * D_MIX ** -0.5,
    }

def second_block(x, norm_g, w_in, att_q_g, att_k_g, att_rel_bias, ml_qk_conv_w, ml_qk_conv_b,
              ml_b_i, ml_b_f, ml_out_g, cv_dw_w, cv_dw_b, cv_ln_g, cv_ln_b, w_out):
    B, S, _ = x.shape
    for l in range(DEPTH):
        h = rms_norm(x, norm_g[l])
        proj = jnp.einsum('bsd,de->bse', h, w_in[l])
        (a_q, a_k, a_v, a_z, m_q, m_k, m_v, m_o, m_z, m_i, m_f,
         c_a, c_b, c_z) = split_columns(proj)

        att = chunk_band_attention(
            a_q.reshape(B, S, ATT_HEADS, ATT_HEAD_DIM),
            a_k.reshape(B, S, ATT_HEADS, ATT_HEAD_DIM),
            a_v.reshape(B, S, ATT_HEADS, ATT_HEAD_DIM),
            att_q_g[l], att_k_g[l], att_rel_bias[l])
        att = att * jax.nn.silu(a_z)

        qk = jax.nn.silu(causal_depthwise_conv(jnp.concatenate([m_q, m_k], axis=-1),
                                               ml_qk_conv_w[l], ml_qk_conv_b[l]))
        m_q, m_k = qk[..., :D_ML], qk[..., D_ML:]
        i_pre = m_i.astype(jnp.float32) + ml_b_i[l].astype(jnp.float32)
        f_pre = m_f.astype(jnp.float32) + ml_b_f[l].astype(jnp.float32)
        hm = mlstm_chunkwise(
            m_q.reshape(B, S, ML_HEADS, ML_HEAD_DIM),
            m_k.reshape(B, S, ML_HEADS, ML_HEAD_DIM),
            m_v.reshape(B, S, ML_HEADS, ML_HEAD_DIM), i_pre, f_pre)
        hm = jax.nn.sigmoid(m_o.astype(jnp.float32)).reshape(B, S, ML_HEADS, ML_HEAD_DIM) * hm
        hm = rms_norm(hm, ml_out_g[l].reshape(ML_HEADS, ML_HEAD_DIM).astype(jnp.float32))
        ml = hm.reshape(B, S, D_ML).astype(x.dtype) * jax.nn.silu(m_z)

        u = c_a * jax.nn.sigmoid(c_b)
        u = causal_depthwise_conv(u, cv_dw_w[l], cv_dw_b[l])
        u = jax.nn.silu(layer_norm(u, cv_ln_g[l], cv_ln_b[l]))
        cv = u * jax.nn.silu(c_z)

        mixed = jnp.concatenate([att.astype(x.dtype), ml, cv.astype(x.dtype)], axis=-1)
        x = x + jnp.einsum('bse,ed->bsd', mixed, w_out[l])
    return x


_first_inputs = second_inputs


def second_inputs(seed=0):
    import zlib

    import numpy as np

    out = dict(_first_inputs(seed))
    spreads = {}
    factors = {'norm_g': 3.236,
     'att_q_g': 8.0,
     'att_k_g': 8.0,
     'att_rel_bias': 8.0,
     'ml_qk_conv_b': 8.0,
     'ml_b_i': 8.0,
     'ml_out_g': 7.112,
     'cv_dw_b': 8.0,
     'cv_ln_g': 8.0,
     'cv_ln_b': 8.0}
    for name, (base, spread) in spreads.items():
        noise = np.random.default_rng([zlib.crc32(name.encode()), seed]).standard_normal(out[name].shape)
        drawn = base * np.exp(spread * noise) if base else spread * noise
        out[name] = __import__('jax').numpy.asarray(drawn.astype(out[name].dtype))
    for name, factor in factors.items():
        out[name] = (out[name] * factor).astype(out[name].dtype)
    return out


_narrow_inputs = second_inputs


def second_inputs(seed=0):

    out = dict(_narrow_inputs(seed))
    wider = {'att_rel_bias': 3.86,
     'ml_qk_conv_b': 5.47,
     'ml_b_i': 12.0,
     'ml_out_g': 3.65,
     'cv_ln_g': 6.41,
     'cv_ln_b': 6.99}
    for name, times in wider.items():
        mean = out[name].mean()
        out[name] = (mean + times * (out[name] - mean)).astype(out[name].dtype)
    return out


def setup_inputs(seed=0):
    out = dict(first_inputs(seed))
    for name, value in second_inputs(seed + 1).items():
        if name != "x":
            out[name + "_2"] = value
    return out


def reference(
    x, p, norm_mix, norm_ffn, norm_ple, norm_final, ssm_lam_re, ssm_lam_im, ssm_log_dt,
    ssm_b_re, ssm_b_im, ssm_c_re, ssm_c_im, ssm_d, ssm_w_glu, conv_w_in, conv_w, conv_w_out,
    fox_w_in, fox_b_f, fox_w_out, mlp_w1, mlp_w2, ple_w, ple_gate_w, norm_g_2, w_in_2,
    att_q_g_2, att_k_g_2, att_rel_bias_2, ml_qk_conv_w_2, ml_qk_conv_b_2, ml_b_i_2, ml_b_f_2,
    ml_out_g_2, cv_dw_w_2, cv_dw_b_2, cv_ln_g_2, cv_ln_b_2, w_out_2,
):
    x = first_block(
        x, p, norm_mix, norm_ffn, norm_ple, norm_final, ssm_lam_re, ssm_lam_im, ssm_log_dt,
        ssm_b_re, ssm_b_im, ssm_c_re, ssm_c_im, ssm_d, ssm_w_glu, conv_w_in, conv_w, conv_w_out,
        fox_w_in, fox_b_f, fox_w_out, mlp_w1, mlp_w2, ple_w, ple_gate_w,
    )
    return second_block(
        x, norm_g_2, w_in_2, att_q_g_2, att_k_g_2, att_rel_bias_2, ml_qk_conv_w_2,
        ml_qk_conv_b_2, ml_b_i_2, ml_b_f_2, ml_out_g_2, cv_dw_w_2, cv_dw_b_2, cv_ln_g_2,
        cv_ln_b_2, w_out_2,
    )


_drawn_inputs = setup_inputs


def setup_inputs(seed=0):
    import zlib

    import numpy as np

    out = dict(_drawn_inputs(seed))
    spreads = {}
    factors = {'norm_ple': 2.747, 'ssm_lam_re': 8.0, 'ml_b_i_2': 5.173}
    for name, (base, spread) in spreads.items():
        noise = np.random.default_rng([zlib.crc32(name.encode()), seed]).standard_normal(out[name].shape)
        drawn = base * np.exp(spread * noise) if base else spread * noise
        out[name] = __import__('jax').numpy.asarray(drawn.astype(out[name].dtype))
    for name, factor in factors.items():
        out[name] = (out[name] * factor).astype(out[name].dtype)
    return out
```

```python
from contextlib import ExitStack

import concourse.bass as bass
from concourse import mybir

ALU = mybir.AluOpType
ACT = mybir.ActivationFunctionType
AX = mybir.AxisListType
F32 = mybir.dt.float32
F32R = mybir.dt.float32r

P = 128
SEQ = 2048
D = 1024
EPS = 1e-6
TWO_PI = 6.283185307179586
PI_LOW = 3.1415925
PI2_A, PI2_B = 6.28125, 0.0019350051879882812
PI2_C = TWO_PI - PI2_A - PI2_B
ROUND = 1.5 * 2.0 ** 23


def tools(nc, ctx):
    held = []

    def release():
        nc.clear_and_free_semaphores(held)
        nc.all_engine_barrier()

    ctx.callback(release)

    def sb(name, shape, dt=F32):
        return ctx.enter_context(nc.sbuf_tensor(name, shape, dt))

    def ps(name, shape):
        return ctx.enter_context(nc.psum_tensor(name, shape, F32))

    def sem(name):
        held.append(nc.alloc_semaphore(name))
        return held[-1]

    return sb, ps, sem


T = 16
NCH = SEQ // T
NP = 32
H = 16
S8 = 8
QP = 4
NQ = NP // QP
QS = 2
NS = NP // QS


def s5_setup(nc, env, d, ctx):
    sb, ps, sem = tools(nc, ctx)
    U, Win, ident = env["U"], env["Win"], env["ident"]
    aT, eps = env["aT"], env["eps"]
    prm = sb("s5_prm", [P, 3, NP])
    bc = sb("s5_bc", [P, 4, NP, H])
    gain = sb("s5_gain", [P, NP, H])
    skip = sb("s5_skip", [2 * H, 2, NP])
    xin = sb("s5_xin", [P, 2, D])
    junk = sb("s5_junk", [P, D])
    ss = sb("s5_ss", [P, T])
    rms = sb("s5_rms", [P, T])
    rexp = sb("s5_rexp", [P, 2, S8, H])
    rtile = sb("s5_rtile", [P, 2, NCH])
    w = sb("s5_w", [P, 16, NP])
    pw = sb("s5_pw", [P, 2, NP, T + 1])
    pwr = sb("s5_pwr", [P, 2, NP, T])
    bb = sb("s5_bb", [P, 2, NP, H])
    bbd = sb("s5_bbd", [P, 2, NP, 2, H])
    ca = sb("s5_ca", [P, 2, QS, T + 1, H])
    cat = sb("s5_cat", [P, 2, QS, T + 1, H])
    ab = sb("s5_ab", [P, 2, QS, T, H])
    tmp = sb("s5_tmp", [P, 4, NP, H])
    bt, pt = tmp, tmp
    abt = sb("s5_abt", [P, 2, QS, T, H])
    zs = sb("s5_zs", [2 * H, QS, T * H])
    zz = sb("s5_zz", [2 * H, NP, H])
    eyeh = sb("s5_eyeh", [2 * H, H])
    zero = sb("s5_zero", [P, (S8 - 1) * H])
    pst = ps("s5_pst", [P, 4, NCH])
    psz = [ps(f"s5_psz{i}", [2 * H, 2, T * H]) for i in range(2)]
    psw = [ps(f"s5_psw{i}", [P, 4, P]) for i in range(2)]
    ld_prm, ld_u = sem("s5_ld_prm"), sem("s5_ld_u")
    ld_x = [sem("s5_ld_x0"), sem("s5_ld_x1")]
    act_prm, sq_done, rms_sqrt = sem("s5_act_prm"), sem("s5_sq_done"), sem("s5_rms_sqrt")
    dve_prm, dve_rms, r_copied = sem("s5_dve_prm"), sem("s5_dve_rms"), sem("s5_r_copied")
    rexp_done, r_turned = sem("s5_rexp_done"), sem("s5_r_turned")
    chain, pchain = sem("s5_chain"), sem("s5_pchain")
    bb_ready, ca_ready, ab_ready = sem("s5_bb_ready"), sem("s5_ca_ready"), sem("s5_ab_ready")
    z_mm, ab_turned, z_ready, win_ready = sem("s5_z_mm"), sem("s5_ab_turned"), sem("s5_z_ready"), sem("s5_win_ready")
    st_ca, st_z, st_zero, zero_set, pool_set = sem("s5_st_ca"), sem("s5_st_z"), sem("s5_st_zero"), sem("s5_zero_set"), sem("s5_pool_set")
    pw_ready, ca_free, u_done = sem("s5_pw_ready"), sem("s5_ca_free"), sem("s5_u_done")

    with nc.Block() as block:
        @block.sync
        def _(sp):
            sp.dma_start(prm[:], d["s5_prm"]).then_inc(ld_prm, 16)
            sp.dma_start(bc[:], d["s5_bc"]).then_inc(ld_prm, 16)
            sp.dma_start(gain[:], d["s5_gain"]).then_inc(ld_prm, 16)
            sp.dma_start(skip[:], d["s5_skip"]).then_inc(ld_prm, 16)
            for i in range(T):
                if i >= 2:
                    sp.wait_ge(sq_done, i - 1)
                sp.dma_start(xin[:, i % 2], d["x_chunk"][:, i]).then_inc(ld_x[i % 2], 16)
            for hf in range(2):
                sp.dma_start(U[:, hf], d["x_group"][:, hf]).then_inc(ld_u, 16)
            sp.wait_ge(zero_set, 1)
            for i in range(2):
                sp.dma_start(d["z"][:, i * 512:(i + 1) * 512, 0:(S8 - 1) * H].rearrange("o (a b) n -> (o a) b n", a=P),
                             zero[:, None, :].to_broadcast([P, 4, (S8 - 1) * H])).then_inc(st_zero, 16)
            for q in range(NS):
                sp.wait_ge(ca_ready, q + 1)
                lo = q % (QP // QS) * QS
                sp.dma_start(d["ca"][:, q // (QP // QS)].rearrange("p (r j n) -> p r j n", r=2, j=QP)[:, :, lo:lo + QS],
                             ca[:].rearrange("p r j t h -> p r j (t h)")).then_inc(st_ca, 16)
                sp.wait_ge(z_ready, q + 1)
                sp.dma_start(d["z"][0].rearrange("(j g) n -> g j n", g=2 * H)[:, q * QS:(q + 1) * QS, (S8 - 1) * H:],
                             zs[:]).then_inc(st_z, 16)
            sp.wait_ge(st_ca, 16 * NS)
            sp.wait_ge(st_z, 16 * NS)
            sp.wait_ge(st_zero, 32)

        @block.scalar
        def _(act):
            act.wait_ge(ld_prm, 64)
            act.activation(w[:, 0], prm[:, 2], ACT.Exp).then_inc(act_prm, 1)
            act.wait_ge(dve_prm, 1)
            act.activation(w[:, 2], w[:, 1], ACT.Exp).then_inc(act_prm, 1)
            act.wait_ge(dve_prm, 2)
            act.activation(w[:, 8], w[:, 7], ACT.Sin).then_inc(act_prm, 1)
            act.activation(w[:, 9], w[:, 7], ACT.Abs).then_inc(act_prm, 1)
            act.wait_ge(act_prm, 4)
            act.activation(w[:, 10], w[:, 9], ACT.Sin, scale=-1.0, bias=env["halfpi"][:]).then_inc(act_prm, 1)
            for i in range(T):
                act.wait_ge(ld_x[i % 2], 16 * (i // 2 + 1))
                if i:
                    act.wait_ge(sq_done, i)
                act.activation(junk[:], xin[:, i % 2], ACT.Square, accum_out=ss[:, i:i + 1]).then_inc(sq_done, 1)
            act.wait_ge(sq_done, T)
            act.activation(rms[:], ss[:], ACT.Sqrt, scale=1.0 / D, bias=eps[:]).then_inc(rms_sqrt, 1)
            act.wait_ge(r_turned, 2)
            act.copy(rtile[:], pst[:, 0:2]).then_inc(r_copied, 1)
            for j in range(NP):
                act.wait_ge(ab_turned, j + 1)
                act.copy(Win[:, j].rearrange("p a b m -> p (a b) m"), psw[j % 2][:]).then_inc(win_ready, 1)

        @block.vector
        def _(dve):
            n = [0]

            def then(ins):
                n[0] += 1
                ins.then_inc(chain, 1)
                dve.wait_ge(chain, n[0])

            dve.wait_ge(ld_prm, 64)
            dve.wait_ge(act_prm, 1)
            dve.tensor_tensor(w[:, 1], prm[:, 0], w[:, 0], ALU.mult).then_inc(dve_prm, 1)
            then(dve.tensor_tensor(w[:, 3], prm[:, 1], w[:, 0], ALU.mult))
            then(dve.tensor_scalar(w[:, 4], w[:, 3], 1.0 / TWO_PI, ROUND, ALU.mult, ALU.add))
            then(dve.tensor_scalar(w[:, 5], w[:, 4], ROUND, None, ALU.subtract))
            then(dve.scalar_tensor_tensor(w[:, 6], w[:, 5], -PI2_A, w[:, 3], ALU.mult, ALU.add))
            then(dve.scalar_tensor_tensor(w[:, 3], w[:, 5], -PI2_B, w[:, 6], ALU.mult, ALU.add))
            then(dve.scalar_tensor_tensor(w[:, 6], w[:, 5], -PI2_C, w[:, 3], ALU.mult, ALU.add))
            dve.tensor_scalar(w[:, 7], w[:, 6], PI_LOW, -PI_LOW, ALU.min, ALU.max).then_inc(dve_prm, 1)
            dve.wait_ge(act_prm, 5)
            a1r, a1i = pw[:, 0, :, 1], pw[:, 1, :, 1]
            then(dve.tensor_tensor(a1r, w[:, 2], w[:, 10], ALU.mult))
            then(dve.tensor_tensor(a1i, w[:, 2], w[:, 8], ALU.mult))
            then(dve.memset(pw[:, 0, :, 0:1], 1.0))
            then(dve.memset(pw[:, 1, :, 0:1], 0.0))
            lr, li = prm[:, 0], prm[:, 1]
            then(dve.tensor_scalar(w[:, 0], a1r, -1.0, None, ALU.add))
            then(dve.tensor_tensor(w[:, 3], lr, lr, ALU.mult))
            then(dve.tensor_tensor(w[:, 4], li, li, ALU.mult))
            then(dve.tensor_tensor(w[:, 5], w[:, 3], w[:, 4], ALU.add))
            then(dve.reciprocal(w[:, 6], w[:, 5]))
            then(dve.tensor_tensor(w[:, 3], w[:, 0], lr, ALU.mult))
            then(dve.tensor_tensor(w[:, 4], a1i, li, ALU.mult))
            then(dve.tensor_tensor(w[:, 5], w[:, 3], w[:, 4], ALU.add))
            then(dve.tensor_tensor(w[:, 11], w[:, 5], w[:, 6], ALU.mult))
            then(dve.tensor_tensor(w[:, 3], a1i, lr, ALU.mult))
            then(dve.tensor_tensor(w[:, 4], w[:, 0], li, ALU.mult))
            then(dve.tensor_tensor(w[:, 5], w[:, 3], w[:, 4], ALU.subtract))
            then(dve.tensor_tensor(w[:, 12], w[:, 5], w[:, 6], ALU.mult))
            cr = w[:, 11, :, None].to_broadcast([P, NP, H])
            ci = w[:, 12, :, None].to_broadcast([P, NP, H])
            then(dve.tensor_tensor(bt[:, 0], bc[:, 0], cr, ALU.mult))
            then(dve.tensor_tensor(bt[:, 1], bc[:, 1], ci, ALU.mult))
            then(dve.tensor_tensor(bt[:, 2], bc[:, 1], cr, ALU.mult))
            then(dve.tensor_tensor(bt[:, 3], bc[:, 0], ci, ALU.mult))
            then(dve.tensor_tensor(bt[:, 0], bt[:, 0], bt[:, 1], ALU.subtract))
            then(dve.tensor_tensor(bt[:, 2], bt[:, 2], bt[:, 3], ALU.add))
            then(dve.tensor_tensor(bb[:, 0], bt[:, 0], gain[:], ALU.mult))
            then(dve.tensor_tensor(bb[:, 1], bt[:, 2], gain[:], ALU.mult))
            m = 1
            while m < T:
                lo_r, lo_i = pw[:, 0, :, 1:m + 1], pw[:, 1, :, 1:m + 1]
                tr = pw[:, 0, :, m:m + 1].to_broadcast([P, NP, m])
                ti = pw[:, 1, :, m:m + 1].to_broadcast([P, NP, m])
                then(dve.tensor_tensor(pt[:, 0, :, 0:m], lo_r, tr, ALU.mult))
                then(dve.tensor_tensor(pt[:, 1, :, 0:m], lo_i, ti, ALU.mult))
                then(dve.tensor_tensor(pt[:, 2, :, 0:m], lo_r, ti, ALU.mult))
                then(dve.tensor_tensor(pt[:, 3, :, 0:m], lo_i, tr, ALU.mult))
                then(dve.tensor_tensor(pw[:, 0, :, m + 1:2 * m + 1], pt[:, 0, :, 0:m], pt[:, 1, :, 0:m], ALU.subtract))
                then(dve.tensor_tensor(pw[:, 1, :, m + 1:2 * m + 1], pt[:, 2, :, 0:m], pt[:, 3, :, 0:m], ALU.add))
                m *= 2
            for s in range(T):
                then(dve.tensor_copy(pwr[:, :, :, s], pw[:, :, :, T - 1 - s]))
            then(dve.tensor_copy(aT[:, 0], pw[:, 0, :, T]))
            then(dve.tensor_copy(aT[:, 1], pw[:, 1, :, T]))
            then(dve.memset(bbd[:], 0.0))
            for g in range(2):
                rows = slice(g * 64, (g + 1) * 64)
                then(dve.tensor_copy(bbd[rows, :, :, g, :], bb[rows]))
            dve.tensor_scalar(w[:, 13], w[:, 11], 0.0, None, ALU.add).then_inc(bb_ready, 1)
            dve.wait_ge(pool_set, 2)
            then(dve.tensor_tensor(w[0:2 * H, 14], skip[:, 0], skip[:, 1], ALU.mult))
            then(dve.tensor_tensor(zz[:], eyeh[:, None, :].to_broadcast([2 * H, NP, H]),
                                   w[0:2 * H, 14, :, None].to_broadcast([2 * H, NP, H]), ALU.mult))
            dve.wait_ge(rms_sqrt, 1)
            then(dve.reciprocal(ss[:], rms[:]))
            dve.tensor_copy(rexp[:].rearrange("p a s h -> p (a s) h"),
                            ss[:, :, None].to_broadcast([P, T, H])).then_inc(rexp_done, 1)
            for q in range(NS):
                js = slice(q * QS, (q + 1) * QS)
                shape = [P, QS, T + 1, H]
                c_r = bc[:, 2, js, None, :].to_broadcast(shape)
                c_i = bc[:, 3, js, None, :].to_broadcast(shape)
                p_r = pw[:, 0, js, :, None].to_broadcast(shape)
                p_i = pw[:, 1, js, :, None].to_broadcast(shape)
                if q:
                    dve.wait_ge(st_ca, 16 * q)
                    dve.wait_ge(z_mm, q)
                then(dve.tensor_tensor(cat[:, 0], c_r, p_r, ALU.mult))
                then(dve.tensor_tensor(cat[:, 1], c_i, p_i, ALU.mult))
                then(dve.tensor_tensor(ca[:, 0], cat[:, 0], cat[:, 1], ALU.subtract))
                then(dve.tensor_tensor(cat[:, 0], c_r, p_i, ALU.mult))
                then(dve.tensor_tensor(cat[:, 1], c_i, p_r, ALU.mult))
                dve.scalar_tensor_tensor(ca[:, 1], cat[:, 0], -1.0, cat[:, 1], ALU.mult, ALU.subtract).then_inc(ca_ready, 1)
                dve.wait_ge(ca_ready, q + 1)
                dve.wait_ge(z_mm, q + 1)
                if q:
                    dve.wait_ge(st_z, 16 * q)
                out = zs[:].rearrange("p j (t h) -> p j t h", h=H)
                src = psz[q % 2][:].rearrange("p j (t h) -> p j t h", h=H)
                then(dve.tensor_copy(out[:, :, 1:], src[:, :, 1:]))
                dve.tensor_tensor(out[:, :, 0], src[:, :, 0], zz[:, js], ALU.add).then_inc(z_ready, 1)
                if q < 2:
                    dve.wait_ge(r_copied, 1)
                    dve.wait_ge(ld_u, 32)
                    dve.tensor_tensor(U[:, q], U[:, q], rtile[:, q, None, :].to_broadcast([P, 2 * NP, NCH]),
                                      ALU.mult).then_inc(u_done, 1)

        @block.gpsimd
        def _(pool):
            n = [0]

            def then(ins):
                n[0] += 1
                ins.then_inc(pchain, 1)
                pool.wait_ge(pchain, n[0])

            pool.memset(zero[:], 0.0).then_inc(zero_set, 1)
            pool.memset(eyeh[:], 0.0).then_inc(pool_set, 1)
            pool.wait_ge(pool_set, 1)
            then(pool.affine_select(out=eyeh[:], in_=eyeh[:], compare_op=ALU.not_equal, fill=1.0, base=0,
                                    pattern=[[-1, H]], channel_multiplier=1))
            pool.affine_select(out=eyeh[:], in_=eyeh[:], compare_op=ALU.not_equal, fill=1.0, base=-H,
                               pattern=[[-1, H]], channel_multiplier=1).then_inc(pool_set, 1)
            pool.wait_ge(bb_ready, 1)
            for q in range(NS):
                js = slice(q * QS, (q + 1) * QS)
                shape = [P, QS, T, H]
                b_r = bb[:, 0, js, None, :].to_broadcast(shape)
                b_i = bb[:, 1, js, None, :].to_broadcast(shape)
                p_r = pwr[:, 0, js, :, None].to_broadcast(shape)
                p_i = pwr[:, 1, js, :, None].to_broadcast(shape)
                then(pool.tensor_tensor(abt[:, 0], b_r, p_r, ALU.mult))
                then(pool.tensor_tensor(abt[:, 1], b_i, p_i, ALU.mult))
                if q:
                    pool.wait_ge(ab_turned, QS * q)
                then(pool.tensor_tensor(ab[:, 0], abt[:, 0], abt[:, 1], ALU.subtract))
                then(pool.tensor_tensor(abt[:, 0], b_r, p_i, ALU.mult))
                then(pool.tensor_tensor(abt[:, 1], b_i, p_r, ALU.mult))
                pool.tensor_tensor(ab[:, 1], abt[:, 0], abt[:, 1], ALU.add).then_inc(ab_ready, 1)
                pool.wait_ge(ab_ready, q + 1)

        @block.tensor
        def _(pe):
            pe.wait_ge(rexp_done, 1)
            for hf in range(2):
                pe.transpose(pst[:, hf], rexp[:, hf].rearrange("p s h -> p (s h)"), ident[:]).then_inc(r_turned, 1)
            for q in range(NS):
                pe.wait_ge(ca_ready, q + 1)
                if q >= 2:
                    pe.wait_ge(z_ready, q - 1)
                for jj in range(QS):
                    for ri in range(2):
                        last = pe.matmul(psz[q % 2][:, jj], bbd[:, ri, q * QS + jj].rearrange("p g h -> p (g h)"),
                                         ca[:, ri, jj, 0:T].rearrange("p t h -> p (t h)"),
                                         start=(ri == 0), stop=(ri == 1))
                last.then_inc(z_mm, 1)
                pe.wait_ge(ab_ready, q + 1)
                for jj in range(QS):
                    j = q * QS + jj
                    if j >= 2:
                        pe.wait_ge(win_ready, j - 1)
                    for hf in range(2):
                        for ri in range(2):
                            last = pe.transpose(psw[j % 2][:, 2 * hf + ri],
                                                ab[:, ri, jj, hf * S8:(hf + 1) * S8].rearrange("p s h -> p (s h)"), ident[:])
                    last.then_inc(ab_turned, 1)


def s5_states(nc, env, d, ctx):
    sb, ps, sem = tools(nc, ctx)
    U, Win, aT, xs = env["U"], env["Win"], env["aT"], env["xs"]
    SC, SU = 8, NCH // 8
    t1 = sb("s5_t1", [P, 2, NP, SU])
    t2 = sb("s5_t2", [P, 2, NP, SU])
    ap = sb("s5_ap", [P, 2, NP, SU])
    ani = sb("s5_ani", [P, NP])
    psx = [ps(f"s5_psx{i}", [P, 2, 2, NCH]) for i in range(4)]
    x_mm, x_copied, chain, xs_zero = sem("s5_x_mm"), sem("s5_x_copied"), sem("s5_scan"), sem("s5_xs_zero")
    with nc.Block() as block:
        @block.tensor
        def _(pe):
            for i in range(NP // 2):
                if i >= 4:
                    pe.wait_ge(x_copied, i - 3)
                for jj in range(2):
                    j = 2 * i + jj
                    for g in range(2):
                        for ri in range(2):
                            for hf in range(2):
                                last = pe.matmul(psx[i % 4][g * 64:(g + 1) * 64, ri, jj],
                                                 Win[:, j, hf, ri, g * 64:(g + 1) * 64], U[:, hf, 2 * j + g],
                                                 start=(hf == 0), stop=(hf == 1))
                last.then_inc(x_mm, 1)

        @block.scalar
        def _(act):
            for i in range(NP // 2):
                act.wait_ge(x_mm, i + 1)
                act.copy(xs[:, :, 2 * i:2 * i + 2, 1:NCH + 1], psx[i % 4][:]).then_inc(x_copied, 1)

        @block.vector
        def _(dve):
            n = [0]

            def then(ins):
                n[0] += 1
                ins.then_inc(chain, 1)
                dve.wait_ge(chain, n[0])

            def times(out, v, ar, ai, shape, tmp):
                then(dve.tensor_tensor(out[0], v[0], ar, ALU.mult))
                then(dve.tensor_tensor(out[1], v[1], ar, ALU.mult))
                then(dve.tensor_tensor(tmp[0], v[1], ai, ALU.mult))
                then(dve.tensor_tensor(tmp[1], v[0], ai, ALU.mult))
                then(dve.tensor_tensor(out[0], out[0], tmp[0], ALU.subtract))
                then(dve.tensor_tensor(out[1], out[1], tmp[1], ALU.add))

            then(dve.memset(xs[:, :, :, 0:1], 0.0))
            then(dve.tensor_copy(ap[:, :, :, 0], aT[:]))
            m = 1
            while m < SU:
                shape = [P, NP, m]
                times([ap[:, r, :, m:2 * m] for r in range(2)], [ap[:, r, :, 0:m] for r in range(2)],
                      ap[:, 0, :, m - 1:m].to_broadcast(shape), ap[:, 1, :, m - 1:m].to_broadcast(shape), shape,
                      [t2[:, r, :, 0:m] for r in range(2)])
                m *= 2
            dve.wait_ge(x_copied, NP // 2)
            view = [xs[:, r, :, 1:].rearrange("p j (c u) -> p j c u", u=SU) for r in range(2)]
            shape = [P, NP, SC]
            ar, ai = (aT[:, r, :, None].to_broadcast(shape) for r in range(2))
            for u in range(1, SU):
                o = [t1[:, r, :, 0:SC] for r in range(2)]
                times(o, [view[r][:, :, :, u - 1] for r in range(2)], ar, ai, shape, [t2[:, r, :, 0:SC] for r in range(2)])
                for r in range(2):
                    then(dve.tensor_tensor(view[r][:, :, :, u], view[r][:, :, :, u], o[r], ALU.add))
            shape = [P, NP, SU]
            for c in range(1, SC):
                o = [t1[:, r] for r in range(2)]
                v = [xs[:, r, :, c * SU:c * SU + 1].to_broadcast(shape) for r in range(2)]
                times(o, v, ap[:, 0], ap[:, 1], shape, [t2[:, r] for r in range(2)])
                for r in range(2):
                    then(dve.tensor_tensor(view[r][:, :, c], view[r][:, :, c], o[r], ALU.add))


def s5_outputs(nc, env, d, ctx):
    sb, ps, sem = tools(nc, ctx)
    U, xs, ident = env["U"], env["xs"], env["ident"]
    G8 = 2 * QP
    mt = sb("s5_mt", [P, 2, G8, T * H])
    ca = sb("s5_cao", [P, 2, 2, QP, (T + 1) * H])
    yc = sb("s5_yc", [P, 2, T, P])
    yh = sb("s5_yh", [P, 2, SEQ], F32R)
    yl = sb("s5_yl", [P, 2, SEQ], F32R)
    psy = [ps(f"s5_psy{i}", [P, 2, T * H]) for i in range(4)]
    psq = [ps(f"s5_psq{i}", [P, 4, NCH]) for i in range(4)]
    ld_m = [sem("s5_ld_m0"), sem("s5_ld_m1")]
    ld_c = [sem("s5_ld_c0"), sem("s5_ld_c1")]
    y_mm, gelu_done, y_turned, hi_done, lo_done = (sem("s5_" + x) for x in ("y_mm", "gelu_done", "y_turned", "hi_done", "lo_done"))
    st_y = [sem("s5_st_y0"), sem("s5_st_y1")]
    with nc.Block() as block:
        @block.sync
        def _(sp):
            def load(q):
                if q >= 2:
                    sp.wait_ge(y_mm, 2 * (q - 1))
                for s in range(S8):
                    lo = (S8 - 1 - s) * H
                    sp.dma_start(mt[s * H:(s + 1) * H, q % 2],
                                 d["z"][0].rearrange("(g h) n -> h g n", h=H)[:, q * G8:(q + 1) * G8, lo:lo + T * H]
                                 ).then_inc(ld_m[q % 2], 16)
                sp.dma_start(ca[:, q % 2].rearrange("p r j n -> p (r j n)"), d["ca"][:, q]).then_inc(ld_c[q % 2], 16)

            load(0)
            load(1)
            for q in range(NQ):
                sp.wait_ge(hi_done, 4 * (q + 1))
                sp.dma_start(d["y_hi"][q], yh[:, q % 2].bitcast(F32)).then_inc(st_y[q % 2], 16)
                sp.wait_ge(lo_done, 4 * (q + 1))
                sp.dma_start(d["y_lo"][q], yl[:, q % 2].bitcast(F32)).then_inc(st_y[q % 2], 16)
                if q + 2 < NQ:
                    load(q + 2)
            for i in range(2):
                sp.wait_ge(st_y[i], 32 * (NQ // 2))

        @block.tensor
        def _(pe):
            def outputs(q):
                pe.wait_ge(ld_m[q % 2], 16 * S8 * (q // 2 + 1))
                pe.wait_ge(ld_c[q % 2], 16 * (q // 2 + 1))
                for pr in range(2):
                    if q:
                        pe.wait_ge(gelu_done, 4 * (q - 1) + 2 * pr + 2)
                    for jj in (2 * pr, 2 * pr + 1):
                        j = q * QP + jj
                        for g in range(2):
                            o, m = psy[2 * pr + g][:, jj % 2], mt[:, q % 2, 2 * jj + g]
                            rows = slice(g * 64, (g + 1) * 64)
                            pe.matmul(o, U[:, 0, 2 * j + g], m, start=True, stop=False)
                            pe.matmul(o[:, T * H // 2:], U[:, 1, 2 * j + g], m[:, 0:T * H // 2], start=False, stop=False)
                            for ri in range(2):
                                last = pe.matmul(o, xs[rows, ri, j, 0:NCH], ca[rows, q % 2, ri, jj, H:],
                                                 start=False, stop=(ri == 1))
                    last.then_inc(y_mm, 1)

            def turn(q):
                pe.wait_ge(gelu_done, 4 * (q + 1))
                for i in range(4):
                    if q:
                        pe.wait_ge(lo_done, 4 * (q - 1) + i + 1)
                    for t in range(4):
                        last = pe.transpose(psq[i][:, t], yc[:, q % 2, 4 * i + t], ident[:])
                    last.then_inc(y_turned, 1)

            for q in range(NQ + 1):
                if q < NQ:
                    outputs(q)
                if q:
                    turn(q - 1)

        @block.scalar
        def _(act):
            for q in range(NQ + 1):
                if q < NQ:
                    for pr in range(2):
                        act.wait_ge(y_mm, 2 * q + pr + 1)
                        if q >= 2:
                            act.wait_ge(y_turned, 4 * (q - 1))
                        for g in range(2):
                            act.activation(yc[:, q % 2].rearrange("p t (j g h) -> p j g t h", h=H, g=2)[:, 2 * pr:2 * pr + 2, g],
                                           psy[2 * pr + g][:].rearrange("p j (t h) -> p j t h", h=H),
                                           ACT.Gelu_apprx_tanh).then_inc(gelu_done, 1)
                if q:
                    r = q - 1
                    for i in range(4):
                        act.wait_ge(y_turned, 4 * r + i + 1)
                        if r >= 2:
                            act.wait_ge(st_y[r % 2], 32 * (r // 2))
                        act.copy(yh[:, r % 2].rearrange("p (c t) -> p t c", t=T)[:, 4 * i:4 * i + 4],
                                 psq[i][:]).then_inc(hi_done, 1)

        @block.vector
        def _(dve):
            for q in range(NQ):
                for i in range(4):
                    dve.wait_ge(hi_done, 4 * q + i + 1)
                    view = (slice(None), slice(4 * i, 4 * i + 4))
                    dve.tensor_tensor(yl[:, q % 2].rearrange("p (c t) -> p t c", t=T)[view], psq[i][:],
                                      yh[:, q % 2].rearrange("p (c t) -> p t c", t=T)[view].bitcast(F32),
                                      ALU.subtract).then_inc(lo_done, 1)


def constants(nc, env, ctx):
    sb, ps, sem = tools(nc, ctx)
    env["ident"] = ident = sb("ident", [P, P])
    env["eps"] = eps = sb("eps", [P, 1])
    env["halfpi"] = halfpi = sb("halfpi", [P, 1])
    made = sem("consts_made")
    with nc.Block() as block:
        @block.gpsimd
        def _(pool):
            pool.memset(ident[:], 0.0).then_inc(made, 1)
            pool.memset(eps[:], EPS)
            pool.memset(halfpi[:], TWO_PI / 4)
            pool.wait_ge(made, 1)
            pool.affine_select(out=ident[:], in_=ident[:], compare_op=ALU.not_equal, fill=1.0, base=0,
                               pattern=[[-1, P]], channel_multiplier=1)


def s5_stage(nc, env, d):
    with ExitStack() as stage:
        env["U"] = stage.enter_context(nc.sbuf_tensor("s5_U", [P, 2, 2 * NP, NCH], F32))
        env["aT"] = stage.enter_context(nc.sbuf_tensor("s5_aT", [P, 2, NP], F32))
        with ExitStack() as win:
            env["Win"] = win.enter_context(nc.sbuf_tensor("s5_Win", [P, NP, 2, 2, P], F32, side="right"))
            with ExitStack() as ctx:
                s5_setup(nc, env, d, ctx)
            env["xs"] = stage.enter_context(nc.sbuf_tensor("s5_xs", [P, 2, NP, NCH + 1], F32))
            with ExitStack() as ctx:
                s5_states(nc, env, d, ctx)
        with ExitStack() as ctx:
            s5_outputs(nc, env, d, ctx)


NB = 2
TB = SEQ // NB
KD = D // P
F_GROUPS, F_TILES = 8, 4
N_GLU, N_MLP, N_PLE, N_FM, N_TM = 2 * KD, F_GROUPS * 2 * F_TILES, 2 * KD, 20, 14
TILE_MLP = N_GLU
TILE_PLE = TILE_MLP + N_MLP
TILE_FM = TILE_PLE + N_PLE
TILE_TM = TILE_FM + N_FM
N_TILE = TILE_TM + N_TM
JOB_STAT1 = N_GLU
JOB_MLP = JOB_STAT1 + 1
JOB_STAT2 = JOB_MLP + F_GROUPS * (F_TILES + KD)
JOB_PLE = JOB_STAT2 + 1
JOB_STAT3 = JOB_PLE + N_PLE
JOB_FM = JOB_STAT3 + 2
JOB_GI = JOB_FM + N_FM
JOB_TM = JOB_GI + 2
TM_COLS = [256, 512, 512, 512]
TM_JOBS = [2, 4, 4, 4]
N_JOB = JOB_TM + sum(TM_JOBS)
N_COPY = N_JOB - JOB_FM
N_XADD = KD + KD * F_GROUPS + KD
assert N_TILE % 2 == 0 and N_JOB % 4 == 0


def dense(nc, env, d, ctx):
    sb, ps, sem = tools(nc, ctx)
    ident, eps = env["ident"], env["eps"]
    X = sb("X", [P, KD, TB])
    Tt = sb("Tt", [P, KD, TB])
    t_at = nc.sbuf_base - KD * TB * 4
    AH, AL = sb("AH", [P, KD, TB], F32R), sb("AL", [P, KD, TB], F32R)
    FH, FL = sb("FH", [P, F_TILES, TB], F32R), sb("FL", [P, F_TILES, TB], F32R)
    WR = [sb(f"WR{i}", [P, TB]) for i in range(2)]
    WH = [sb(f"WH{i}", [P, TB], F32R) for i in range(2)]
    WL = [sb(f"WL{i}", [P, TB], F32R) for i in range(2)]
    SG = [sb(f"SG{i}", [P, 2, TB // 2]) for i in range(2)]
    V = [sb(f"V{i}", [P, 2, TB // 2]) for i in range(2)]
    RB = sb("RB", [P, TB])
    ones = sb("ones_d", [P, P])
    gains = sb("gains", [P, 4, KD])
    gwr = sb("gwr", [P, KD, 8])
    gwh, gwl = sb("gwh", [P, KD, 8], F32R), sb("gwl", [P, KD, 8], F32R)
    GH = [FH[:].rearrange("p a b -> p (a b)").rearrange("p (k n) -> p k n", k=KD), None]
    GL = [FL[:].rearrange("p a b -> p (a b)").rearrange("p (k n) -> p k n", k=KD), None]
    GH[1] = nc.alloc_sbuf_tensor_at("TH", [P, KD, 512], F32R, offset=t_at)[:]
    GL[1] = nc.alloc_sbuf_tensor_at("TL", [P, KD, 512], F32R, offset=t_at + KD * 512 * 4)[:]
    ps4 = [ps(f"ps_job{i}", [P, 2, TB // 2]) for i in range(4)]

    raw_loaded = [sem("raw_loaded0"), sem("raw_loaded1")]
    hi_done, raw_free = sem("w_hi_done"), sem("w_raw_free")
    job_done, sg_done, mix_done, xadd = sem("job_done"), sem("sg_done"), sem("mix_done"), sem("x_added")
    sq_done, acc_done, ln_done, r_done = sem("sq_done"), sem("acc_done"), sem("ln_done"), sem("r_done")
    t_done, ah_done, al_done, xfin = sem("t_done"), sem("ah_done"), sem("al_done"), sem("x_final")
    relu_done, v_done, fh_done, fl_done = sem("relu_done"), sem("v_done"), sem("fh_done"), sem("fl_done")
    ld_x, ld_y, ld_p, ld_g = sem("ld_x"), sem("ld_y"), sem("ld_p"), sem("ld_gains")
    ph_done, pl_done, gh_done, gl_done, ones_set = sem("ph_done"), sem("pl_done"), sem("gh_done"), sem("gl_done"), sem("ones_set")
    x_stored = sem("x_stored")
    copied, st_out, st_x = sem("copied"), [sem("st_out0"), sem("st_out1")], sem("st_x")
    halves = lambda v: v.rearrange("p (a b) -> p a b", a=2)

    with nc.Block() as block:
        @block.sync
        def _(sp):
            sp.dma_start(gains[:], d["gains"]).then_inc(ld_g, 16)
            sp.dma_start(gwr[:], d["w_gi"]).then_inc(ld_g, 16)

            def load(w, tile, s, n):
                free, at = (w + 1, tile) if n == 0 else (sp.snap(w + 1), sp.snap(tile, min_val=0, max_val=N_TILE - 1))
                sp.wait_ge(raw_free, free)
                tile = bass.ds(at, 1)
                sp.dma_start(WR[s][:], d["wall"][tile].rearrange("o p n -> p (o n)")).then_inc(raw_loaded[s], 16)

            for s in range(2):
                load(s, s, s, 0)
            with sp.Fori(0, NB) as tb:
                tok = sp.snap(tb * TB, min_val=0, max_val=SEQ - TB)
                sp.dma_start(X[:], d["x_feat"][:, :, bass.ds(tok, TB)].rearrange("k p n -> p k n")).then_inc(ld_x, 16)
                for a, name in ((AH, "y_hi"), (AL, "y_lo")):
                    sp.dma_start(a[:].bitcast(F32), d[name][:, :, bass.ds(tok, TB)].rearrange("k p n -> p k n")).then_inc(ld_y, 16)
                with sp.Fori(1, TILE_PLE // 2 + 1) as i:
                    for s in range(2):
                        load(tb * N_TILE + 2 * i + s, 2 * i + s, s, 1)
                sp.wait_ge(al_done, 24 * tb + 16)
                sp.dma_start(Tt[:, 0:2], d["p_feat"][:, :, bass.ds(tok, TB)].rearrange("k p n -> p k n")).then_inc(ld_p, 16)
                with sp.Fori(TILE_PLE // 2 + 1, N_TILE // 2) as i:
                    for s in range(2):
                        load(tb * N_TILE + 2 * i + s, 2 * i + s, s, 1)
                for s in range(2):
                    load(tb * N_TILE + N_TILE + s, s, s, 0)
                sp.wait_ge(st_x, 16 * tb + 16)
                sp.sem_inc(x_stored, 1)
                sp.wait_ge(t_done, 24 * tb + 24)
                sp.sem_inc(x_stored, 1)
                sp.wait_ge(job_done, N_JOB * tb + N_JOB)
                sp.sem_inc(x_stored, 1)

        @block.scalar
        def _(act):
            act.sem_inc(sg_done, 2)
            for s in range(2):
                act.sem_inc(st_out[s], 16)

            def hi(w2, s, dst):
                act.wait_ge(raw_loaded[s], 16 * w2 + 16)
                act.copy(dst, WR[s][:]).then_inc(hi_done, 1)

            def whi(w2, s):
                hi(w2, s, WH[s][:])

            act.wait_ge(ld_g, 32)
            act.copy(gwh[:], gwr[:]).then_inc(gh_done, 1)
            for s in range(2):
                whi(0, s)
            with act.Fori(0, NB) as tb:
                job0, w0 = tb * N_JOB, tb * (N_TILE // 2)

                def gates(job, tile2, count, b):
                    for j in range(4):
                        act.wait_ge(job_done, job0 + (job + 1 + j) + 4 * b)
                        if j % 2 == 0:
                            act.wait_ge(mix_done, 16 * tb + 2 * b + (j // 2 + 1 + (0 if job == 0 else KD)))
                            act.activation(SG[j // 2][:], ps4[(job + j) % 4][:], ACT.Sigmoid).then_inc(sg_done, 1)
                        whi(w0 + 2 * b + (tile2 + j // 2 + 1), j % 2)

                def norm(i, job, xs):
                    for k in range(KD):
                        xs(k)
                        if k >= 2:
                            act.wait_ge(acc_done, 32 * tb + (8 * i + k - 1))
                        act.activation(V[k % 2][:], halves(X[:, k]), ACT.Square).then_inc(sq_done, 1)
                    act.wait_ge(job_done, job0 + (job + 1))
                    act.activation(SG[0][:], ps4[job % 4][:], ACT.Ln, bias=eps[:]).then_inc(ln_done, 1)
                    act.wait_ge(ln_done, 4 * tb + (i + 1))
                    act.activation(SG[1][:], SG[0][:], ACT.Exp, scale=-0.5).then_inc(r_done, 1)

                def split(i):
                    for k in range(KD):
                        act.wait_ge(t_done, 24 * tb + (8 * i + k + 1))
                        act.copy(AH[:, k], Tt[:, k]).then_inc(ah_done, 1)

                with act.Fori(0, N_GLU // 4) as b:
                    gates(0, 0, N_GLU, b)
                norm(0, JOB_STAT1, lambda k: act.wait_ge(xadd, N_XADD * tb + (2 + KD)))
                split(0)
                with act.Fori(0, F_GROUPS) as fg:
                    w1 = w0 + fg * F_TILES + TILE_MLP // 2
                    for f in range(F_TILES):
                        n = 32 * tb + 4 * fg + f
                        act.wait_ge(job_done, job0 + fg * (F_TILES + KD) + (JOB_MLP + f + 1))
                        act.wait_ge(v_done, n + 1)
                        act.activation(SG[f % 2][:], ps4[(JOB_MLP + f) % 4][:], ACT.Relu).then_inc(relu_done, 1)
                        whi(w1 + (f // 2 + 1), f % 2)
                        act.wait_ge(v_done, n + 3)
                        act.copy(halves(FH[:, f]), V[f % 2][:]).then_inc(fh_done, 1)
                    for m2 in range(F_TILES):
                        act.wait_ge(job_done, job0 + fg * (F_TILES + KD) + (JOB_MLP + F_TILES + 2 * m2 + 2))
                        whi(w1 + (F_TILES + m2) // 2 + 1, m2 % 2)
                norm(1, JOB_STAT2, lambda k: act.wait_ge(xadd, N_XADD * tb + (2 + KD * F_GROUPS + k + 1)))
                split(1)
                act.wait_ge(ld_p, 16 * tb + 16)
                for k in range(2):
                    act.copy(FH[:, k], Tt[:, k]).then_inc(ph_done, 1)
                with act.Fori(0, N_PLE // 4) as b:
                    gates(JOB_PLE, TILE_PLE // 2, N_PLE, b)
                norm(2, JOB_STAT3, lambda k: act.wait_ge(xadd, N_XADD * tb + (2 + N_XADD)))
                norm(3, JOB_STAT3 + 1, lambda k: act.wait_ge(xfin, 8 * tb + (k + 1)))
                split(2)
                act.dma_start(d["x2"][:, :, bass.ds(tb * TB, TB)].rearrange("k p n -> p k n"), X[:]).then_inc(st_x, 16)

                def store(c, dst, src, off=0):
                    act.wait_ge(copied, N_COPY * tb + (c + 5) + off)
                    act.dma_start(dst, src).then_inc(st_out[c % 2], 16)

                tok = bass.ds(tb * TB, TB)
                with act.Fori(0, N_FM // 4 - 1) as b:
                    for j in range(4):
                        act.wait_ge(job_done, job0 + 4 * b + (JOB_FM + j + 1))
                        whi(w0 + 2 * b + (TILE_FM // 2 + j // 2 + 1), j % 2)
                        store(j, d["fm"][bass.ds(4 * b + j, 1), :, tok].rearrange("o p n -> p (o n)"),
                              V[j % 2][:].rearrange("p a b -> p (a b)"), 4 * b)

                def ghi(i):
                    g = 0 if i < 2 else (i + 2) // 4
                    c = (i if i < 2 else (i - 2) % 4) * P
                    hi(w0 + (TILE_TM + i) // 2, i % 2, GH[g % 2][:, :, c:c + P])

                for j in range(N_FM - 4, N_FM):
                    act.wait_ge(job_done, job0 + (JOB_FM + j + 1))
                    if j < N_FM - 2:
                        whi(w0 + (TILE_FM + j + 2) // 2, j % 2)
                    else:
                        ghi(j - (N_FM - 2))
                    store(j, d["fm"][j, :, tok], V[j % 2][:].rearrange("p a b -> p (a b)"))
                for n in range(2):
                    store(N_FM + n, d["gi"][:, bass.ds(tb * TB + n * (TB // 2), TB // 2)], V[n][0:8, 0])
                c, first = N_FM + 2, 2
                for g in range(4):
                    if g + 1 < 4:
                        for i in range(first, first + 4):
                            ghi(i)
                        first += 4
                    cols = slice(sum(TM_COLS[:g]), sum(TM_COLS[:g + 1]))
                    per = TB // TM_JOBS[g]
                    for j in range(TM_JOBS[g]):
                        dst = d["tm"][bass.ds(tb * TB + j * per, per), cols].rearrange("(t p) n -> p t n", p=P)
                        src = V[c % 2][:].rearrange("p a b -> p (a b)").rearrange("p (t n) -> p t n", n=TM_COLS[g])
                        store(c, dst, src)
                        c += 1
                for s in range(2):
                    whi(w0 + N_TILE // 2, s)
            act.wait_ge(st_x, 16 * NB)
            for s in range(2):
                act.wait_ge(st_out[s], 16 * NB * (N_COPY // 2) + 16)

        @block.gpsimd
        def _(pool):
            pool.memset(ones[:], 1.0 / D).then_inc(ones_set, 1)
            pool.sem_inc(raw_free, 2)
            pool.sem_inc(fl_done, 2)
            pool.wait_ge(gh_done, 1)
            pool.tensor_tensor(gwl[:], gwr[:], gwh[:].bitcast(F32), ALU.subtract).then_inc(gl_done, 1)

            def lo(w, s, dst, src, raw):
                pool.wait_ge(hi_done, w + 1)
                pool.tensor_tensor(dst, raw, src.bitcast(F32), ALU.subtract).then_inc(raw_free, 1)

            def wlo(w, s):
                lo(w, s, WL[s][:], WH[s][:], WR[s][:])

            for s in range(2):
                wlo(s, s)
            with pool.Fori(0, NB) as tb:
                w0 = tb * N_TILE

                def split(i):
                    for k in range(KD):
                        pool.wait_ge(ah_done, 24 * tb + (8 * i + k + 1))
                        pool.tensor_tensor(AL[:, k], Tt[:, k], AH[:, k].bitcast(F32), ALU.subtract).then_inc(al_done, 1)

                with pool.Fori(0, N_GLU // 2) as b:
                    for s in range(2):
                        wlo(w0 + 2 * b + (s + 2), s)
                split(0)
                with pool.Fori(0, F_GROUPS) as fg:
                    w1 = w0 + fg * (2 * F_TILES) + TILE_MLP
                    for f in range(F_TILES):
                        wlo(w1 + (f + 2), f % 2)
                        pool.wait_ge(fh_done, 32 * tb + 4 * fg + (f + 1))
                        pool.tensor_tensor(halves(FL[:, f]), V[f % 2][:], halves(FH[:, f]).bitcast(F32), ALU.subtract).then_inc(fl_done, 1)
                    for m2 in range(F_TILES):
                        wlo(w1 + (F_TILES + m2 + 2), m2 % 2)
                split(1)
                for k in range(2):
                    pool.wait_ge(ph_done, 2 * tb + k + 1)
                    pool.tensor_tensor(FL[:, k], Tt[:, k], FH[:, k].bitcast(F32), ALU.subtract).then_inc(pl_done, 1)
                with pool.Fori(0, N_PLE // 2) as b:
                    for s in range(2):
                        wlo(w0 + 2 * b + (TILE_PLE + s + 2), s)
                split(2)
                with pool.Fori(0, N_FM // 2 - 1) as b:
                    for s in range(2):
                        wlo(w0 + 2 * b + (TILE_FM + s + 2), s)
                for i in range(N_TM):
                    g = 0 if i < 2 else (i + 2) // 4
                    c = (i if i < 2 else (i - 2) % 4) * P
                    lo(w0 + (TILE_TM + i), i % 2, GL[g % 2][:, :, c:c + P], GH[g % 2][:, :, c:c + P],
                       WR[i % 2][:].rearrange("p (k n) -> p k n", k=KD))
                for s in range(2):
                    wlo(w0 + (N_TILE + s), s)

        @block.vector
        def _(dve):
            dve.memset(V[0][:, 0, 0:1], 0.0).then_inc(mix_done, 2)
            dve.memset(V[0][:, 0, 1:2], 0.0).then_inc(xadd, 2)
            dve.memset(V[0][:, 0, 2:3], 0.0).then_inc(v_done, 2)
            dve.memset(V[0][:, 0, 3:4], 0.0).then_inc(copied, 4)
            dve.wait_ge(copied, 4)
            dve.wait_ge(ld_g, 32)
            with dve.Fori(0, NB) as tb:
                job0 = tb * N_JOB

                def mix(job, base, b):
                    for jj in range(2):
                        m = 2 * b + jj
                        dve.wait_ge(sg_done, 16 * tb + (base % 16) + m + 3)
                        dve.wait_ge(job_done, job0 + 4 * b + (job + 2 * jj + 2))
                        dve.wait_ge(xadd, N_XADD * tb + m + (1 + (KD * F_GROUPS + KD if base else 0)))
                        if base == 0:
                            dve.wait_ge(st_out[jj], 16 * (N_COPY // 2) * tb + 16)
                        dve.tensor_tensor(V[jj][:], ps4[(job + 2 * jj + 1) % 4][:], SG[jj][:], ALU.mult).then_inc(mix_done, 1)
                        dve.wait_ge(mix_done, 16 * tb + (base % 16) + m + 3)
                        xm = X[:, bass.ds(m, 1), :].rearrange("p o (a n) -> p (o a) n", a=2)
                        dve.tensor_tensor(xm, xm, V[jj][:], ALU.add).then_inc(xadd, 1)

                def norm(i, out, done, count):
                    a0 = 32 * tb + 8 * i
                    for k in range(KD):
                        dve.wait_ge(sq_done, a0 + (k + 1))
                        if k:
                            dve.wait_ge(acc_done, a0 + k)
                            dve.tensor_tensor(halves(RB[:]), halves(RB[:]), V[k % 2][:], ALU.add).then_inc(acc_done, 1)
                        else:
                            dve.tensor_copy(halves(RB[:]), V[0][:]).then_inc(acc_done, 1)
                    dve.wait_ge(r_done, 4 * tb + (i + 1))
                    for k in range(KD):
                        dve.scalar_tensor_tensor(halves(out[:, k]), halves(X[:, k]), gains[:, i, k:k + 1], SG[1][:],
                                                 ALU.mult, ALU.mult).then_inc(done, 1)

                with dve.Fori(0, N_GLU // 4) as b:
                    dve.wait_ge(ld_x, 16 * tb + 16)
                    mix(0, 0, b)
                norm(0, Tt, t_done, 0)
                with dve.Fori(0, F_GROUPS) as fg:
                    for f in range(F_TILES):
                        n = 32 * tb + 4 * fg + f
                        dve.wait_ge(relu_done, n + 1)
                        dve.wait_ge(fl_done, n + 1)
                        dve.tensor_tensor(V[f % 2][:], SG[f % 2][:], SG[f % 2][:], ALU.mult).then_inc(v_done, 1)
                    for m in range(KD):
                        dve.wait_ge(job_done, job0 + fg * (F_TILES + KD) + (JOB_MLP + F_TILES + m + 1))
                        xm = halves(X[:, m])
                        dve.tensor_tensor(xm, xm, ps4[(JOB_MLP + F_TILES + m) % 4][:], ALU.add).then_inc(xadd, 1)
                norm(1, Tt, t_done, 0)
                with dve.Fori(0, N_PLE // 4) as b:
                    mix(JOB_PLE, KD, b)
                norm(2, X, xfin, 0)
                norm(3, Tt, t_done, 0)

                def copy(c, n, out, src, extra=None):
                    off = extra if extra is not None else 0
                    dve.wait_ge(job_done, job0 + (JOB_FM + c + 1) + off)
                    dve.wait_ge(st_out[c % 2], 8 * off + 16 * (N_COPY // 2) * tb + 16 * (c // 2 + 1))
                    dve.tensor_copy(out, src).then_inc(copied, 1)

                with dve.Fori(0, N_FM // 4) as b:
                    for j in range(4):
                        copy(j, 0, V[j % 2][:], ps4[(JOB_FM + j) % 4][:], 4 * b)
                for n in range(2):
                    copy(N_FM + n, 0, V[n][0:8, 0], ps4[(JOB_GI + n) % 4][0:8, 0])
                for j in range(sum(TM_JOBS)):
                    copy(N_FM + 2 + j, 0, V[j % 2][:], ps4[(JOB_TM + j) % 4][:])

        @block.tensor
        def _(pe):
            def product(out, k_tiles, passes, wait=None):
                for k in range(k_tiles):
                    if wait:
                        wait(k)
                    for i, (l, r) in enumerate(passes(k)):
                        last = pe.matmul(out, l, r, start=(k == 0 and i == 0), stop=(k == k_tiles - 1 and i == 2))
                return last

            def job(slot, k_tiles, wh, wl, ah, al, wait=None):
                for n in range(2):
                    t = slice(n * (TB // 2), (n + 1) * (TB // 2))
                    last = product(ps4[slot][:, n], k_tiles,
                                   lambda k: ((wh(k), ah[:, k, t]), (wh(k), al[:, k, t]), (wl(k), ah[:, k, t])),
                                   wait if n == 0 else None)
                last.then_inc(job_done, 1)

            def tile(s, at=0):
                return (lambda k: WH[s][:, (at + k) * P:(at + k + 1) * P]), (lambda k: WL[s][:, (at + k) * P:(at + k + 1) * P])

            def stat(slot, count):
                pe.wait_ge(acc_done, count)
                for n in range(2):
                    last = pe.matmul(ps4[slot][:, n], ones[:], halves(RB[:])[:, n], start=True, stop=True)
                last.then_inc(job_done, 1)

            pe.wait_ge(ones_set, 1)
            with pe.Fori(0, NB) as tb:
                w0 = tb * N_TILE
                with pe.Fori(0, N_GLU // 4) as b:
                    pe.wait_ge(copied, N_COPY * tb + 4)
                    pe.wait_ge(ld_y, 32 * tb + 32)
                    for j in range(4):
                        pe.wait_ge(raw_free, w0 + 4 * b + (j + 3))
                        pe.wait_ge(mix_done if j % 2 else sg_done, 16 * tb + 2 * b + (j // 2 + 1))
                        job(j, KD, *tile(j % 2), AH, AL)
                stat(JOB_STAT1 % 4, 32 * tb + 8)
                with pe.Fori(0, F_GROUPS) as fg:
                    w1 = w0 + fg * (2 * F_TILES) + TILE_MLP
                    x1 = N_XADD * tb + KD * fg
                    for f in range(F_TILES):
                        pe.wait_ge(raw_free, w1 + (f + 3))
                        pe.wait_ge(xadd, x1 + (f + 5 + 2))
                        job((JOB_MLP + f) % 4, KD, *tile(f % 2), AH, AL,
                            (lambda k: pe.wait_ge(al_done, 24 * tb + (k + 1))) if f == 0 else None)
                    for m in range(KD):
                        if m % 2 == 0:
                            pe.wait_ge(raw_free, w1 + (F_TILES + m // 2 + 3))
                        if m < 4:
                            pe.wait_ge(relu_done, 32 * tb + 4 * fg + (m + 1))
                        else:
                            pe.wait_ge(xadd, x1 + (KD + m - 3 + 2))
                        job((JOB_MLP + F_TILES + m) % 4, F_TILES, *tile(m // 2 % 2, m % 2 * F_TILES), FH, FL,
                            (lambda k: pe.wait_ge(fl_done, 32 * tb + 4 * fg + (k + 1 + 2))) if m == 0 else None)
                stat(JOB_STAT2 % 4, 32 * tb + 16)
                with pe.Fori(0, N_PLE // 4) as b:
                    for j in range(4):
                        pe.wait_ge(raw_free, w0 + 4 * b + (TILE_PLE + j + 3))
                        pe.wait_ge(mix_done if j % 2 else sg_done, 16 * tb + 2 * b + (KD + j // 2 + 1))
                        if j % 2:
                            pe.wait_ge(pl_done, 2 * tb + 2)
                            job((JOB_PLE + j) % 4, 2, *tile(j % 2), FH, FL)
                        else:
                            job((JOB_PLE + j) % 4, KD, *tile(j % 2), AH, AL,
                                (lambda k: pe.wait_ge(al_done, 24 * tb + (8 + k + 1))) if j == 0 else None)
                stat(JOB_STAT3 % 4, 32 * tb + 24)
                stat((JOB_STAT3 + 1) % 4, 32 * tb + 32)
                with pe.Fori(0, N_FM // 4) as b:
                    for j in range(4):
                        pe.wait_ge(raw_free, w0 + 4 * b + (TILE_FM + j + 3))
                        pe.wait_ge(copied, N_COPY * tb + 4 * b + (j + 1))
                        job((JOB_FM + j) % 4, KD, *tile(j % 2), AH, AL,
                            (lambda k: pe.wait_ge(al_done, 24 * tb + (16 + k + 1))) if j == 0 else None)
                pe.wait_ge(gl_done, 1)
                for n in range(2):
                    t = slice(n * (TB // 2), (n + 1) * (TB // 2))
                    pe.wait_ge(copied, N_COPY * tb + (N_FM + n + 1))
                    product(ps4[(JOB_GI + n) % 4][0:8, 0], KD,
                            lambda k: ((gwh[:, k], AH[:, k, t]), (gwh[:, k], AL[:, k, t]), (gwl[:, k], AH[:, k, t]))
                            ).then_inc(job_done, 1)
                c, tiles = N_FM + 2, 0
                for g in range(4):
                    n = TM_COLS[g]
                    tiles += n // P
                    pe.wait_ge(raw_free, w0 + (TILE_TM + tiles + 2))
                    per = TB // P // TM_JOBS[g]
                    for j in range(TM_JOBS[g]):
                        pe.wait_ge(copied, N_COPY * tb + (c + 1))
                        out = ps4[(JOB_FM + c) % 4][:].rearrange("p a b -> p (a b)")
                        for i in range(per):
                            t = slice((j * per + i) * P, (j * per + i + 1) * P)
                            last = product(out[:, i * n:(i + 1) * n], KD,
                                           lambda k: ((AH[:, k, t], GH[g % 2][:, k, 0:n]), (AL[:, k, t], GH[g % 2][:, k, 0:n]),
                                                      (AH[:, k, t], GL[g % 2][:, k, 0:n])))
                        last.then_inc(job_done, 1)
                        c += 1


A_HEADS, A_DIM = 4, 64
A_TILES = A_HEADS * A_DIM // P
QB = 128
N_QB = SEQ // QB
WIN = 512 + QB
KT = WIN // QB
NEG = -1e30
NQ4 = 4
QC = SEQ // NQ4


def attention(nc, env, d, ctx):
    sb, ps, sem = tools(nc, ctx)
    ident, eps = env["ident"], env["eps"]
    qk = sb("at_qk", [P, 2 * A_TILES, SEQ])
    z = sb("at_z", [P, A_TILES, SEQ])
    v = sb("at_v", [P, N_QB, A_HEADS * A_DIM])
    bias = sb("at_bias", [P, A_HEADS, WIN])
    gain = sb("at_gain", [P, 2])
    blk = sb("at_blk", [P, P])
    half = sb("at_half", [P, 2])
    sq = sb("at_sq", [P, 2, QC])
    lnv, rr = sb("at_ln", [P, 2, QC]), sb("at_r", [P, 2, QC])
    qs = sb("at_qs", [P, 2, 2, A_TILES, QB])
    sbv = sb("at_sb", [P, 2, WIN])
    e = sb("at_e", [P, 2, WIN])
    pT = sb("at_pT", [P, 2, KT, QB])
    mx, ng, sm, rc = (sb(f"at_{n}", [P, 2]) for n in ("mx", "ng", "sm", "rc"))
    o = sb("at_o", [P, 2, A_HEADS * A_DIM])
    om = sb("at_om", [P, 2, A_TILES, QB])
    s_ps = [ps(f"at_s_ps{i}", [P, 2, 512]) for i in range(2)]
    t_ps = ps("at_t_ps", [P, 2 * 512])
    o_ps = [ps(f"at_o_ps{i}", [P, 512]) for i in range(2)]
    x_ps = o_ps[0][:, 256:512].rearrange("p (t n) -> p t n", n=QB)
    ld_qk, ld_z, ld_v, ld_b, ld_g = (sem(f"at_ld_{n}") for n in ("qk", "z", "v", "b", "g"))
    blk_set, bias_set, g_done = sem("at_blk_set"), sem("at_bias_set"), sem("at_g_done")
    sq_done, ms_done, ln_done, r_done, qk_done, z_done = (sem(f"at_{n}_done") for n in ("sq", "ms", "ln", "r", "qk", "z"))
    qs_done, s_done, b_done, n_done, e_done, t_done, p_done, pv_done, rc_done, o_done, x_done, m_done = (
        sem(f"at_{n}_done") for n in ("qs", "s", "b", "neg", "e", "t", "p", "pv", "rc", "o", "x", "m"))
    may_add = sem("at_may_add")
    st = [sem("at_st0"), sem("at_st1")]
    N_NORM = 2 * A_TILES * NQ4

    with nc.Block() as block:
        @block.sync
        def _(sp):
            sp.dma_start(qk[:], d["fm"][0:2 * A_TILES].rearrange("k p n -> p k n")).then_inc(ld_qk, 16)
            sp.dma_start(gain[:], d["att_gain"]).then_inc(ld_g, 16)
            sp.dma_start(z[:], d["fm"][2 * A_TILES:3 * A_TILES].rearrange("k p n -> p k n")).then_inc(ld_z, 16)
            sp.dma_start(v[:], d["tm"][:, 0:A_HEADS * A_DIM].rearrange("(t p) n -> p t n", p=P)).then_inc(ld_v, 16)
            sp.dma_start(bias[:], d["att_bias"]).then_inc(ld_b, 16)

            def store(b, s):
                dst = d["mixed"][0:A_TILES, :, bass.ds(sp.snap(b * QB, min_val=0, max_val=SEQ - QB), QB)]
                sp.wait_ge(m_done, b + 1 + 2)
                sp.dma_start(dst.rearrange("k p n -> p k n"), om[:, s]).then_inc(st[s], 16)

            with sp.Fori(0, N_QB // 2) as b2:
                for s in range(2):
                    store(2 * b2 + s, s)
            for s in range(2):
                sp.wait_ge(st[s], 16 * (N_QB // 2))

        @block.gpsimd
        def _(pool):
            pool.wait_ge(ld_g, 16)
            pool.tensor_scalar(gain[:, 0:1], gain[:, 0:1], A_DIM ** -0.5, None, ALU.mult).then_inc(g_done, 1)
            pool.sem_inc(qs_done, 2)
            pool.wait_ge(blk_set, 8)

            def queries(b, s, wait):
                if wait:
                    pool.wait_ge(s_done, A_HEADS * b - A_HEADS)
                for hh in range(2):
                    pool.tensor_tensor(qs[:, s, hh], qk[:, 0:A_TILES, bass.ds(b * QB, QB)],
                                       half[:, hh:hh + 1, None].to_broadcast([P, A_TILES, QB]), ALU.mult).then_inc(qs_done, 1)

            pool.wait_ge(qk_done, A_TILES * NQ4)
            for s in range(2):
                queries(s, s, False)
            with pool.Fori(1, N_QB // 2) as b2:
                for s in range(2):
                    queries(2 * b2 + s, s, True)

        @block.scalar
        def _(act):
            act.wait_ge(ld_qk, 16)
            for i in range(N_NORM):
                t, c = i // NQ4, slice(i % NQ4 * QC, (i % NQ4 + 1) * QC)
                if i >= 2:
                    act.wait_ge(ms_done, i - 1)
                act.activation(sq[:, i % 2], qk[:, t, c], ACT.Square).then_inc(sq_done, 1)
                act.wait_ge(ms_done, i + 1)
                act.activation(lnv[:, i % 2], s_ps[i % 2][:, 0], ACT.Ln, bias=eps[:]).then_inc(ln_done, 1)
                act.wait_ge(ln_done, i + 1)
                if i >= 2:
                    act.wait_ge(qk_done, i - 1)
                act.activation(rr[:, i % 2], lnv[:, i % 2], ACT.Exp, scale=-0.5).then_inc(r_done, 1)
            act.wait_ge(ld_z, 16)
            for t in range(A_TILES):
                act.activation(z[:, t], z[:, t], ACT.Silu).then_inc(z_done, 1)

            def block_(b, nb):
                w = slice(WIN - nb * QB, WIN)
                for h in range(A_HEADS):
                    u = A_HEADS * b + h
                    act.wait_ge(n_done, u + 1)
                    act.wait_ge(t_done, u + 1)
                    act.activation(e[:, h % 2, w], sbv[:, h % 2, w], ACT.Exp, bias=ng[:, h % 2:h % 2 + 1],
                                   accum_out=sm[:, h % 2:h % 2 + 1]).then_inc(e_done, 1)
                    act.wait_ge(t_done, u + 1 + 2)
                    act.wait_ge(pv_done, u + 1)
                    act.copy(pT[:, h % 2, 0:nb], t_ps[:, 0:nb * QB].rearrange("p (t n) -> p t n", n=QB)).then_inc(p_done, 1)

            for b in range(KT - 1):
                block_(b, b + 1)
            with act.Fori(KT - 1, N_QB) as b:
                block_(b, KT)

        @block.vector
        def _(dve):
            dve.memset(om[:, 0, 0, 0:1], 0.0).then_inc(m_done, 2)
            for hh in range(2):
                rows = slice(hh * A_DIM, (hh + 1) * A_DIM)
                dve.memset(blk[rows, rows], 1.0 / A_DIM).then_inc(blk_set, 1)
                dve.memset(blk[rows, (1 - hh) * A_DIM:(2 - hh) * A_DIM], 0.0).then_inc(blk_set, 1)
                dve.memset(half[rows, hh:hh + 1], 1.0).then_inc(blk_set, 1)
                dve.memset(half[rows, 1 - hh:2 - hh], 0.0).then_inc(blk_set, 1)
            dve.wait_ge(ld_b, 16)
            dve.memset(bias[0:64, :, WIN - 64:WIN], NEG).then_inc(bias_set, 1)
            dve.memset(bias[64:P, :, 0:64], NEG).then_inc(bias_set, 1)
            dve.wait_ge(m_done, 2)
            dve.wait_ge(g_done, 1)
            for i in range(N_NORM):
                t, c = i // NQ4, slice(i % NQ4 * QC, (i % NQ4 + 1) * QC)
                dve.wait_ge(r_done, i + 1)
                dve.scalar_tensor_tensor(qk[:, t, c], qk[:, t, c], gain[:, t // A_TILES:t // A_TILES + 1], rr[:, i % 2],
                                         ALU.mult, ALU.mult).then_inc(qk_done, 1)
            dve.wait_ge(bias_set, 2)
            dve.wait_ge(z_done, A_TILES)

            def block_(b, s, nb, early):
                w = slice(WIN - nb * QB, WIN)
                hw = nb * QB // 2

                def scores(h):
                    u = A_HEADS * b + h
                    i = slice(h % 2, h % 2 + 1)
                    two = lambda a: a.rearrange("p (a n) -> p a n", a=2)
                    dve.wait_ge(s_done, u + 1)
                    if early > 0 or h >= 2:
                        dve.wait_ge(e_done, u - 1)
                        dve.wait_ge(n_done, u - 1)
                    dve.sem_inc(may_add, 1)
                    dve.tensor_tensor_reduce(two(sbv[:, h % 2, w]), s_ps[h % 2][:, :, 0:hw], two(bias[:, h, w]), 1.0, -3e38,
                                             ALU.add, ALU.max, accum_out=mx[:, i]).then_inc(b_done, 1)
                    dve.wait_ge(b_done, u + 1)
                    dve.tensor_scalar(ng[:, i], mx[:, i], -1.0, None, ALU.mult).then_inc(n_done, 1)

                def output(h):
                    u = A_HEADS * b + h
                    i = slice(h % 2, h % 2 + 1)
                    f = slice(h * A_DIM, (h + 1) * A_DIM)
                    dve.wait_ge(e_done, u + 1)
                    if early > 0 or h >= 2:
                        dve.wait_ge(o_done, u - 1)
                    dve.reciprocal(rc[:, i], sm[:, i]).then_inc(rc_done, 1)
                    dve.wait_ge(rc_done, u + 1)
                    dve.wait_ge(pv_done, u + 1 + 2)
                    dve.tensor_scalar(o[:, s, f], o_ps[h % 2][:, h // 2 * A_DIM:(h // 2 + 1) * A_DIM], rc[:, i], None, ALU.mult).then_inc(o_done, 1)

                for h in range(A_HEADS):
                    scores(h)
                    if h:
                        output(h - 1)
                output(A_HEADS - 1)
                dve.wait_ge(x_done, b + 1)
                if early >= 2:
                    dve.wait_ge(st[s], 8 * b - 8 * s)
                dve.tensor_tensor(om[:, s], x_ps, z[:, :, bass.ds(b * QB, QB)], ALU.mult).then_inc(m_done, 1)

            for b in range(KT - 1):
                block_(b, b % 2, b + 1, b)
            with dve.Fori((KT - 1) // 2, N_QB // 2) as b2:
                for s in range(2):
                    block_(2 * b2 + s, s, KT, KT)

        @block.tensor
        def _(pe):
            pe.sem_inc(t_done, 2)
            pe.sem_inc(pv_done, 2)
            pe.wait_ge(blk_set, 8)
            for i in range(N_NORM):
                pe.wait_ge(sq_done, i + 1)
                if i >= 2:
                    pe.wait_ge(ln_done, i - 1)
                pe.matmul(s_ps[i % 2][:, 0], blk[:], sq[:, i % 2], start=True, stop=True).then_inc(ms_done, 1)
            pe.wait_ge(qk_done, N_NORM)
            pe.wait_ge(ld_v, 16)

            def block_(b, s, nb, early):
                hw = nb * QB // 2
                key0 = (b + 1 - nb) * QB

                def scores(h):
                    u = A_HEADS * b + h
                    if early > 0 or h >= 2:
                        pe.wait_ge(b_done, u - 1)
                    for n in range(2):
                        last = pe.matmul(s_ps[h % 2][:, n, 0:hw], qs[:, s, h % 2, h // 2],
                                         qk[:, A_TILES + h // 2, bass.ds(key0 + n * hw, hw)], start=True, stop=True)
                    last.then_inc(s_done, 1)

                def turn(h):
                    u = A_HEADS * b + h
                    pe.wait_ge(e_done, u + 1)
                    if early > 0 or h > 0:
                        pe.wait_ge(p_done, u)
                    for t in range(nb):
                        last = pe.transpose(t_ps[:, t * QB:(t + 1) * QB], e[:, h % 2, WIN - (nb - t) * QB:WIN - (nb - t - 1) * QB], ident[:])
                    last.then_inc(t_done, 1)

                def values(h):
                    u = A_HEADS * b + h
                    f = slice(h * A_DIM, (h + 1) * A_DIM)
                    pe.wait_ge(p_done, u + 1)
                    if early > 0 or h >= 2:
                        pe.wait_ge(o_done, u - 1)
                    if h == 0:
                        pe.wait_ge(m_done, b + 2)
                    for t in range(nb):
                        vt = v[:, bass.ds(b + 1 - nb + t, 1), f].rearrange("p o n -> p (o n)")
                        last = pe.matmul(o_ps[h % 2][:, h // 2 * A_DIM:(h // 2 + 1) * A_DIM], pT[:, h % 2, t], vt, start=(t == 0), stop=(t == nb - 1))
                    last.then_inc(pv_done, 1)

                pe.wait_ge(qs_done, 2 * b + 4)
                for h in range(A_HEADS):
                    scores(h)
                    if h:
                        turn(h - 1)
                        values(h - 1)
                turn(A_HEADS - 1)
                values(A_HEADS - 1)
                pe.wait_ge(o_done, A_HEADS * b + A_HEADS)
                for t in range(A_TILES):
                    last = pe.transpose(x_ps[:, t], o[:, s, t * P:(t + 1) * P], ident[:])
                last.then_inc(x_done, 1)

            for b in range(KT - 1):
                block_(b, b % 2, b + 1, b)
            with pe.Fori((KT - 1) // 2, N_QB // 2) as b2:
                for s in range(2):
                    block_(2 * b2 + s, s, KT, KT)


M_HEADS = 4
MC = 128
N_MC = SEQ // MC
M_TAPS = 4
M_SCALE = float(P) ** -0.5
FM_ML = 6
M_W = M_HEADS * P
CW = P + 1


def mlstm(nc, env, d, ctx):
    sb, ps, sem = tools(nc, ctx)
    env["m_qk"] = sb("m_qk", [P, 2 * M_HEADS, SEQ])
    env["m_oz"] = sb("m_oz", [P, N_MC, 2 * M_W])
    env["m_tok"] = sb("m_tok", [P, N_MC, 3 * M_HEADS])
    env["m_dec"] = sb("m_dec", [P, M_HEADS, N_MC])
    with ExitStack() as c:
        mlstm_prepare(nc, env, d, c)
    with ExitStack() as c:
        mlstm_chunks(nc, env, d, c)


def mlstm_prepare(nc, env, d, ctx):
    sb, ps, sem = tools(nc, ctx)
    ident, eps, qk, oz, tok, dec = (env[n] for n in ("ident", "eps", "m_qk", "m_oz", "m_tok", "m_dec"))
    H = M_HEADS
    rA, rB, rC, rE, rT, rst = (sb(f"m_row_{n}", [H, SEQ]) for n in "ABCETR")
    bif = sb("m_bif", [H, 2])
    mp, dt, dd = sb("m_mp", [H, N_MC]), sb("m_dt", [H, N_MC]), sb("m_dd", [H, H, N_MC])
    one = sb("m_one", [H, P])
    xs = sb("m_x", [P, 2, M_TAPS - 1 + SEQ])
    cw, cb = sb("m_cw", [P, 2 * H, M_TAPS]), sb("m_cb", [P, 2 * H])
    tok_ps = ps("m_tok_ps", [P, 512])
    dec_ps = ps("m_dec_ps", [P, 512])
    ld_g, ld_w, ld_oz, ld_x = sem("m_ld_g"), sem("m_ld_w"), sem("m_ld_oz"), [sem("m_ld_x0"), sem("m_ld_x1")]
    a_done, v_done, pad_set, conv, convd = sem("m_a_done"), sem("m_v_done"), sem("m_pad_set"), sem("m_conv"), sem("m_convd")
    turned, spread, silu, st = sem("m_turned"), sem("m_spread"), sem("m_silu"), sem("m_st")
    rst_set, g_made = sem("m_rst_set"), sem("m_g_made")
    by_chunk = lambda v: v.rearrange("p (c n) -> p c n", n=MC)
    last = lambda v: by_chunk(v)[:, :, MC - 1]

    with nc.Block() as block:
        @block.sync
        def _(sp):
            sp.dma_start(rA[:], d["gi"][0:H]).then_inc(ld_g, 16)
            sp.dma_start(rB[:], d["gi"][H:2 * H]).then_inc(ld_g, 16)
            sp.dma_start(bif[:], d["ml_bif"]).then_inc(ld_g, 16)
            sp.dma_start(cw[:], d["ml_cw"]).then_inc(ld_w, 16)
            sp.dma_start(cb[:], d["ml_cb"]).then_inc(ld_w, 16)
            for k in range(2 * H):
                if k >= 2:
                    sp.wait_ge(convd, k - 1)
                sp.dma_start(xs[:, k % 2, M_TAPS - 1:], d["fm"][FM_ML + k]).then_inc(ld_x[k % 2], 16)
            sp.wait_ge(v_done, 8)
            sp.dma_start(d["rows"][0], rT[:]).then_inc(st, 16)
            sp.wait_ge(a_done, 4)
            sp.dma_start(d["rows"][1], rB[:]).then_inc(st, 16)
            sp.wait_ge(st, 32)

        @block.scalar
        def _(act):
            act.dma_start(oz[:], d["tm"][:, 256 + M_W:256 + 3 * M_W].rearrange("(t p) n -> p t n", p=P)).then_inc(ld_oz, 16)
            act.wait_ge(ld_g, 48)
            act.activation(rT[:], rB[:], ACT.Abs, bias=bif[:, 1:2]).then_inc(a_done, 1)
            act.wait_ge(a_done, 1)
            act.activation(rT[:], rT[:], ACT.Exp, scale=-1.0).then_inc(a_done, 1)
            act.wait_ge(a_done, 2)
            act.activation(rT[:], rT[:], ACT.Ln, bias=1.0).then_inc(a_done, 1)
            act.wait_ge(v_done, 8)
            act.activation(rB[:], rB[:], ACT.Exp).then_inc(a_done, 1)
            act.activation(rC[:], rC[:], ACT.Exp, scale=-1.0).then_inc(a_done, 1)
            act.wait_ge(v_done, 9)
            act.activation(mp[:], dt[:], ACT.Exp).then_inc(a_done, 1)
            act.wait_ge(v_done, 10)
            act.activation(rE[:], rE[:], ACT.Exp).then_inc(a_done, 1)
            for k in range(2 * H):
                act.wait_ge(convd, k + 1)
                act.activation(qk[:, k], qk[:, k], ACT.Silu).then_inc(silu, 1)
            act.wait_ge(ld_oz, 16)
            act.activation(oz[:, :, 0:M_W], oz[:, :, 0:M_W], ACT.Sigmoid).then_inc(silu, 1)
            act.activation(oz[:, :, M_W:], oz[:, :, M_W:], ACT.Silu).then_inc(silu, 1)

        @block.gpsimd
        def _(pool):
            pool.memset(rst[:], 1.0).then_inc(rst_set, 1)
            pool.wait_ge(rst_set, 1)
            pool.memset(by_chunk(rst[:])[:, :, 0:1], 0.0).then_inc(rst_set, 1)
            pool.memset(one[:], 1.0).then_inc(rst_set, 1)

        @block.vector
        def _(dve):
            dve.memset(xs[:, :, 0:M_TAPS - 1], 0.0).then_inc(pad_set, 1)
            dve.wait_ge(ld_w, 32)
            dve.wait_ge(pad_set, 1)

            def convolve(k):
                dve.wait_ge(ld_x[k % 2], 16 * (k // 2) + 16)
                for j in range(M_TAPS):
                    x = xs[:, k % 2, j:j + SEQ]
                    if j == 0:
                        step = dve.tensor_scalar(qk[:, k], x, cw[:, k, j:j + 1], cb[:, k:k + 1], ALU.mult, ALU.add)
                    else:
                        dve.wait_ge(conv, (M_TAPS - 1) * k + j)
                        step = dve.scalar_tensor_tensor(qk[:, k], x, cw[:, k, j:j + 1], qk[:, k], ALU.mult, ALU.add)
                    step.then_inc(convd if j == M_TAPS - 1 else conv, 1)

            dve.wait_ge(ld_g, 48)
            dve.tensor_scalar(rA[:], rA[:], bif[:, 0:1], None, ALU.add).then_inc(v_done, 1)
            dve.tensor_scalar(rE[:], rB[:], bif[:, 1:2], 0.0, ALU.add, ALU.min).then_inc(v_done, 1)
            dve.wait_ge(a_done, 3)
            dve.wait_ge(v_done, 2)
            dve.tensor_tensor(rB[:], rE[:], rT[:], ALU.subtract).then_inc(v_done, 1)
            dve.wait_ge(v_done, 3)
            dve.wait_ge(rst_set, 3)
            dve.tensor_tensor_scan(rC[:], rB[:], rA[:], 0.0, ALU.add, ALU.max).then_inc(v_done, 1)
            dve.tensor_tensor_scan(rE[:], rst[:], rB[:], 0.0, ALU.mult, ALU.add).then_inc(v_done, 1)
            dve.memset(mp[:, 0:1], 0.0)
            dve.wait_ge(v_done, 5)
            dve.tensor_copy(mp[:, 1:], by_chunk(rC[:])[:, 0:N_MC - 1, MC - 1]).then_inc(v_done, 1)
            dve.tensor_tensor(rT[:], rE[:], rC[:], ALU.subtract).then_inc(v_done, 1)
            dve.wait_ge(v_done, 7)
            dve.tensor_tensor(by_chunk(rB[:]), by_chunk(rT[:]), mp[:, :, None].to_broadcast([H, N_MC, MC]), ALU.add).then_inc(v_done, 1)
            dve.tensor_tensor(dt[:], last(rT[:]), mp[:], ALU.add).then_inc(v_done, 1)
            dve.tensor_tensor(rA[:], rA[:], rE[:], ALU.subtract).then_inc(g_made, 1)
            dve.wait_ge(g_made, 1)
            dve.tensor_tensor(by_chunk(rE[:]), by_chunk(rA[:]), by_chunk(rT[:])[:, :, MC - 1:MC].to_broadcast([H, N_MC, MC]),
                              ALU.add).then_inc(v_done, 1)
            dve.wait_ge(a_done, 6)
            dve.tensor_tensor(dd[:], mp[:, None, :].to_broadcast([H, H, N_MC]),
                              ident[0:H, 0:H, None].to_broadcast([H, H, N_MC]), ALU.mult).then_inc(spread, 1)
            for k in range(2 * H):
                convolve(k)
            dve.wait_ge(turned, 1)
            t = tok_ps[:, 0:3 * H * N_MC].rearrange("p (c n) -> p c n", n=3 * H)
            dve.tensor_copy(tok[:, :, 0:2 * H], t[:, :, 0:2 * H])
            dve.tensor_scalar(tok[:, :, 2 * H:], t[:, :, 2 * H:], M_SCALE, None, ALU.mult)
            dve.wait_ge(turned, 2)
            dve.tensor_copy(dec[:], dec_ps[:, 0:H * N_MC].rearrange("p (h c) -> p h c", h=H))

        @block.tensor
        def _(pe):
            pe.wait_ge(spread, 1)
            pe.wait_ge(a_done, 7)
            pe.wait_ge(rst_set, 3)
            for c in range(N_MC):
                for i, r in enumerate((rA, rC, rE)):
                    at = (3 * c + i) * H
                    last_ = pe.transpose(tok_ps[:, at:at + H], r[:, c * MC:(c + 1) * MC], ident[0:H, 0:H])
            last_.then_inc(turned, 1)
            pe.matmul(dec_ps[:, 0:H * N_MC], one[:], dd[:].rearrange("p h c -> p (h c)"), start=True, stop=True).then_inc(turned, 1)


def mlstm_chunks(nc, env, d, ctx):
    sb, ps, sem = tools(nc, ctx)
    ident, eps, qk, oz, tok, dec = (env[n] for n in ("ident", "eps", "m_qk", "m_oz", "m_tok", "m_dec"))
    H = M_HEADS
    va = sb("m_va", [P, 2, H, CW])
    bc = sb("m_bc", [P, 2, 2, H, MC])
    sc = sb("m_sc", [P, 2, 4 * H])
    ks = sb("m_ks", [P, 2, H, MC])
    qp = sb("m_qp", [P, 2, H, MC])
    am = sb("m_am", [P, 2, H, MC])
    dm = sb("m_dm", [P, 2, H, MC])
    sd = sb("m_sd", [P, 2, H, MC])
    kw = sb("m_kw", [P, 2, H, P])
    hb, hm = sb("m_hb", [P, 2, H, P]), sb("m_hm", [P, 2, H, P])
    om = sb("m_om", [P, 2, H, MC])
    junk = sb("m_junk", [P, H, P])
    state = sb("m_state", [P, H, CW])
    mask = sb("m_mask", [P, MC])
    ad, dn, rc = (sb(f"m_{n}", [P, 2, H]) for n in ("ad", "dn", "rc"))
    ssq, ln, rr = (sb(f"m_{n}", [P, 2, H]) for n in ("ssq", "ln", "rr"))
    gain = sb("m_gain", [P, H])
    s_ps = [ps(f"m_s_ps{i}", [P, H, MC]) for i in range(2)]
    kt_ps, x_ps = ps("m_kt_ps", [P, H, P]), ps("m_x_ps", [P, H, P])
    n_ps, u_ps = ps("m_n_ps", [P, 2, 512]), ps("m_u_ps", [P, 2, 512])
    head = lambda v, h: v[:, h // 2, h % 2 * CW:(h % 2 + 1) * CW]
    heads = lambda v: v[:, :, 0:2 * CW].rearrange("p a (b n) -> p a b n", n=CW)
    two = lambda v: v.rearrange("p (a b) n -> p a b n", a=2)
    ld_g, va_ld, bc_ld = sem("m_ld_gain"), [sem("m_va_ld0"), sem("m_va_ld1")], [sem("m_bc_ld0"), sem("m_bc_ld1")]
    st = [sem("m_st0"), sem("m_st1")]
    names = ("ks qp sc am dm s kt sd kw num upd c ad den rec h hm sq rn r h2 h3 x om").split()
    S = {n: sem(f"m_{n}_done") for n in names}
    (ks_done, qp_done, sc_done, am_done, dm_done, s_done, kt_done, sd_done, kw_done, num_done, upd_done, c_done,
     ad_done, den_done, rec_done, h_done, hm_done, sq_done, rn_done, r_done, h2_done, h3_done, x_done, om_done) = S.values()
    ready, va_set, mask_set = sem("m_ready"), sem("m_va_set"), sem("m_mask_set")

    def schedule(engine, s1, s2, s3, s4):
        def step(c, par, full=True):
            for off, stage in ((1, s1), (0, s2), (-1, s3), (-2, s4)):
                if stage and (full or 0 <= c + off < N_MC):
                    stage(c + off, (par + off) % 2)
        for c in range(-1, 2):
            step(c, c % 2, False)
        with engine.Fori(1, N_MC // 2 - 1) as i:
            for par in range(2):
                step(2 * i + par, par)
        for c in range(N_MC - 2, N_MC + 2):
            step(c, c % 2, False)

    with nc.Block() as block:
        @block.sync
        def _(sp):
            for s in range(2):
                sp.sem_inc(st[s], 16)
            sp.dma_start(gain[:], d["ml_gain"]).then_inc(ld_g, 16)

            def load(c, s):
                tok_at = bass.ds(c * MC, MC) if isinstance(c, int) else bass.ds(sp.snap(c * MC, min_val=0, max_val=SEQ - MC), MC)
                src = d["tm"][tok_at, 256:256 + M_W].rearrange("p (h n) -> p h n", h=H)
                rows = d["rows"][:, :, tok_at].partition_broadcast(P)
                sp.wait_ge(num_done, c + 1)
                sp.sem_inc(ready, 1)
                sp.wait_ge(upd_done, c + 1)
                sp.sem_inc(ready, 1)
                sp.dma_start(va[:, s, :, 0:P], src).then_inc(va_ld[s], 16)
                sp.wait_ge(am_done, c + 1)
                sp.sem_inc(ready, 1)
                sp.wait_ge(qp_done, c + 1)
                sp.sem_inc(ready, 1)
                sp.dma_start(bc[:, s], rows).then_inc(bc_ld[s], 16)

            def store(c, s):
                tok_at = bass.ds(c * MC, MC) if isinstance(c, int) else bass.ds(sp.snap(c * MC, min_val=0, max_val=SEQ - MC), MC)
                dst = d["mixed"][2:2 + H, :, tok_at].rearrange("k p n -> p k n")
                sp.wait_ge(om_done, c + 1)
                sp.dma_start(dst, om[:, s]).then_inc(st[s], 16)

            for c in range(2):
                load(c, c)
            load(2, 0)
            load(3, 1)
            with sp.Fori(0, N_MC // 2 - 2) as i:
                for s in range(2):
                    store(2 * i + s, s)
                    load(2 * i + (4 + s), s)
            for c in range(N_MC - 4, N_MC):
                store(c, c % 2)
            for s in range(2):
                sp.wait_ge(st[s], 16 + 16 * (N_MC // 2))

        @block.gpsimd
        def _(pool):
            pool.memset(mask[:], 0.0).then_inc(mask_set, 1)
            pool.wait_ge(mask_set, 1)
            pool.affine_select(out=mask[:], in_=mask[:], compare_op=ALU.is_ge, fill=NEG, base=0,
                               pattern=[[1, MC]], channel_multiplier=-1).then_inc(mask_set, 1)
            pool.sem_inc(qp_done, 2)
            pool.sem_inc(hm_done, 2)
            pool.sem_inc(h3_done, 2)

            def stage1(c, s):
                at = bass.ds(c * MC, MC)
                pool.wait_ge(kt_done, c + 1)
                pool.tensor_copy(ks[:, s], qk[:, H:, at]).then_inc(ks_done, 1)
                pool.wait_ge(kw_done, c + 1)
                pool.wait_ge(den_done, c + 1)
                pool.tensor_copy(sc[:, s, 0:3 * H], tok[:, bass.ds(c, 1)].rearrange("p o n -> p (o n)")).then_inc(sc_done, 1)
                pool.tensor_copy(sc[:, s, 3 * H:], dec[:, :, bass.ds(c, 1)].rearrange("p h o -> p (h o)")).then_inc(sc_done, 1)
                pool.wait_ge(bc_ld[s], 8 * c + (16 - 8 * s))
                pool.wait_ge(num_done, c + 1)
                pool.tensor_tensor(qp[:, s], qk[:, 0:H, at], bc[:, s, 1], ALU.mult).then_inc(qp_done, 1)

            def stage2(c, s):
                pool.wait_ge(h_done, c + 2)
                pool.wait_ge(h2_done, c + 1)
                pool.tensor_tensor(hm[:, s], hb[:, s], oz[:, bass.ds(c, 1), 0:M_W].rearrange("p o (h n) -> p (o h) n", h=H),
                                   ALU.mult).then_inc(hm_done, 1)

            def stage3(c, s):
                pool.wait_ge(h2_done, c + 3)
                pool.tensor_tensor(hb[:, s], hb[:, s], oz[:, bass.ds(c, 1), M_W:].rearrange("p o (h n) -> p (o h) n", h=H),
                                   ALU.mult).then_inc(h3_done, 1)

            schedule(pool, stage1, stage2, stage3, None)

        @block.scalar
        def _(act):
            act.sem_inc(dm_done, 2)
            act.sem_inc(kw_done, 2)

            def stage1(c, s):
                act.wait_ge(am_done, c + 3)
                act.wait_ge(sc_done, 2 * c + 2)
                act.wait_ge(sd_done, c + 1)
                for h in range(H):
                    step = act.activation(dm[:, s, h], am[:, s, h], ACT.Exp, bias=sc[:, s, h:h + 1])
                step.then_inc(dm_done, 1)
                act.wait_ge(kt_done, c + 3)
                act.wait_ge(upd_done, c + 1)
                for h in range(H):
                    step = act.activation(kw[:, s, h], kt_ps[:, h], ACT.Copy, scale=sc[:, s, 2 * H + h:2 * H + h + 1])
                step.then_inc(kw_done, 1)

            def stage2(c, s):
                act.wait_ge(num_done, c + 3)
                act.wait_ge(den_done, c + 1)
                act.activation(two(ad[:, s, :, None]), heads(n_ps)[:, :, :, P:CW], ACT.Abs).then_inc(ad_done, 1)
                act.wait_ge(hm_done, c + 3)
                for h in range(H):
                    step = act.activation(junk[:, h], hm[:, s, h], ACT.Square, accum_out=ssq[:, s, h:h + 1])
                step.then_inc(sq_done, 1)
                act.wait_ge(sq_done, c + 1)
                act.activation(ln[:, s], ssq[:, s], ACT.Ln, bias=eps[:], scale=1.0 / P).then_inc(rn_done, 1)
                act.wait_ge(rn_done, c + 1)
                act.activation(rr[:, s], ln[:, s], ACT.Exp, scale=-0.5).then_inc(r_done, 1)

            schedule(act, stage1, stage2, None, None)

        @block.vector
        def _(dve):
            for n in ("am", "sd", "den", "h2"):
                dve.sem_inc(S[n], 2)
            dve.memset(va[:, :, :, P:CW], 1.0).then_inc(va_set, 1)
            dve.memset(state[:], 0.0).then_inc(c_done, 1)
            dve.sem_inc(h_done, 1)

            def stage1(c, s):
                dve.wait_ge(bc_ld[s], 8 * c + (16 - 8 * s))
                dve.wait_ge(dm_done, c + 1)
                dve.tensor_tensor(am[:, s], bc[:, s, 0], mask[:, None, :].to_broadcast([P, H, MC]), ALU.add).then_inc(am_done, 1)
                dve.wait_ge(s_done, c + 1)
                dve.wait_ge(dm_done, c + 3)
                dve.wait_ge(num_done, c + 1)
                dve.scalar_tensor_tensor(sd[:, s], s_ps[s][:], M_SCALE, dm[:, s], ALU.mult, ALU.mult).then_inc(sd_done, 1)

            def stage2(c, s):
                dve.wait_ge(upd_done, c + 3)
                dve.wait_ge(sc_done, 2 * c + 2)
                dve.wait_ge(c_done, c + 1)
                for h in range(H):
                    step = dve.scalar_tensor_tensor(state[:, h], state[:, h], sc[:, s, 3 * H + h:3 * H + h + 1], head(u_ps, h),
                                                    ALU.mult, ALU.add)
                step.then_inc(c_done, 1)
                dve.wait_ge(ad_done, c + 1)
                dve.tensor_tensor(dn[:, s], ad[:, s], sc[:, s, H:2 * H], ALU.max).then_inc(den_done, 1)
                dve.wait_ge(den_done, c + 3)
                dve.reciprocal(rc[:, s], dn[:, s]).then_inc(rec_done, 1)
                dve.wait_ge(rec_done, c + 1)
                dve.wait_ge(x_done, c + 1)
                dve.tensor_tensor(two(hb[:, s]), heads(n_ps)[:, :, :, 0:P],
                                  two(rc[:, s, :, None]).to_broadcast([P, 2, 2, P]), ALU.mult).then_inc(h_done, 1)

            def stage3(c, s):
                dve.wait_ge(r_done, c + 1)
                dve.tensor_tensor(hb[:, s], hm[:, s], rr[:, s, :, None].to_broadcast([P, H, P]), ALU.mult).then_inc(h2_done, 1)

            def stage4(c, s):
                dve.wait_ge(x_done, c + 3)
                dve.wait_ge(st[s], 8 * c + (16 - 8 * s))
                dve.tensor_tensor(om[:, s], x_ps[:], gain[:, :, None].to_broadcast([P, H, MC]), ALU.mult).then_inc(om_done, 1)

            dve.wait_ge(ld_g, 16)
            dve.wait_ge(mask_set, 2)
            schedule(dve, stage1, stage2, stage3, stage4)

        @block.tensor
        def _(pe):
            for n in ("kt", "num", "upd", "x"):
                pe.sem_inc(S[n], 2)
            pe.wait_ge(va_set, 1)

            def stage1(c, s):
                pe.wait_ge(ks_done, c + 1)
                pe.wait_ge(sd_done, c + 1)
                for h in range(H):
                    last = pe.matmul(s_ps[s][:, h], ks[:, s, h], qk[:, h, bass.ds(c * MC, MC)], start=True, stop=True)
                last.then_inc(s_done, 1)
                pe.wait_ge(kw_done, c + 2)
                for h in range(H):
                    last = pe.transpose(kt_ps[:, h], ks[:, s, h], ident[:])
                last.then_inc(kt_done, 1)

            def stage2(c, s):
                pe.wait_ge(va_ld[s], 8 * c + (16 - 8 * s))
                pe.wait_ge(sd_done, c + 3)
                pe.wait_ge(qp_done, c + 3)
                pe.wait_ge(c_done, c + 1)
                pe.wait_ge(h_done, c + 1)
                for h in range(H):
                    pe.matmul(head(n_ps, h), sd[:, s, h], va[:, s, h], start=True, stop=False)
                    last = pe.matmul(head(n_ps, h), qp[:, s, h], state[:, h], start=False, stop=True)
                last.then_inc(num_done, 1)
                pe.wait_ge(kw_done, c + 3)
                for h in range(H):
                    last = pe.matmul(head(u_ps, h), kw[:, s, h], va[:, s, h], start=True, stop=True)
                last.then_inc(upd_done, 1)

            def stage3(c, s):
                pe.wait_ge(h3_done, c + 3)
                pe.wait_ge(om_done, c) if not isinstance(c, int) or c > 0 else None
                for h in range(H):
                    last = pe.transpose(x_ps[:, h], hb[:, s, h], ident[:])
                last.then_inc(x_done, 1)

            schedule(pe, stage1, stage2, stage3, None)


C_TILES, C_TAPS = 2, 31
FM_CV = 14
CN = 512


def conv_mixer(nc, env, d, ctx):
    sb, ps, sem = tools(nc, ctx)
    eps = env["eps"]
    u = sb("cv_u", [P, C_TILES, C_TAPS - 1 + SEQ])
    g = sb("cv_g", [P, C_TILES, SEQ])
    z = sb("cv_z", [P, C_TILES, SEQ])
    acc = sb("cv_acc", [P, C_TILES, SEQ])
    w, par = sb("cv_w", [P, C_TILES, C_TAPS]), sb("cv_par", [P, 3, C_TILES])
    ones = sb("cv_ones", [P, P])
    xc, sq, ln, rr = (sb(f"cv_{n}", [P, C_TILES, CN]) for n in ("xc", "sq", "ln", "rr"))
    m_ps, v_ps = ps("cv_m_ps", [P, 2, CN]), ps("cv_v_ps", [P, 2, CN])
    ld_a, ld_b, ld_z, ld_w = (sem(f"cv_ld_{n}") for n in "abzw")
    pad_set, g_done, u_done, z_done, tap, ones_set = (sem(f"cv_{n}") for n in ("pad_set", "g_done", "u_done", "z_done", "tap", "ones_set"))
    mean, xc_done, sq_done, var, ln_done, r_done, y_done, s_done, out_done, st = (
        sem(f"cv_{n}") for n in ("mean", "xc_done", "sq_done", "var", "ln_done", "r_done", "y_done", "s_done", "out_done", "st"))
    steps = SEQ // CN

    with nc.Block() as block:
        @block.sync
        def _(sp):
            tiles_of = lambda i: d["fm"][FM_CV + i * C_TILES:FM_CV + (i + 1) * C_TILES].rearrange("k p n -> p k n")
            sp.dma_start(g[:], tiles_of(1)).then_inc(ld_b, 16)
            sp.dma_start(u[:, :, C_TAPS - 1:], tiles_of(0)).then_inc(ld_a, 16)
            sp.dma_start(w[:], d["cv_w"]).then_inc(ld_w, 16)
            sp.dma_start(par[:], d["cv_par"]).then_inc(ld_w, 16)
            sp.dma_start(z[:], tiles_of(2)).then_inc(ld_z, 16)
            sp.wait_ge(out_done, steps)
            sp.dma_start(d["mixed"][6:6 + C_TILES].rearrange("k p n -> p k n"), acc[:]).then_inc(st, 16)
            sp.wait_ge(st, 16)

        @block.gpsimd
        def _(pool):
            pool.memset(ones[:], 1.0 / (C_TILES * P)).then_inc(ones_set, 1)

        @block.scalar
        def _(act):
            act.wait_ge(ld_b, 16)
            for t in range(C_TILES):
                act.activation(g[:, t], g[:, t], ACT.Sigmoid).then_inc(g_done, 1)
            act.wait_ge(ld_z, 16)
            for t in range(C_TILES):
                act.activation(z[:, t], z[:, t], ACT.Silu).then_inc(z_done, 1)
            act.wait_ge(ld_w, 32)
            for i in range(steps):
                act.wait_ge(xc_done, 2 * i + 2)
                if i:
                    act.wait_ge(var, i)
                act.activation(sq[:], xc[:], ACT.Square).then_inc(sq_done, 1)
                act.wait_ge(var, i + 1)
                act.activation(ln[:, 0], v_ps[:, i % 2], ACT.Ln, bias=eps[:]).then_inc(ln_done, 1)
                act.wait_ge(ln_done, i + 1)
                act.activation(rr[:, 0], ln[:, 0], ACT.Exp, scale=-0.5).then_inc(r_done, 1)
                act.wait_ge(y_done, 2 * i + 2)
                for t in range(C_TILES):
                    act.activation(xc[:, t], xc[:, t], ACT.Silu, bias=par[:, 2, t:t + 1], scale=par[:, 1, t:t + 1]).then_inc(s_done, 1)

        @block.vector
        def _(dve):
            dve.memset(u[:, :, 0:C_TAPS - 1], 0.0).then_inc(pad_set, 1)
            dve.wait_ge(ld_a, 16)
            for t in range(C_TILES):
                dve.wait_ge(g_done, t + 1)
                x = u[:, t, C_TAPS - 1:]
                dve.tensor_tensor(x, x, g[:, t], ALU.mult).then_inc(u_done, 1)
            dve.wait_ge(ld_w, 32)
            dve.wait_ge(u_done, C_TILES)
            dve.wait_ge(pad_set, 1)
            for j in range(C_TAPS):
                for t in range(C_TILES):
                    x, wj = u[:, t, j:j + SEQ], w[:, t, j:j + 1]
                    if j == 0:
                        step = dve.tensor_scalar(acc[:, t], x, wj, par[:, 0, t:t + 1], ALU.mult, ALU.add)
                    else:
                        dve.wait_ge(tap, C_TILES * (j - 1) + t + 1)
                        step = dve.scalar_tensor_tensor(acc[:, t], x, wj, acc[:, t], ALU.mult, ALU.add)
                    step.then_inc(tap, 1)
            dve.wait_ge(z_done, C_TILES)
            for i in range(steps):
                at = slice(i * CN, (i + 1) * CN)
                dve.wait_ge(mean, i + 1)
                if i:
                    dve.wait_ge(out_done, i)
                for t in range(C_TILES):
                    dve.tensor_tensor(xc[:, t], acc[:, t, at], m_ps[:, i % 2], ALU.subtract).then_inc(xc_done, 1)
                dve.wait_ge(r_done, i + 1)
                dve.wait_ge(xc_done, 2 * i + 2)
                for t in range(C_TILES):
                    dve.tensor_tensor(xc[:, t], xc[:, t], rr[:, 0], ALU.mult).then_inc(y_done, 1)
                dve.wait_ge(s_done, 2 * i + 2)
                dve.tensor_tensor(acc[:, :, at], xc[:], z[:, :, at], ALU.mult).then_inc(out_done, 1)

        @block.tensor
        def _(pe):
            pe.wait_ge(ones_set, 1)
            pe.wait_ge(tap, C_TILES * C_TAPS)
            for i in range(steps):
                if i >= 2:
                    pe.wait_ge(xc_done, 2 * i - 2)
                for t in range(C_TILES):
                    last = pe.matmul(m_ps[:, i % 2], ones[:], acc[:, t, i * CN:(i + 1) * CN], start=(t == 0), stop=(t == C_TILES - 1))
                last.then_inc(mean, 1)
                pe.wait_ge(sq_done, i + 1)
                if i >= 2:
                    pe.wait_ge(ln_done, i - 1)
                for t in range(C_TILES):
                    last = pe.matmul(v_ps[:, i % 2], ones[:], sq[:, t], start=(t == 0), stop=(t == C_TILES - 1))
                last.then_inc(var, 1)


OT = P
N_OT = SEQ // OT


def final(nc, env, d, ctx):
    sb, ps, sem = tools(nc, ctx)
    ident = env["ident"]
    wr = sb("o_wr", [P, 2, D])
    wh, wl = sb("o_wh", [P, KD, D], F32R), sb("o_wl", [P, KD, D], F32R)
    m = sb("o_m", [P, 2, KD, OT])
    mh, ml = sb("o_mh", [P, 2, KD, OT], F32R), sb("o_ml", [P, 2, KD, OT], F32R)
    x = sb("o_x", [P, 2, KD, OT])
    y = sb("o_y", [P, 2, D])
    y_ps = [ps(f"o_y_ps{i}", [P, 2, D // 2]) for i in range(2)]
    x_ps = [ps(f"o_x_ps{i}", [P, 2, D // 2]) for i in range(2)]
    ld_w, ld_m, ld_x, st = ([sem(f"o_{n}{s}") for s in range(2)] for n in ("ld_w", "ld_m", "ld_x", "st"))
    wh_done, wl_done, mh_done, ml_done, y_done, add_done, turned = (
        sem(f"o_{n}") for n in ("wh_done", "wl_done", "mh_done", "ml_done", "y_done", "add_done", "turned"))
    ready, xs_copied = sem("o_ready"), sem("o_xs_copied")

    with nc.Block() as block:
        @block.sync
        def _(sp):
            for s in range(2):
                sp.sem_inc(st[s], 16)
            w = d["w_out"].rearrange("(k p) n -> k p n", p=P)

            def load(c, s):
                at = bass.ds(c * OT if isinstance(c, int) else sp.snap(c * OT, min_val=0, max_val=SEQ - OT), OT)
                src_m, src_x = (d[n][:, :, at].rearrange("k p n -> p k n") for n in ("mixed", "x2"))
                sp.wait_ge(ml_done, c + 1)
                sp.sem_inc(ready, 1)
                sp.dma_start(m[:, s], src_m).then_inc(ld_m[s], 16)
                sp.wait_ge(turned, c + 1)
                sp.sem_inc(ready, 1)
                sp.dma_start(x[:, s], src_x).then_inc(ld_x[s], 16)

            def store(c, s):
                dst = d["out"][bass.ds(c * OT if isinstance(c, int) else sp.snap(c * OT, min_val=0, max_val=SEQ - OT), OT)]
                sp.wait_ge(add_done, c + 1 + 2)
                sp.sem_inc(ready, 1)
                sp.dma_start(dst, y[:, s]).then_inc(st[s], 16)

            for c in range(2):
                load(c, c)
            for k in range(KD):
                if k >= 2:
                    sp.wait_ge(wl_done, k - 1)
                sp.dma_start(wr[:, k % 2], w[k]).then_inc(ld_w[k % 2], 16)
            with sp.Fori(0, N_OT // 2 - 1) as i:
                for s in range(2):
                    load(2 * i + (2 + s), s)
                    store(2 * i + s, s)
            for s in range(2):
                store(N_OT - 2 + s, s)
            for s in range(2):
                sp.wait_ge(st[s], 16 + 16 * (N_OT // 2))

        @block.scalar
        def _(act):
            def split(c, s):
                act.wait_ge(ld_m[s], 8 * c + (16 - 8 * s))
                act.wait_ge(y_done, c + 1)
                act.copy(mh[:, s], m[:, s]).then_inc(mh_done, 1)

            split(0, 0)
            for k in range(KD):
                act.wait_ge(ld_w[k % 2], 16 * (k // 2) + 16)
                act.copy(wh[:, k], wr[:, k % 2]).then_inc(wh_done, 1)
            split(1, 1)
            with act.Fori(1, N_OT // 2) as i:
                for s in range(2):
                    split(2 * i + s, s)

        @block.gpsimd
        def _(pool):
            pool.sem_inc(ml_done, 2)

            def split(c, s):
                pool.wait_ge(mh_done, c + 1)
                pool.tensor_tensor(ml[:, s], m[:, s], mh[:, s].bitcast(F32), ALU.subtract).then_inc(ml_done, 1)

            split(0, 0)
            for k in range(KD):
                pool.wait_ge(wh_done, k + 1)
                pool.tensor_tensor(wl[:, k], wr[:, k % 2], wh[:, k].bitcast(F32), ALU.subtract).then_inc(wl_done, 1)
            split(1, 1)
            with pool.Fori(1, N_OT // 2) as i:
                for s in range(2):
                    split(2 * i + s, s)

        @block.vector
        def _(dve):
            dve.memset(y[:, 0, 0:1], 0.0).then_inc(add_done, 2)
            dve.wait_ge(add_done, 2)

            def add(c, s):
                dve.wait_ge(turned, c + 1 + 2)
                dve.wait_ge(st[s], 8 * c + (16 - 8 * s))
                dve.tensor_copy(y[:, s].rearrange("p (a n) -> p a n", a=2), x_ps[s][:]).then_inc(xs_copied, 1)
                dve.wait_ge(y_done, c + 1 + 2)
                dve.wait_ge(xs_copied, c + 1)
                ys = y[:, s].rearrange("p (a n) -> p a n", a=2)
                dve.tensor_tensor(ys, ys, y_ps[s][:], ALU.add).then_inc(add_done, 1)

            with dve.Fori(0, N_OT // 2) as i:
                for s in range(2):
                    add(2 * i + s, s)

        @block.tensor
        def _(pe):
            pe.sem_inc(y_done, 2)
            pe.sem_inc(turned, 2)

            def step(c, s, split_wait):
                pe.wait_ge(ld_x[s], 8 * c + (16 - 8 * s))
                pe.wait_ge(add_done, c + 1)
                for k in range(KD):
                    last = pe.transpose(x_ps[s][:, k // 4, k % 4 * P:(k % 4 + 1) * P], x[:, s, k], ident[:])
                last.then_inc(turned, 1)
                pe.wait_ge(ml_done, c + 1 + 2)
                for n in range(2):
                    cols = slice(n * (D // 2), (n + 1) * (D // 2))
                    for k in range(KD):
                        if split_wait and n == 0:
                            pe.wait_ge(wl_done, k + 1)
                        for i, (l, r) in enumerate(((mh, wh), (ml, wh), (mh, wl))):
                            last = pe.matmul(y_ps[s][:, n], l[:, s, k], r[:, k, cols], start=(k == 0 and i == 0),
                                             stop=(k == KD - 1 and i == 2))
                last.then_inc(y_done, 1)

            for s in range(2):
                step(s, s, s == 0)
            with pe.Fori(1, N_OT // 2) as i:
                for s in range(2):
                    step(2 * i + s, s, False)


def layouts(a):
    import numpy as np
    c = np.ascontiguousarray
    x = a["x"][0]
    pair = lambda v: v.reshape(NP, 2 * 64, *v.shape[2:]).swapaxes(0, 1)
    out = {}
    out["x_chunk"] = c(x.reshape(NCH, T, D))
    out["x_group"] = c(x.reshape(NCH, 2, S8, 2 * NP, H).transpose(2, 4, 1, 3, 0).reshape(P, 2, 2 * NP, NCH))
    dt = np.repeat(a["ssm_log_dt"][0][:, None], 64, 1)
    out["s5_prm"] = c(np.stack([pair(a["ssm_lam_re"][0]), pair(a["ssm_lam_im"][0]), pair(dt)], 1))
    cT = lambda v: pair(v.swapaxes(1, 2))
    out["s5_bc"] = c(np.stack([pair(a["ssm_b_re"][0]), pair(a["ssm_b_im"][0]),
                               cT(a["ssm_c_re"][0]), cT(a["ssm_c_im"][0])], 1))
    g = a["norm_mix"][0].reshape(NP, 2, 1, H)
    out["s5_gain"] = c(np.repeat(g, 64, 2).reshape(NP, P, H).swapaxes(0, 1))
    out["s5_skip"] = c(np.stack([a["ssm_d"][0].reshape(NP, 2 * H).T, a["norm_mix"][0].reshape(NP, 2 * H).T], 1))
    return out


def tiles(w, cols, k_tiles=None):
    import numpy as np
    w = w[:, cols]
    k = w.shape[0] // P
    return np.ascontiguousarray(w.reshape(k, P, -1, P).transpose(2, 1, 0, 3).reshape(-1, P, k * P))


FM_COLS = [(0, 512), (768, 1024), (1024, 2048), (3592, 4360)]
TM_SRC = [(512, 768), (2048, 3584)]
GI_COLS = (3584, 3592)


def layouts2(a):
    import numpy as np
    c = np.ascontiguousarray
    out = {}
    by_feat = lambda v: c(v.T.reshape(-1, P, SEQ))
    out["x_feat"], out["p_feat"] = by_feat(a["x"][0]), by_feat(a["p"][0, 0])
    out["gains"] = c(np.stack([a[k].reshape(KD, P).T for k in ("norm_ffn", "norm_ple", "norm_final", "norm_g_2")], 1))
    glu, w1, w2 = a["ssm_w_glu"][0], a["mlp_w1"][0], a["mlp_w2"][0]
    order = lambda spans: np.concatenate([np.arange(*s) for s in spans])
    glu_t = tiles(glu, slice(None))
    parts = [glu_t[i] for m in range(KD) for i in (KD + m, m)]
    w1_t = tiles(w1, slice(None))
    w2_t = tiles(w2, slice(None)).reshape(KD // 2, 2, P, F_GROUPS, F_TILES * P)
    for fg in range(F_GROUPS):
        parts += [w1_t[fg * F_TILES + f] for f in range(F_TILES)]
        parts += [w2_t[m2, :, :, fg].transpose(1, 0, 2).reshape(P, -1) for m2 in range(KD // 2)]
    gate_t, ple_t = tiles(a["ple_gate_w"][0], slice(None)), tiles(a["ple_w"][0], slice(None))
    for m in range(KD):
        parts += [gate_t[m], np.tile(ple_t[m], (1, 4))]
    w_in = a["w_in_2"][0]
    parts += list(tiles(w_in, order(FM_COLS))) + list(tiles(w_in, order(TM_SRC)))
    out["wall"] = c(np.stack(parts))
    out["w_gi"] = c(w_in[:, GI_COLS[0]:GI_COLS[1]].reshape(KD, P, 8).transpose(1, 0, 2))
    return out


def layouts3(a):
    import numpy as np
    c = np.ascontiguousarray
    out = {}
    out["att_gain"] = c(np.stack([np.tile(a[k][0], P // A_DIM) for k in ("att_q_g_2", "att_k_g_2")], 1))
    rel = np.clip(np.arange(QB)[:, None] - np.arange(WIN)[None, :] + (WIN - QB), -128, 128) + 128
    out["att_bias"] = c(a["att_rel_bias_2"][0][:, rel].swapaxes(0, 1))
    per = lambda v, n: v.reshape(*v.shape[:-1], n, P)
    out["ml_cw"] = c(per(a["ml_qk_conv_w_2"][0], 2 * M_HEADS).transpose(2, 1, 0))
    out["ml_cb"] = c(per(a["ml_qk_conv_b_2"][0], 2 * M_HEADS).T)
    out["ml_bif"] = c(np.stack([a["ml_b_i_2"][0], a["ml_b_f_2"][0]], 1))
    out["ml_gain"] = c(per(a["ml_out_g_2"][0], M_HEADS).T)
    out["cv_w"] = c(per(a["cv_dw_w_2"][0], C_TILES).transpose(2, 1, 0))
    out["cv_par"] = c(np.stack([per(a[k][0], C_TILES).T for k in ("cv_dw_b_2", "cv_ln_g_2", "cv_ln_b_2")], 1))
    out["w_out"] = c(a["w_out_2"][0])
    return out


def scratch(nc, d):
    shapes = {
        "ca": (P, NQ, 2 * QP * (T + 1) * H), "z": (1, 2 * NP * H, (S8 - 1) * H + T * H),
        "y_hi": (KD, P, SEQ), "y_lo": (KD, P, SEQ),
        "x2": (KD, P, SEQ),
        "fm": (N_FM, P, SEQ), "gi": (2 * M_HEADS, SEQ), "tm": (SEQ, sum(TM_COLS)),
        "rows": (2, M_HEADS, SEQ), "mixed": (KD, P, SEQ),
    }
    for name, shape in shapes.items():
        if name not in d:
            d[name] = nc.dram_tensor(name + "_scratch", shape, F32).ap()


def program(nc, d):
    scratch(nc, d)
    env = {}
    with ExitStack() as ctx:
        constants(nc, env, ctx)
        s5_stage(nc, env, d)
        for stage in (dense, attention, mlstm, conv_mixer, final):
            with ExitStack() as c:
                stage(nc, env, d, c)


def kernel(**inputs):
    import numpy as np
    import concourse.bacc as bacc
    from concourse.bass_utils import run_bass_kernel_spmd
    a = {k: np.asarray(v) for k, v in inputs.items()}
    arrays = {"in_" + k: v for part in (layouts, layouts2, layouts3) for k, v in part(a).items()}
    nc = bacc.Bacc("TRN2", target_bir_lowering=False, num_devices=1)
    d = {k[3:]: nc.dram_tensor(k, v.shape, F32, kind="ExternalInput").ap() for k, v in arrays.items()}
    d["out"] = nc.dram_tensor("out", (SEQ, D), F32, kind="ExternalOutput").ap()
    program(nc, d)
    r = run_bass_kernel_spmd(nc, [arrays], core_ids=[0])
    return r.results[0]["out"].reshape(1, SEQ, D)
```

```python
from contextlib import ExitStack

import concourse.bass as bass
from concourse import mybir

ALU = mybir.AluOpType
ACT = mybir.ActivationFunctionType
AX = mybir.AxisListType
F32 = mybir.dt.float32
F32R = mybir.dt.float32r

P = 128
SEQ = 2048
D = 1024
EPS = 1e-6
TWO_PI = 6.283185307179586
PI_LOW = 3.1415925
PI2_A, PI2_B = 6.28125, 0.0019350051879882812
PI2_C = TWO_PI - PI2_A - PI2_B
ROUND = 1.5 * 2.0 ** 23


def tools(nc, ctx):
    held = []

    def release():
        nc.clear_and_free_semaphores(held)
        nc.all_engine_barrier()

    ctx.callback(release)

    def sb(name, shape, dt=F32):
        return ctx.enter_context(nc.sbuf_tensor(name, shape, dt))

    def ps(name, shape):
        return ctx.enter_context(nc.psum_tensor(name, shape, F32))

    def sem(name):
        held.append(nc.alloc_semaphore(name))
        return held[-1]

    return sb, ps, sem


T = 16
NCH = SEQ // T
NP = 32
H = 16
S8 = 8
QP = 4
NQ = NP // QP
QS = 2
NS = NP // QS


def s5_setup(nc, env, d, ctx):
    sb, ps, sem = tools(nc, ctx)
    U, Win, ident = env["U"], env["Win"], env["ident"]
    aT, eps = env["aT"], env["eps"]
    prm = sb("s5_prm", [P, 3, NP])
    bc = sb("s5_bc", [P, 4, NP, H])
    gain = sb("s5_gain", [P, NP, H])
    skip = sb("s5_skip", [2 * H, 2, NP])
    xin = sb("s5_xin", [P, 2, D])
    ss = sb("s5_ss", [P, T])
    rms = sb("s5_rms", [P, T])
    rexp = sb("s5_rexp", [P, 2, S8, H])
    rtile = sb("s5_rtile", [P, 2, NCH])
    w = sb("s5_w", [P, 16, NP])
    pw = sb("s5_pw", [P, 2, NP, T + 1])
    pwr = sb("s5_pwr", [P, 2, NP, T])
    bb = sb("s5_bb", [P, 2, NP, H])
    bbd = sb("s5_bbd", [P, 2, NP, 2, H])
    cas = [sb(f"s5_ca{i}", [P, 2, QS, T + 1, H]) for i in range(2)]
    cat = sb("s5_cat", [P, 2, QS, T + 1, H])
    ab = sb("s5_ab", [P, 2, QS, T, H])
    tmp = sb("s5_tmp", [P, 4, NP, H])
    bt, pt = tmp, tmp
    abt = sb("s5_abt", [P, 2, QS, T, H])
    zss = [sb(f"s5_zs{i}", [2 * H, QS, T * H]) for i in range(2)]
    zz = sb("s5_zz", [2 * H, NP, H])
    eyeh = sb("s5_eyeh", [2 * H, H])
    zero = sb("s5_zero", [P, (S8 - 1) * H])
    pst = ps("s5_pst", [P, 4, NCH])
    psz = [ps(f"s5_psz{i}", [2 * H, 2, T * H]) for i in range(2)]
    psw = [ps(f"s5_psw{i}", [P, 4, P]) for i in range(2)]
    ld_prm, ld_u = sem("s5_ld_prm"), sem("s5_ld_u")
    ld_x = [sem("s5_ld_x0"), sem("s5_ld_x1")]
    act_prm, sq_done, rms_sqrt = sem("s5_act_prm"), sem("s5_sq_done"), sem("s5_rms_sqrt")
    dve_prm, dve_rms, r_copied = sem("s5_dve_prm"), sem("s5_dve_rms"), sem("s5_r_copied")
    rexp_done, r_turned = sem("s5_rexp_done"), sem("s5_r_turned")
    chain, pchain = sem("s5_chain"), sem("s5_pchain")
    bb_ready, ca_ready, ab_ready = sem("s5_bb_ready"), sem("s5_ca_ready"), sem("s5_ab_ready")
    z_mm, ab_turned, z_ready, win_ready = sem("s5_z_mm"), sem("s5_ab_turned"), sem("s5_z_ready"), sem("s5_win_ready")
    st_ca, st_z = [sem("s5_st_ca0"), sem("s5_st_ca1")], [sem("s5_st_z0"), sem("s5_st_z1")]
    st_zero, zero_set, pool_set = sem("s5_st_zero"), sem("s5_zero_set"), sem("s5_pool_set")
    pw_ready, ca_free, u_done = sem("s5_pw_ready"), sem("s5_ca_free"), sem("s5_u_done")

    with nc.Block() as block:
        @block.sync
        def _(sp):
            sp.dma_start(prm[:], d["s5_prm"]).then_inc(ld_prm, 16)
            sp.dma_start(bc[:], d["s5_bc"]).then_inc(ld_prm, 16)
            sp.dma_start(gain[:], d["s5_gain"]).then_inc(ld_prm, 16)
            sp.dma_start(skip[:], d["s5_skip"]).then_inc(ld_prm, 16)
            for i in range(T):
                if i >= 2:
                    sp.wait_ge(sq_done, i - 1)
                sp.dma_start(xin[:, i % 2], d["x_chunk"][:, i]).then_inc(ld_x[i % 2], 16)
            for hf in range(2):
                sp.dma_start(U[:, hf], d["x_group"][:, hf]).then_inc(ld_u, 16)
            sp.wait_ge(zero_set, 1)
            for i in range(2):
                sp.dma_start(d["z"][:, i * 512:(i + 1) * 512, 0:(S8 - 1) * H].rearrange("o (a b) n -> (o a) b n", a=P),
                             zero[:, None, :].to_broadcast([P, 4, (S8 - 1) * H])).then_inc(st_zero, 16)
            def store_taps(q):
                sp.wait_ge(z_ready, q + 1)
                sp.dma_start(d["z"][0].rearrange("(j g) n -> g j n", g=2 * H)[:, q * QS:(q + 1) * QS, (S8 - 1) * H:],
                             zss[q % 2][:]).then_inc(st_z[q % 2], 16)

            for q in range(NS):
                sp.wait_ge(ca_ready, q + 1)
                lo = q % (QP // QS) * QS
                sp.dma_start(d["ca"][:, q // (QP // QS)].rearrange("p (r j n) -> p r j n", r=2, j=QP)[:, :, lo:lo + QS],
                             cas[q % 2][:].rearrange("p r j t h -> p r j (t h)")).then_inc(st_ca[q % 2], 16)
                if q:
                    store_taps(q - 1)
            store_taps(NS - 1)
            for i in range(2):
                sp.wait_ge(st_ca[i], 16 * (NS // 2))
                sp.wait_ge(st_z[i], 16 * (NS // 2))
            sp.wait_ge(st_zero, 32)

        @block.scalar
        def _(act):
            act.wait_ge(ld_prm, 64)
            act.activation(w[:, 0], prm[:, 2], ACT.Exp).then_inc(act_prm, 1)
            act.wait_ge(dve_prm, 1)
            act.activation(w[:, 2], w[:, 1], ACT.Exp).then_inc(act_prm, 1)
            act.wait_ge(dve_prm, 2)
            act.activation(w[:, 8], w[:, 7], ACT.Sin).then_inc(act_prm, 1)
            act.activation(w[:, 9], w[:, 7], ACT.Abs).then_inc(act_prm, 1)
            act.wait_ge(act_prm, 4)
            act.activation(w[:, 10], w[:, 9], ACT.Sin, scale=-1.0, bias=env["halfpi"][:]).then_inc(act_prm, 1)
            for i in range(T):
                act.wait_ge(ld_x[i % 2], 16 * (i // 2 + 1))
                act.activation(xin[:, i % 2], xin[:, i % 2], ACT.Square, accum_out=ss[:, i:i + 1]).then_inc(sq_done, 1)
            act.wait_ge(sq_done, T)
            act.activation(rms[:], ss[:], ACT.Sqrt, scale=1.0 / D, bias=eps[:]).then_inc(rms_sqrt, 1)
            act.wait_ge(r_turned, 2)
            act.copy(rtile[:], pst[:, 0:2]).then_inc(r_copied, 1)
            for j in range(NP):
                act.wait_ge(ab_turned, j + 1)
                act.copy(Win[:, j].rearrange("p a b m -> p (a b) m"), psw[j % 2][:]).then_inc(win_ready, 1)

        @block.vector
        def _(dve):
            n = [0]

            def then(ins):
                n[0] += 1
                ins.then_inc(chain, 1)
                dve.wait_ge(chain, n[0])

            dve.wait_ge(ld_prm, 64)
            dve.wait_ge(act_prm, 1)
            dve.tensor_tensor(w[:, 1], prm[:, 0], w[:, 0], ALU.mult).then_inc(dve_prm, 1)
            then(dve.tensor_tensor(w[:, 3], prm[:, 1], w[:, 0], ALU.mult))
            then(dve.tensor_scalar(w[:, 4], w[:, 3], 1.0 / TWO_PI, ROUND, ALU.mult, ALU.add))
            then(dve.tensor_scalar(w[:, 5], w[:, 4], ROUND, None, ALU.subtract))
            then(dve.scalar_tensor_tensor(w[:, 6], w[:, 5], -PI2_A, w[:, 3], ALU.mult, ALU.add))
            then(dve.scalar_tensor_tensor(w[:, 3], w[:, 5], -PI2_B, w[:, 6], ALU.mult, ALU.add))
            then(dve.scalar_tensor_tensor(w[:, 6], w[:, 5], -PI2_C, w[:, 3], ALU.mult, ALU.add))
            dve.tensor_scalar(w[:, 7], w[:, 6], PI_LOW, -PI_LOW, ALU.min, ALU.max).then_inc(dve_prm, 1)
            dve.wait_ge(act_prm, 5)
            a1r, a1i = pw[:, 0, :, 1], pw[:, 1, :, 1]
            then(dve.tensor_tensor(a1r, w[:, 2], w[:, 10], ALU.mult))
            then(dve.tensor_tensor(a1i, w[:, 2], w[:, 8], ALU.mult))
            then(dve.memset(pw[:, 0, :, 0:1], 1.0))
            then(dve.memset(pw[:, 1, :, 0:1], 0.0))
            lr, li = prm[:, 0], prm[:, 1]
            then(dve.tensor_scalar(w[:, 0], a1r, -1.0, None, ALU.add))
            then(dve.tensor_tensor(w[:, 3], lr, lr, ALU.mult))
            then(dve.tensor_tensor(w[:, 4], li, li, ALU.mult))
            then(dve.tensor_tensor(w[:, 5], w[:, 3], w[:, 4], ALU.add))
            then(dve.reciprocal(w[:, 6], w[:, 5]))
            then(dve.tensor_tensor(w[:, 3], w[:, 0], lr, ALU.mult))
            then(dve.tensor_tensor(w[:, 4], a1i, li, ALU.mult))
            then(dve.tensor_tensor(w[:, 5], w[:, 3], w[:, 4], ALU.add))
            then(dve.tensor_tensor(w[:, 11], w[:, 5], w[:, 6], ALU.mult))
            then(dve.tensor_tensor(w[:, 3], a1i, lr, ALU.mult))
            then(dve.tensor_tensor(w[:, 4], w[:, 0], li, ALU.mult))
            then(dve.tensor_tensor(w[:, 5], w[:, 3], w[:, 4], ALU.subtract))
            then(dve.tensor_tensor(w[:, 12], w[:, 5], w[:, 6], ALU.mult))
            cr = w[:, 11, :, None].to_broadcast([P, NP, H])
            ci = w[:, 12, :, None].to_broadcast([P, NP, H])
            then(dve.tensor_tensor(bt[:, 0], bc[:, 0], cr, ALU.mult))
            then(dve.tensor_tensor(bt[:, 1], bc[:, 1], ci, ALU.mult))
            then(dve.tensor_tensor(bt[:, 2], bc[:, 1], cr, ALU.mult))
            then(dve.tensor_tensor(bt[:, 3], bc[:, 0], ci, ALU.mult))
            then(dve.tensor_tensor(bt[:, 0], bt[:, 0], bt[:, 1], ALU.subtract))
            then(dve.tensor_tensor(bt[:, 2], bt[:, 2], bt[:, 3], ALU.add))
            then(dve.tensor_tensor(bb[:, 0], bt[:, 0], gain[:], ALU.mult))
            then(dve.tensor_tensor(bb[:, 1], bt[:, 2], gain[:], ALU.mult))
            m = 1
            while m < T:
                lo_r, lo_i = pw[:, 0, :, 1:m + 1], pw[:, 1, :, 1:m + 1]
                tr = pw[:, 0, :, m:m + 1].to_broadcast([P, NP, m])
                ti = pw[:, 1, :, m:m + 1].to_broadcast([P, NP, m])
                then(dve.tensor_tensor(pt[:, 0, :, 0:m], lo_r, tr, ALU.mult))
                then(dve.tensor_tensor(pt[:, 1, :, 0:m], lo_i, ti, ALU.mult))
                then(dve.tensor_tensor(pt[:, 2, :, 0:m], lo_r, ti, ALU.mult))
                then(dve.tensor_tensor(pt[:, 3, :, 0:m], lo_i, tr, ALU.mult))
                then(dve.tensor_tensor(pw[:, 0, :, m + 1:2 * m + 1], pt[:, 0, :, 0:m], pt[:, 1, :, 0:m], ALU.subtract))
                then(dve.tensor_tensor(pw[:, 1, :, m + 1:2 * m + 1], pt[:, 2, :, 0:m], pt[:, 3, :, 0:m], ALU.add))
                m *= 2
            for s in range(T):
                then(dve.tensor_copy(pwr[:, :, :, s], pw[:, :, :, T - 1 - s]))
            then(dve.tensor_copy(aT[:, 0], pw[:, 0, :, T]))
            then(dve.tensor_copy(aT[:, 1], pw[:, 1, :, T]))
            then(dve.memset(bbd[:], 0.0))
            for g in range(2):
                rows = slice(g * 64, (g + 1) * 64)
                then(dve.tensor_copy(bbd[rows, :, :, g, :], bb[rows]))
            dve.tensor_scalar(w[:, 13], w[:, 11], 0.0, None, ALU.add).then_inc(bb_ready, 1)
            dve.wait_ge(pool_set, 2)
            then(dve.tensor_tensor(w[0:2 * H, 14], skip[:, 0], skip[:, 1], ALU.mult))
            then(dve.tensor_tensor(zz[:], eyeh[:, None, :].to_broadcast([2 * H, NP, H]),
                                   w[0:2 * H, 14, :, None].to_broadcast([2 * H, NP, H]), ALU.mult))
            dve.wait_ge(rms_sqrt, 1)
            then(dve.reciprocal(ss[:], rms[:]))
            dve.tensor_copy(rexp[:].rearrange("p a s h -> p (a s) h"),
                            ss[:, :, None].to_broadcast([P, T, H])).then_inc(rexp_done, 1)
            def taps(q):
                js = slice(q * QS, (q + 1) * QS)
                dve.wait_ge(z_mm, q + 1)
                if q >= 2:
                    dve.wait_ge(st_z[q % 2], 16 * (q // 2))
                out = zss[q % 2][:].rearrange("p j (t h) -> p j t h", h=H)
                src = psz[q % 2][:].rearrange("p j (t h) -> p j t h", h=H)
                dve.tensor_copy(out[:, :, 1:], src[:, :, 1:])
                dve.tensor_tensor(out[:, :, 0], src[:, :, 0], zz[:, js], ALU.add).then_inc(z_ready, 1)

            for q in range(NS):
                js = slice(q * QS, (q + 1) * QS)
                shape = [P, QS, T + 1, H]
                c_r = bc[:, 2, js, None, :].to_broadcast(shape)
                c_i = bc[:, 3, js, None, :].to_broadcast(shape)
                p_r = pw[:, 0, js, :, None].to_broadcast(shape)
                p_i = pw[:, 1, js, :, None].to_broadcast(shape)
                ca = cas[q % 2]
                if q >= 2:
                    dve.wait_ge(st_ca[q % 2], 16 * (q // 2))
                    dve.wait_ge(z_mm, q - 1)
                then(dve.tensor_tensor(cat[:, 0], c_r, p_r, ALU.mult))
                then(dve.tensor_tensor(cat[:, 1], c_i, p_i, ALU.mult))
                then(dve.tensor_tensor(ca[:, 0], cat[:, 0], cat[:, 1], ALU.subtract))
                then(dve.tensor_tensor(cat[:, 0], c_r, p_i, ALU.mult))
                then(dve.tensor_tensor(cat[:, 1], c_i, p_r, ALU.mult))
                dve.scalar_tensor_tensor(ca[:, 1], cat[:, 0], -1.0, cat[:, 1], ALU.mult, ALU.subtract).then_inc(ca_ready, 1)
                dve.wait_ge(ca_ready, q + 1)
                if q:
                    taps(q - 1)
                if q in (NS - 2, NS - 1):
                    hf = q - (NS - 2)
                    dve.wait_ge(r_copied, 1)
                    dve.wait_ge(ld_u, 32)
                    dve.tensor_tensor(U[:, hf], U[:, hf], rtile[:, hf, None, :].to_broadcast([P, 2 * NP, NCH]),
                                      ALU.mult).then_inc(u_done, 1)
            taps(NS - 1)

        @block.gpsimd
        def _(pool):
            n = [0]

            def then(ins):
                n[0] += 1
                ins.then_inc(pchain, 1)
                pool.wait_ge(pchain, n[0])

            pool.memset(zero[:], 0.0).then_inc(zero_set, 1)
            pool.memset(eyeh[:], 0.0).then_inc(pool_set, 1)
            pool.wait_ge(pool_set, 1)
            then(pool.affine_select(out=eyeh[:], in_=eyeh[:], compare_op=ALU.not_equal, fill=1.0, base=0,
                                    pattern=[[-1, H]], channel_multiplier=1))
            pool.affine_select(out=eyeh[:], in_=eyeh[:], compare_op=ALU.not_equal, fill=1.0, base=-H,
                               pattern=[[-1, H]], channel_multiplier=1).then_inc(pool_set, 1)
            pool.wait_ge(bb_ready, 1)
            for q in range(NS):
                js = slice(q * QS, (q + 1) * QS)
                shape = [P, QS, T, H]
                b_r = bb[:, 0, js, None, :].to_broadcast(shape)
                b_i = bb[:, 1, js, None, :].to_broadcast(shape)
                p_r = pwr[:, 0, js, :, None].to_broadcast(shape)
                p_i = pwr[:, 1, js, :, None].to_broadcast(shape)
                then(pool.tensor_tensor(abt[:, 0], b_r, p_r, ALU.mult))
                then(pool.tensor_tensor(abt[:, 1], b_i, p_i, ALU.mult))
                if q:
                    pool.wait_ge(ab_turned, QS * q)
                then(pool.tensor_tensor(ab[:, 0], abt[:, 0], abt[:, 1], ALU.subtract))
                then(pool.tensor_tensor(abt[:, 0], b_r, p_i, ALU.mult))
                then(pool.tensor_tensor(abt[:, 1], b_i, p_r, ALU.mult))
                pool.tensor_tensor(ab[:, 1], abt[:, 0], abt[:, 1], ALU.add).then_inc(ab_ready, 1)
                pool.wait_ge(ab_ready, q + 1)

        @block.tensor
        def _(pe):
            pe.wait_ge(rexp_done, 1)
            for hf in range(2):
                pe.transpose(pst[:, hf], rexp[:, hf].rearrange("p s h -> p (s h)"), ident[:]).then_inc(r_turned, 1)
            for q in range(NS):
                pe.wait_ge(ca_ready, q + 1)
                if q >= 2:
                    pe.wait_ge(z_ready, q - 1)
                for jj in range(QS):
                    for ri in range(2):
                        last = pe.matmul(psz[q % 2][:, jj], bbd[:, ri, q * QS + jj].rearrange("p g h -> p (g h)"),
                                         cas[q % 2][:, ri, jj, 0:T].rearrange("p t h -> p (t h)"),
                                         start=(ri == 0), stop=(ri == 1))
                last.then_inc(z_mm, 1)
                pe.wait_ge(ab_ready, q + 1)
                for jj in range(QS):
                    j = q * QS + jj
                    if j >= 2:
                        pe.wait_ge(win_ready, j - 1)
                    for hf in range(2):
                        for ri in range(2):
                            last = pe.transpose(psw[j % 2][:, 2 * hf + ri],
                                                ab[:, ri, jj, hf * S8:(hf + 1) * S8].rearrange("p s h -> p (s h)"), ident[:])
                    last.then_inc(ab_turned, 1)


def s5_states(nc, env, d, ctx):
    sb, ps, sem = tools(nc, ctx)
    U, Win, aT, xs = env["U"], env["Win"], env["aT"], env["xs"]
    SC, SU = 8, NCH // 8
    t1 = sb("s5_t1", [P, 2, NP, SU])
    t2 = sb("s5_t2", [P, 2, NP, SU])
    ap = sb("s5_ap", [P, 2, NP, SU])
    ani = sb("s5_ani", [P, NP])
    psx = [ps(f"s5_psx{i}", [P, 2, 2, NCH]) for i in range(4)]
    x_mm, x_copied, chain, pchain = sem("s5_x_mm"), sem("s5_x_copied"), sem("s5_scan"), sem("s5_pool_scan")
    BY_DVE = 22
    with nc.Block() as block:
        @block.tensor
        def _(pe):
            for i in range(NP // 2):
                if i >= 4:
                    pe.wait_ge(x_copied, i - 3)
                for jj in range(2):
                    j = 2 * i + jj
                    for g in range(2):
                        for ri in range(2):
                            for hf in range(2):
                                last = pe.matmul(psx[i % 4][g * 64:(g + 1) * 64, ri, jj],
                                                 Win[:, j, hf, ri, g * 64:(g + 1) * 64], U[:, hf, 2 * j + g],
                                                 start=(hf == 0), stop=(hf == 1))
                last.then_inc(x_mm, 1)

        @block.scalar
        def _(act):
            for i in range(NP // 2):
                act.wait_ge(x_mm, i + 1)
                act.copy(xs[:, :, 2 * i:2 * i + 2, 1:NCH + 1], psx[i % 4][:]).then_inc(x_copied, 1)

        def scan(eng, chain, js):
            n, pairs = [0], js.stop - js.start

            def then(ins):
                n[0] += 1
                ins.then_inc(chain, 1)
                eng.wait_ge(chain, n[0])

            def times(out, v, ar, ai, tmp):
                eng.tensor_tensor(out[0], v[0], ar, ALU.mult).then_inc(chain, 1)
                eng.tensor_tensor(out[1], v[1], ar, ALU.mult).then_inc(chain, 1)
                eng.tensor_tensor(tmp[0], v[1], ai, ALU.mult).then_inc(chain, 1)
                n[0] += 3
                then(eng.tensor_tensor(tmp[1], v[0], ai, ALU.mult))
                eng.tensor_tensor(out[0], out[0], tmp[0], ALU.subtract).then_inc(chain, 1)
                n[0] += 1
                then(eng.tensor_tensor(out[1], out[1], tmp[1], ALU.add))

            eng.memset(xs[:, :, js, 0:1], 0.0)
            then(eng.tensor_copy(ap[:, :, js, 0], aT[:, :, js]))
            m = 1
            while m < SU:
                shape = [P, pairs, m]
                times([ap[:, r, js, m:2 * m] for r in range(2)], [ap[:, r, js, 0:m] for r in range(2)],
                      ap[:, 0, js, m - 1:m].to_broadcast(shape), ap[:, 1, js, m - 1:m].to_broadcast(shape),
                      [t2[:, r, js, 0:m] for r in range(2)])
                m *= 2
            eng.wait_ge(x_copied, NP // 2)
            view = [xs[:, r, js, 1:].rearrange("p j (c u) -> p j c u", u=SU) for r in range(2)]
            shape = [P, pairs, SC]
            ar, ai = (aT[:, r, js, None].to_broadcast(shape) for r in range(2))
            for u in range(1, SU):
                o = [t1[:, r, js, 0:SC] for r in range(2)]
                times(o, [view[r][:, :, :, u - 1] for r in range(2)], ar, ai, [t2[:, r, js, 0:SC] for r in range(2)])
                eng.tensor_tensor(view[0][:, :, :, u], view[0][:, :, :, u], o[0], ALU.add).then_inc(chain, 1)
                n[0] += 1
                then(eng.tensor_tensor(view[1][:, :, :, u], view[1][:, :, :, u], o[1], ALU.add))
            shape = [P, pairs, SU]
            for c in range(1, SC):
                o = [t1[:, r, js] for r in range(2)]
                v = [xs[:, r, js, c * SU:c * SU + 1].to_broadcast(shape) for r in range(2)]
                times(o, v, ap[:, 0, js], ap[:, 1, js], [t2[:, r, js] for r in range(2)])
                eng.tensor_tensor(view[0][:, :, c], view[0][:, :, c], o[0], ALU.add).then_inc(chain, 1)
                n[0] += 1
                then(eng.tensor_tensor(view[1][:, :, c], view[1][:, :, c], o[1], ALU.add))

        @block.vector
        def _(dve):
            scan(dve, chain, slice(0, BY_DVE))

        @block.gpsimd
        def _(pool):
            scan(pool, pchain, slice(BY_DVE, NP))


def s5_outputs(nc, env, d, ctx):
    sb, ps, sem = tools(nc, ctx)
    U, xs, ident = env["U"], env["xs"], env["ident"]
    G8 = 2 * QP
    mt = sb("s5_mt", [P, 2, G8, T * H])
    ca = sb("s5_cao", [P, 2, 2, QP, (T + 1) * H])
    yc = sb("s5_yc", [P, 2, T, P])
    yh = sb("s5_yh", [P, 2, SEQ], F32R)
    yl = sb("s5_yl", [P, 2, SEQ], F32R)
    psy = [ps(f"s5_psy{i}", [P, 2, T * H]) for i in range(4)]
    psq = [ps(f"s5_psq{i}", [P, 4, NCH]) for i in range(4)]
    ld_m = [sem("s5_ld_m0"), sem("s5_ld_m1")]
    ld_c = [sem("s5_ld_c0"), sem("s5_ld_c1")]
    y_mm, gelu_done, y_turned, hi_done, lo_done = (sem("s5_" + x) for x in ("y_mm", "gelu_done", "y_turned", "hi_done", "lo_done"))
    st_y = [sem("s5_st_y0"), sem("s5_st_y1")]
    with nc.Block() as block:
        @block.sync
        def _(sp):
            def load(q):
                if q >= 2:
                    sp.wait_ge(y_mm, 2 * (q - 1))
                for s in range(S8):
                    lo = (S8 - 1 - s) * H
                    sp.dma_start(mt[s * H:(s + 1) * H, q % 2],
                                 d["z"][0].rearrange("(g h) n -> h g n", h=H)[:, q * G8:(q + 1) * G8, lo:lo + T * H]
                                 ).then_inc(ld_m[q % 2], 16)
                sp.dma_start(ca[:, q % 2].rearrange("p r j n -> p (r j n)"), d["ca"][:, q]).then_inc(ld_c[q % 2], 16)

            load(0)
            load(1)
            for q in range(NQ):
                if q + 2 < NQ:
                    load(q + 2)
                sp.wait_ge(hi_done, 4 * (q + 1))
                sp.dma_start(d["y_hi"][q], yh[:, q % 2].bitcast(F32)).then_inc(st_y[q % 2], 16)
                sp.wait_ge(lo_done, 4 * (q + 1))
                sp.dma_start(d["y_lo"][q], yl[:, q % 2].bitcast(F32)).then_inc(st_y[q % 2], 16)
            for i in range(2):
                sp.wait_ge(st_y[i], 32 * (NQ // 2))

        @block.tensor
        def _(pe):
            def outputs(q):
                pe.wait_ge(ld_m[q % 2], 16 * S8 * (q // 2 + 1))
                pe.wait_ge(ld_c[q % 2], 16 * (q // 2 + 1))
                for pr in range(2):
                    if q:
                        pe.wait_ge(gelu_done, 4 * (q - 1) + 2 * pr + 2)
                    for jj in (2 * pr, 2 * pr + 1):
                        j = q * QP + jj
                        for g in range(2):
                            o, m = psy[2 * pr + g][:, jj % 2], mt[:, q % 2, 2 * jj + g]
                            rows = slice(g * 64, (g + 1) * 64)
                            pe.matmul(o, U[:, 0, 2 * j + g], m, start=True, stop=False)
                            pe.matmul(o[:, T * H // 2:], U[:, 1, 2 * j + g], m[:, 0:T * H // 2], start=False, stop=False)
                            for ri in range(2):
                                last = pe.matmul(o, xs[rows, ri, j, 0:NCH], ca[rows, q % 2, ri, jj, H:],
                                                 start=False, stop=(ri == 1))
                    last.then_inc(y_mm, 1)

            def turn(q):
                pe.wait_ge(gelu_done, 4 * (q + 1))
                for i in range(4):
                    if q:
                        pe.wait_ge(lo_done, 4 * (q - 1) + i + 1)
                    for t in range(4):
                        last = pe.transpose(psq[i][:, t], yc[:, q % 2, 4 * i + t], ident[:])
                    last.then_inc(y_turned, 1)

            for q in range(NQ + 1):
                if q < NQ:
                    outputs(q)
                if q:
                    turn(q - 1)

        @block.scalar
        def _(act):
            for q in range(NQ + 1):
                if q < NQ:
                    for pr in range(2):
                        act.wait_ge(y_mm, 2 * q + pr + 1)
                        if q >= 2:
                            act.wait_ge(y_turned, 4 * (q - 1))
                        for g in range(2):
                            act.activation(yc[:, q % 2].rearrange("p t (j g h) -> p j g t h", h=H, g=2)[:, 2 * pr:2 * pr + 2, g],
                                           psy[2 * pr + g][:].rearrange("p j (t h) -> p j t h", h=H),
                                           ACT.Gelu_apprx_tanh).then_inc(gelu_done, 1)
                if q:
                    r = q - 1
                    for i in range(4):
                        act.wait_ge(y_turned, 4 * r + i + 1)
                        if r >= 2:
                            act.wait_ge(st_y[r % 2], 32 * (r // 2))
                        act.copy(yh[:, r % 2].rearrange("p (c t) -> p t c", t=T)[:, 4 * i:4 * i + 4],
                                 psq[i][:]).then_inc(hi_done, 1)

        @block.vector
        def _(dve):
            for q in range(NQ):
                for i in range(4):
                    dve.wait_ge(hi_done, 4 * q + i + 1)
                    view = (slice(None), slice(4 * i, 4 * i + 4))
                    dve.tensor_tensor(yl[:, q % 2].rearrange("p (c t) -> p t c", t=T)[view], psq[i][:],
                                      yh[:, q % 2].rearrange("p (c t) -> p t c", t=T)[view].bitcast(F32),
                                      ALU.subtract).then_inc(lo_done, 1)


def constants(nc, env, ctx):
    sb, ps, sem = tools(nc, ctx)
    env["ident"] = ident = sb("ident", [P, P])
    env["eps"] = eps = sb("eps", [P, 1])
    env["halfpi"] = halfpi = sb("halfpi", [P, 1])
    made = sem("consts_made")
    with nc.Block() as block:
        @block.gpsimd
        def _(pool):
            pool.memset(ident[:], 0.0).then_inc(made, 1)
            pool.memset(eps[:], EPS)
            pool.memset(halfpi[:], TWO_PI / 4)
            pool.wait_ge(made, 1)
            pool.affine_select(out=ident[:], in_=ident[:], compare_op=ALU.not_equal, fill=1.0, base=0,
                               pattern=[[-1, P]], channel_multiplier=1)


def s5_stage(nc, env, d):
    with ExitStack() as stage:
        env["U"] = stage.enter_context(nc.sbuf_tensor("s5_U", [P, 2, 2 * NP, NCH], F32))
        env["aT"] = stage.enter_context(nc.sbuf_tensor("s5_aT", [P, 2, NP], F32))
        with ExitStack() as win:
            env["Win"] = win.enter_context(nc.sbuf_tensor("s5_Win", [P, NP, 2, 2, P], F32, side="right"))
            with ExitStack() as ctx:
                s5_setup(nc, env, d, ctx)
            env["xs"] = stage.enter_context(nc.sbuf_tensor("s5_xs", [P, 2, NP, NCH + 1], F32))
            with ExitStack() as ctx:
                s5_states(nc, env, d, ctx)
        with ExitStack() as ctx:
            s5_outputs(nc, env, d, ctx)


NB = 2
TB = SEQ // NB
KD = D // P
F_GROUPS, F_TILES = 8, 4
N_GLU, N_MLP, N_PLE, N_FM, N_TM = 2 * KD, F_GROUPS * 2 * F_TILES, 2 * KD, 20, 14
TILE_MLP = N_GLU
TILE_PLE = TILE_MLP + N_MLP
TILE_FM = TILE_PLE + N_PLE
TILE_TM = TILE_FM + N_FM
N_TILE = TILE_TM + N_TM
JOB_STAT1 = N_GLU
JOB_MLP = JOB_STAT1 + 1
JOB_STAT2 = JOB_MLP + F_GROUPS * (F_TILES + KD)
JOB_PLE = JOB_STAT2 + 1
JOB_STAT3 = JOB_PLE + N_PLE
JOB_FM = JOB_STAT3 + 2
JOB_GI = JOB_FM + N_FM
JOB_TM = JOB_GI + 2
TM_COLS = [256, 512, 512, 512]
TM_JOBS = [2, 4, 4, 4]
N_JOB = JOB_TM + sum(TM_JOBS)
N_COPY = N_JOB - JOB_FM
C_B, C_A, C_Z, A_Z, M_QK, A_QK = (slice(*v) for v in ((0, 2), (2, 4), (4, 6), (6, 8), (8, 16), (16, 20)))
GI_AT, TM_AT = N_FM, N_FM + 2
KINDS = ["c_b"] * 2 + ["c_a"] * 2 + ["silu"] * 4 + ["conv"] * 8 + ["copy"] * 4 + ["gi"] * 2
KINDS += ["tm"] * (TM_JOBS[0] + TM_JOBS[1]) + ["tm_sigmoid"] * TM_JOBS[2] + ["tm_silu"] * TM_JOBS[3]
BY_ACT = [k in ("c_b", "silu", "tm_sigmoid", "tm_silu") for k in KINDS]
before = lambda j, by_act: sum(b == by_act for b in BY_ACT[:j])
N_BY_ACT, N_BY_DVE = before(N_COPY, True), before(N_COPY, False)
FIRST_V = 4
N_STORE = (N_COPY - FIRST_V) // 2
M_TAPS, C_TAPS = 4, 31
N_TAP = 2 * C_TAPS
MC_INC = M_TAPS + 1
TAPS_AT = {j: 3 for j in range(4, 8)} | {j: 2 for j in range(8, 16)} | {j: 3 for j in range(16, N_COPY)}
assert len(KINDS) == N_COPY and sum(TAPS_AT.values()) >= N_TAP
N_XADD = KD + KD * F_GROUPS + KD
assert N_TILE % 2 == 0 and N_JOB % 4 == 0


def dense(nc, env, d, ctx):
    sb, ps, sem = tools(nc, ctx)
    ident, eps = env["ident"], env["eps"]
    X = sb("X", [P, KD, TB])
    x_at = nc.sbuf_base - KD * TB * 4
    Tt = sb("Tt", [P, KD, TB])
    t_at = nc.sbuf_base - KD * TB * 4
    AH, AL = sb("AH", [P, KD, TB], F32R), sb("AL", [P, KD, TB], F32R)
    FH, FL = sb("FH", [P, F_TILES, TB], F32R), sb("FL", [P, F_TILES, TB], F32R)
    WR = [sb(f"WR{i}", [P, TB]) for i in range(2)]
    WH = [sb(f"WH{i}", [P, TB], F32R) for i in range(2)]
    WL = [sb(f"WL{i}", [P, TB], F32R) for i in range(2)]
    SG = [sb(f"SG{i}", [P, 2, TB // 2]) for i in range(2)]
    V = [sb(f"V{i}", [P, 2, TB // 2]) for i in range(2)]
    RB = sb("RB", [P, TB])
    ones = sb("ones_d", [P, P])
    cv_n, cu_n = 2 * TB * 4, -(-2 * (C_TAPS - 1 + TB) * 4 // 32) * 32
    CV = nc.alloc_sbuf_tensor_at("CV", [P, 2, TB], F32, offset=x_at)
    CU = nc.alloc_sbuf_tensor_at("CU", [P, 2, C_TAPS - 1 + TB], F32, offset=x_at + cv_n)
    MX = nc.alloc_sbuf_tensor_at("MX", [P, 2, M_TAPS - 1 + TB], F32, offset=x_at + cv_n + cu_n)
    cu_tail, mx_tail = sb("cu_tail", [P, 2, C_TAPS - 1]), sb("mx_tail", [P, 8, M_TAPS - 1])
    m_w, m_b = sb("d_mw", [P, 8, M_TAPS]), sb("d_mb", [P, 8])
    c_w, c_b = sb("d_cw", [P, 2, C_TAPS]), sb("d_cb", [P, 2])
    gains = sb("gains", [P, 4, KD])
    gwr = sb("gwr", [P, KD, 8])
    gwh, gwl = sb("gwh", [P, KD, 8], F32R), sb("gwl", [P, KD, 8], F32R)
    GH = [FH[:].rearrange("p a b -> p (a b)").rearrange("p (k n) -> p k n", k=KD), None]
    GL = [FL[:].rearrange("p a b -> p (a b)").rearrange("p (k n) -> p k n", k=KD), None]
    GH[1] = nc.alloc_sbuf_tensor_at("TH", [P, KD, 512], F32R, offset=t_at)[:]
    GL[1] = nc.alloc_sbuf_tensor_at("TL", [P, KD, 512], F32R, offset=t_at + KD * 512 * 4)[:]
    ps4 = [ps(f"ps_job{i}", [P, 2, TB // 2]) for i in range(4)]

    raw_loaded = [sem("raw_loaded0"), sem("raw_loaded1")]
    hi_done, raw_free = sem("w_hi_done"), sem("w_raw_free")
    job_done, sg_done, mix_done, xadd = sem("job_done"), sem("sg_done"), sem("mix_done"), sem("x_added")
    sq_done, acc_done, ln_done, r_done = sem("sq_done"), sem("acc_done"), sem("ln_done"), sem("r_done")
    t_done, ah_done, al_done, xfin = sem("t_done"), sem("ah_done"), sem("al_done"), sem("x_final")
    relu_done, v_done, fh_done, fl_done = sem("relu_done"), sem("v_done"), sem("fh_done"), sem("fl_done")
    ld_x, ld_y, ld_p, ld_g = sem("ld_x"), [sem("ld_y0"), sem("ld_y1")], sem("ld_p"), sem("ld_gains")
    ph_done, pl_done, gh_done, gl_done, ones_set = sem("ph_done"), sem("pl_done"), sem("gh_done"), sem("gl_done"), sem("ones_set")
    x_stored, gated, conv_out, silu_out = sem("x_stored"), sem("gated"), sem("conv_out"), sem("silu_out")
    mc, tap, cu_done, cu_free, ld_c, st_c, tails_set = (sem(n) for n in ("mc", "tap", "cu_done", "cu_free", "ld_c", "st_c", "tails_set"))
    copied, st_out, st_x = sem("copied"), [sem("st_out0"), sem("st_out1")], sem("st_x")
    halves = lambda v: v.rearrange("p (a b) -> p a b", a=2)

    with nc.Block() as block:
        @block.sync
        def _(sp):
            sp.dma_start(gains[:], d["gains"]).then_inc(ld_g, 16)
            sp.dma_start(gwr[:], d["w_gi"]).then_inc(ld_g, 16)
            for v, name in ((m_w, "ml_cw"), (m_b, "ml_cb"), (c_w, "cv_w"), (c_b, "cv_b")):
                sp.dma_start(v[:], d[name]).then_inc(ld_c, 16)

            def load(w, tile, s, n):
                free, at = (w + 1, tile) if n == 0 else (sp.snap(w + 1), sp.snap(tile, min_val=0, max_val=N_TILE - 1))
                sp.wait_ge(raw_free, free)
                tile = bass.ds(at, 1)
                sp.dma_start(WR[s][:], d["wall"][tile].rearrange("o p n -> p (o n)")).then_inc(raw_loaded[s], 16)

            for s in range(2):
                load(s, s, s, 0)
            with sp.Fori(0, NB) as tb:
                tok = sp.snap(tb * TB, min_val=0, max_val=SEQ - TB)
                for n in range(2):
                    for a, name in ((AH, "y_hi"), (AL, "y_lo")):
                        src = d[name][:, :, bass.ds(sp.snap(tok + n * (TB // 2), min_val=0, max_val=SEQ - TB // 2), TB // 2)]
                        sp.dma_start(a[:, :, n * (TB // 2):(n + 1) * (TB // 2)].bitcast(F32),
                                     src.rearrange("k p n -> p k n")).then_inc(ld_y[n], 16)
                sp.dma_start(X[:], d["x_feat"][:, :, bass.ds(tok, TB)].rearrange("k p n -> p k n")).then_inc(ld_x, 16)
                with sp.Fori(1, TILE_PLE // 2 + 1) as i:
                    for s in range(2):
                        load(tb * N_TILE + 2 * i + s, 2 * i + s, s, 1)
                sp.wait_ge(al_done, 24 * tb + 16)
                sp.dma_start(Tt[:, 0:2], d["p_feat"][:, :, bass.ds(tok, TB)].rearrange("k p n -> p k n")).then_inc(ld_p, 16)
                with sp.Fori(TILE_PLE // 2 + 1, N_TILE // 2) as i:
                    for s in range(2):
                        load(tb * N_TILE + 2 * i + s, 2 * i + s, s, 1)
                for s in range(2):
                    load(tb * N_TILE + N_TILE + s, s, s, 0)
                sp.wait_ge(st_x, 16 * tb + 16)
                sp.sem_inc(x_stored, 1)
                sp.wait_ge(st_c, 16 * tb + 16)
                sp.sem_inc(x_stored, 1)
                sp.wait_ge(cu_free, tb + 1)
                sp.sem_inc(x_stored, 1)
                sp.wait_ge(t_done, 24 * tb + 24)
                sp.sem_inc(x_stored, 1)
                sp.wait_ge(job_done, N_JOB * tb + N_JOB)
                sp.sem_inc(x_stored, 1)

        @block.scalar
        def _(act):
            act.sem_inc(sg_done, 2)
            act.sem_inc(gated, 1)
            for s in range(2):
                act.sem_inc(st_out[s], 16)

            def hi(w2, s, dst):
                act.wait_ge(raw_loaded[s], 16 * w2 + 16)
                act.copy(dst, WR[s][:]).then_inc(hi_done, 1)

            def whi(w2, s):
                hi(w2, s, WH[s][:])

            act.wait_ge(ld_g, 32)
            act.copy(gwh[:], gwr[:]).then_inc(gh_done, 1)
            for s in range(2):
                whi(0, s)
            with act.Fori(0, NB) as tb:
                job0, w0 = tb * N_JOB, tb * (N_TILE // 2)

                def gates(job, tile2, count, b):
                    for j in range(4):
                        act.wait_ge(job_done, job0 + (job + 1 + j) + 4 * b)
                        if j % 2 == 0:
                            act.wait_ge(mix_done, 16 * tb + 2 * b + (j // 2 + 1 + (0 if job == 0 else KD)))
                            act.activation(SG[j // 2][:], ps4[(job + j) % 4][:], ACT.Sigmoid).then_inc(sg_done, 1)
                        whi(w0 + 2 * b + (tile2 + j // 2 + 1), j % 2)

                def norm(i, job, xs):
                    act.preload_act_table_set("natural_log_exp_and_others")
                    for k in range(KD):
                        xs(k)
                        if k >= 2:
                            act.wait_ge(acc_done, 32 * tb + (8 * i + k - 1))
                        act.activation(V[k % 2][:], halves(X[:, k]), ACT.Square).then_inc(sq_done, 1)
                    act.wait_ge(job_done, job0 + (job + 1))
                    act.activation(SG[0][:], ps4[job % 4][:], ACT.Ln, bias=eps[:]).then_inc(ln_done, 1)
                    act.wait_ge(ln_done, 4 * tb + (i + 1))
                    act.activation(SG[1][:], SG[0][:], ACT.Exp, scale=-0.5).then_inc(r_done, 1)

                def split(i):
                    for k in range(KD):
                        act.wait_ge(t_done, 24 * tb + (8 * i + k + 1))
                        act.copy(AH[:, k], Tt[:, k]).then_inc(ah_done, 1)

                with act.Fori(0, N_GLU // 4) as b:
                    gates(0, 0, N_GLU, b)
                norm(0, JOB_STAT1, lambda k: act.wait_ge(xadd, N_XADD * tb + (2 + KD)))
                split(0)
                with act.Fori(0, F_GROUPS) as fg:
                    w1 = w0 + fg * F_TILES + TILE_MLP // 2
                    for f in range(F_TILES):
                        n = 32 * tb + 4 * fg + f
                        act.wait_ge(job_done, job0 + fg * (F_TILES + KD) + (JOB_MLP + f + 1))
                        act.wait_ge(v_done, n + 1)
                        act.activation(SG[f % 2][:], ps4[(JOB_MLP + f) % 4][:], ACT.Relu).then_inc(relu_done, 1)
                        whi(w1 + (f // 2 + 1), f % 2)
                        act.wait_ge(v_done, n + 3)
                        act.copy(halves(FH[:, f]), V[f % 2][:]).then_inc(fh_done, 1)
                    for m2 in range(F_TILES):
                        act.wait_ge(job_done, job0 + fg * (F_TILES + KD) + (JOB_MLP + F_TILES + 2 * m2 + 2))
                        whi(w1 + (F_TILES + m2) // 2 + 1, m2 % 2)
                norm(1, JOB_STAT2, lambda k: act.wait_ge(xadd, N_XADD * tb + (2 + KD * F_GROUPS + k + 1)))
                split(1)
                act.wait_ge(ld_p, 16 * tb + 16)
                for k in range(2):
                    act.copy(FH[:, k], Tt[:, k]).then_inc(ph_done, 1)
                with act.Fori(0, N_PLE // 4) as b:
                    gates(JOB_PLE, TILE_PLE // 2, N_PLE, b)
                norm(2, JOB_STAT3, lambda k: act.wait_ge(xadd, N_XADD * tb + (2 + N_XADD)))
                norm(3, JOB_STAT3 + 1, lambda k: act.wait_ge(xfin, 8 * tb + (k + 1)))
                split(2)
                act.dma_start(d["x2"][:, :, bass.ds(tb * TB, TB)].rearrange("k p n -> p k n"), X[:]).then_inc(st_x, 16)

                tok = bass.ds(tb * TB, TB)
                flat = lambda v: v.rearrange("p a b -> p (a b)")

                def ghi(i):
                    g = 0 if i < 2 else (i + 2) // 4
                    c = (i if i < 2 else (i - 2) % 4) * P
                    hi(w0 + (TILE_TM + i) // 2, i % 2, GH[g % 2][:, :, c:c + P])

                def take(j):
                    src, fn = ps4[(JOB_FM + j) % 4][:], ACT.Sigmoid if KINDS[j] in ("c_b", "tm_sigmoid") else ACT.Silu
                    if BY_ACT[j]:
                        act.wait_ge(job_done, job0 + (JOB_FM + j + 1))
                        if KINDS[j] == "c_b":
                            act.wait_ge(t_done, 24 * tb + 24)
                            act.activation(SG[j][:], src, fn).then_inc(gated, 1)
                        else:
                            act.wait_ge(st_out[j % 2], 16 * N_STORE * tb + 16 * ((j - FIRST_V) // 2 + 1))
                            act.activation(V[j % 2][:], src, fn).then_inc(gated, 1)

                def store(j):
                    v = V[j % 2]
                    if BY_ACT[j]:
                        act.wait_ge(gated, N_BY_ACT * tb + (before(j, True) + 2))
                    elif KINDS[j] == "conv":
                        i = j - M_QK.start
                        act.wait_ge(conv_out, 8 * tb + (i + 2))
                        act.activation(v[:], v[:], ACT.Silu).then_inc(silu_out, 1)
                        act.wait_ge(silu_out, 8 * tb + (i + 1))
                    else:
                        act.wait_ge(copied, N_BY_DVE * tb + (before(j, False) + 1 + 4))
                    if j < N_FM:
                        dst, src = d["fm"][j, :, tok], flat(v[:])
                    elif KINDS[j] == "gi":
                        n = j - GI_AT
                        dst, src = d["gi"][:, bass.ds(tb * TB + n * (TB // 2), TB // 2)], v[0:8, 0]
                    else:
                        g = [i for i in range(4) if TM_AT + sum(TM_JOBS[:i]) <= j][-1]
                        n = j - TM_AT - sum(TM_JOBS[:g])
                        per = TB // TM_JOBS[g]
                        dst = d["tm"][bass.ds(tb * TB + n * per, per), sum(TM_COLS[:g]):sum(TM_COLS[:g + 1])]
                        dst = dst.rearrange("(t p) n -> p t n", p=P)
                        src = flat(v[:]).rearrange("p (t n) -> p t n", n=TM_COLS[g])
                    act.dma_start(dst, src).then_inc(st_out[j % 2], 16)

                for j in range(N_COPY):
                    if j < N_FM:
                        act.wait_ge(job_done, job0 + (JOB_FM + j + 1))
                        if j < N_FM - 2:
                            whi(w0 + (TILE_FM + j + 2) // 2, j % 2)
                        else:
                            ghi(j - (N_FM - 2))
                    for g in range(3):
                        if j == TM_AT + sum(TM_JOBS[:g]):
                            act.wait_ge(job_done, job0 + (JOB_FM + j))
                            for i in range(2 + 4 * g, 6 + 4 * g):
                                ghi(i)
                    take(j)
                    if j > FIRST_V:
                        store(j - 1)
                store(N_COPY - 1)
                act.wait_ge(tap, N_TAP * tb + N_TAP)
                act.dma_start(d["cva"][:, :, tok].rearrange("k p n -> p k n"), CV[:]).then_inc(st_c, 16)
                for s in range(2):
                    whi(w0 + N_TILE // 2, s)
            act.wait_ge(st_x, 16 * NB)
            act.wait_ge(st_c, 16 * NB)
            for s in range(2):
                act.wait_ge(st_out[s], 16 * NB * N_STORE + 16)

        @block.gpsimd
        def _(pool):
            pool.memset(ones[:], 1.0 / D).then_inc(ones_set, 1)
            pool.sem_inc(raw_free, 2)
            pool.sem_inc(fl_done, 2)
            pool.wait_ge(gh_done, 1)
            pool.tensor_tensor(gwl[:], gwr[:], gwh[:].bitcast(F32), ALU.subtract).then_inc(gl_done, 1)

            def lo(w, s, dst, src, raw):
                pool.wait_ge(hi_done, w + 1)
                pool.tensor_tensor(dst, raw, src.bitcast(F32), ALU.subtract).then_inc(raw_free, 1)

            def wlo(w, s):
                lo(w, s, WL[s][:], WH[s][:], WR[s][:])

            for s in range(2):
                wlo(s, s)
            with pool.Fori(0, NB) as tb:
                w0 = tb * N_TILE

                def split(i):
                    for k in range(KD):
                        pool.wait_ge(ah_done, 24 * tb + (8 * i + k + 1))
                        pool.tensor_tensor(AL[:, k], Tt[:, k], AH[:, k].bitcast(F32), ALU.subtract).then_inc(al_done, 1)

                with pool.Fori(0, N_GLU // 2) as b:
                    for s in range(2):
                        wlo(w0 + 2 * b + (s + 2), s)
                split(0)
                with pool.Fori(0, F_GROUPS) as fg:
                    w1 = w0 + fg * (2 * F_TILES) + TILE_MLP
                    for f in range(F_TILES):
                        wlo(w1 + (f + 2), f % 2)
                        pool.wait_ge(fh_done, 32 * tb + 4 * fg + (f + 1))
                        pool.tensor_tensor(halves(FL[:, f]), V[f % 2][:], halves(FH[:, f]).bitcast(F32), ALU.subtract).then_inc(fl_done, 1)
                    for m2 in range(F_TILES):
                        wlo(w1 + (F_TILES + m2 + 2), m2 % 2)
                split(1)
                for k in range(2):
                    pool.wait_ge(ph_done, 2 * tb + k + 1)
                    pool.tensor_tensor(FL[:, k], Tt[:, k], FH[:, k].bitcast(F32), ALU.subtract).then_inc(pl_done, 1)
                with pool.Fori(0, N_PLE // 2) as b:
                    for s in range(2):
                        wlo(w0 + 2 * b + (TILE_PLE + s + 2), s)
                split(2)
                with pool.Fori(0, N_FM // 2 - 1) as b:
                    for s in range(2):
                        wlo(w0 + 2 * b + (TILE_FM + s + 2), s)
                for i in range(N_TM):
                    g = 0 if i < 2 else (i + 2) // 4
                    c = (i if i < 2 else (i - 2) % 4) * P
                    lo(w0 + (TILE_TM + i), i % 2, GL[g % 2][:, :, c:c + P], GH[g % 2][:, :, c:c + P],
                       WR[i % 2][:].rearrange("p (k n) -> p k n", k=KD))
                for s in range(2):
                    wlo(w0 + (N_TILE + s), s)

        @block.vector
        def _(dve):
            dve.memset(V[0][:, 0, 0:1], 0.0).then_inc(mix_done, 2)
            dve.memset(V[0][:, 0, 1:2], 0.0).then_inc(xadd, 2)
            dve.memset(V[0][:, 0, 2:3], 0.0).then_inc(v_done, 2)
            dve.memset(V[0][:, 0, 3:4], 0.0).then_inc(copied, 4)
            dve.wait_ge(copied, 4)
            dve.memset(cu_tail[:], 0.0).then_inc(tails_set, 1)
            dve.memset(mx_tail[:], 0.0).then_inc(mc, 1)
            dve.sem_inc(conv_out, 1)
            dve.wait_ge(tails_set, 1)
            dve.wait_ge(ld_c, 64)
            dve.wait_ge(ld_g, 32)
            with dve.Fori(0, NB) as tb:
                job0 = tb * N_JOB

                def mix(job, base, b):
                    for jj in range(2):
                        m = 2 * b + jj
                        dve.wait_ge(sg_done, 16 * tb + (base % 16) + m + 3)
                        dve.wait_ge(job_done, job0 + 4 * b + (job + 2 * jj + 2))
                        dve.wait_ge(xadd, N_XADD * tb + m + (1 + (KD * F_GROUPS + KD if base else 0)))
                        if base == 0:
                            dve.wait_ge(st_out[jj], 16 * N_STORE * tb + 16)
                        dve.tensor_tensor(V[jj][:], ps4[(job + 2 * jj + 1) % 4][:], SG[jj][:], ALU.mult).then_inc(mix_done, 1)
                        dve.wait_ge(mix_done, 16 * tb + (base % 16) + m + 3)
                        xm = X[:, bass.ds(m, 1), :].rearrange("p o (a n) -> p (o a) n", a=2)
                        dve.tensor_tensor(xm, xm, V[jj][:], ALU.add).then_inc(xadd, 1)

                def norm(i, out, done, count):
                    a0 = 32 * tb + 8 * i
                    for k in range(KD):
                        dve.wait_ge(sq_done, a0 + (k + 1))
                        if k:
                            dve.wait_ge(acc_done, a0 + k)
                            dve.tensor_tensor(halves(RB[:]), halves(RB[:]), V[k % 2][:], ALU.add).then_inc(acc_done, 1)
                        else:
                            dve.tensor_copy(halves(RB[:]), V[0][:]).then_inc(acc_done, 1)
                    dve.wait_ge(r_done, 4 * tb + (i + 1))
                    for k in range(KD):
                        dve.scalar_tensor_tensor(halves(out[:, k]), halves(X[:, k]), gains[:, i, k:k + 1], SG[1][:],
                                                 ALU.mult, ALU.mult).then_inc(done, 1)

                with dve.Fori(0, N_GLU // 4) as b:
                    dve.wait_ge(ld_x, 16 * tb + 16)
                    mix(0, 0, b)
                norm(0, Tt, t_done, 0)
                with dve.Fori(0, F_GROUPS) as fg:
                    for f in range(F_TILES):
                        n = 32 * tb + 4 * fg + f
                        dve.wait_ge(relu_done, n + 1)
                        dve.wait_ge(fl_done, n + 1)
                        dve.tensor_tensor(V[f % 2][:], SG[f % 2][:], SG[f % 2][:], ALU.mult).then_inc(v_done, 1)
                    for m in range(KD):
                        dve.wait_ge(job_done, job0 + fg * (F_TILES + KD) + (JOB_MLP + F_TILES + m + 1))
                        xm = halves(X[:, m])
                        dve.tensor_tensor(xm, xm, ps4[(JOB_MLP + F_TILES + m) % 4][:], ALU.add).then_inc(xadd, 1)
                norm(1, Tt, t_done, 0)
                with dve.Fori(0, N_PLE // 4) as b:
                    mix(JOB_PLE, KD, b)
                norm(2, X, xfin, 0)
                norm(3, Tt, t_done, 0)

                def slot_free(j):
                    dve.wait_ge(st_out[j % 2], 16 * N_STORE * tb + 16 * ((j - FIRST_V) // 2 + 1))

                def convolve(j, i):
                    x, out, m0 = MX[:, i % 2], V[j % 2], MC_INC * 8 * tb + MC_INC * i + 1
                    tail = slice(TB, TB + M_TAPS - 1)
                    dve.wait_ge(mc, m0)
                    dve.wait_ge(conv_out, 8 * tb + (i + 1))
                    dve.tensor_copy(halves(x[:, M_TAPS - 1:]), ps4[(JOB_FM + j) % 4][:]).then_inc(copied, 1)
                    dve.tensor_copy(x[:, 0:M_TAPS - 1], mx_tail[:, i]).then_inc(mc, 1)
                    dve.wait_ge(copied, N_BY_DVE * tb + (before(j, False) + 1 + 4))
                    slot_free(j)
                    for k in range(M_TAPS):
                        xk = halves(x[:, k:k + TB])
                        dve.wait_ge(mc, m0 + (k + 1))
                        if k == 0:
                            step = dve.tensor_scalar(out[:], xk, m_w[:, i, 0:1], m_b[:, i:i + 1], ALU.mult, ALU.add)
                        else:
                            step = dve.scalar_tensor_tensor(out[:], xk, m_w[:, i, k:k + 1], out[:], ALU.mult, ALU.add)
                        step.then_inc(conv_out if k == M_TAPS - 1 else mc, 1)
                    dve.tensor_copy(mx_tail[:, i], x[:, tail]).then_inc(mc, 1)

                def add_tap(n):
                    k, t = n // 2, n % 2
                    xk = CU[:, t, k:k + TB]
                    if k == 0:
                        dve.wait_ge(cu_done, 4 * tb + (3 + t))
                        step = dve.tensor_scalar(CV[:, t], xk, c_w[:, t, 0:1], c_b[:, t:t + 1], ALU.mult, ALU.add)
                    else:
                        dve.wait_ge(tap, N_TAP * tb + (n - 1))
                        step = dve.scalar_tensor_tensor(CV[:, t], xk, c_w[:, t, k:k + 1], CV[:, t], ALU.mult, ALU.add)
                    step.then_inc(tap, 1)

                taps = 0
                dve.wait_ge(st_x, 16 * tb + 16)
                dve.wait_ge(t_done, 24 * tb + 24)
                for t in range(2):
                    dve.tensor_copy(CU[:, t, 0:C_TAPS - 1], cu_tail[:, t]).then_inc(cu_done, 1)
                for j in range(N_COPY):
                    if not BY_ACT[j]:
                        dve.wait_ge(job_done, job0 + (JOB_FM + j + 1))
                    src = ps4[(JOB_FM + j) % 4]
                    if KINDS[j] == "c_a":
                        t = j - C_A.start
                        dve.wait_ge(gated, N_BY_ACT * tb + (t + 2))
                        dve.tensor_tensor(halves(CU[:, t, C_TAPS - 1:]), src[:], SG[t][:], ALU.mult).then_inc(copied, 1)
                        dve.wait_ge(copied, N_BY_DVE * tb + (before(j, False) + 1 + 4))
                        dve.sem_inc(cu_done, 1)
                    elif KINDS[j] == "conv":
                        convolve(j, j - M_QK.start)
                    elif KINDS[j] == "gi":
                        slot_free(j)
                        dve.tensor_copy(V[j % 2][0:8, 0], src[0:8, 0]).then_inc(copied, 1)
                    elif not BY_ACT[j]:
                        slot_free(j)
                        dve.tensor_copy(V[j % 2][:], src[:]).then_inc(copied, 1)
                    for n in range(taps, min(taps + TAPS_AT.get(j, 0), N_TAP)):
                        add_tap(n)
                        taps += 1
                dve.wait_ge(tap, N_TAP * tb + N_TAP)
                dve.tensor_copy(cu_tail[:], CU[:, :, TB:]).then_inc(cu_free, 1)

        @block.tensor
        def _(pe):
            def product(out, k_tiles, passes, wait=None):
                for k in range(k_tiles):
                    if wait:
                        wait(k)
                    for i, (l, r) in enumerate(passes(k)):
                        last = pe.matmul(out, l, r, start=(k == 0 and i == 0), stop=(k == k_tiles - 1 and i == 2))
                return last

            def job(slot, k_tiles, wh, wl, ah, al, wait=None, wait_half=None):
                for n in range(2):
                    if wait_half:
                        wait_half(n)
                    t = slice(n * (TB // 2), (n + 1) * (TB // 2))
                    last = product(ps4[slot][:, n], k_tiles,
                                   lambda k: ((wh(k), ah[:, k, t]), (wh(k), al[:, k, t]), (wl(k), ah[:, k, t])),
                                   wait if n == 0 else None)
                last.then_inc(job_done, 1)

            def tile(s, at=0):
                return (lambda k: WH[s][:, (at + k) * P:(at + k + 1) * P]), (lambda k: WL[s][:, (at + k) * P:(at + k + 1) * P])

            def stat(slot, count):
                pe.wait_ge(acc_done, count)
                for n in range(2):
                    last = pe.matmul(ps4[slot][:, n], ones[:], halves(RB[:])[:, n], start=True, stop=True)
                last.then_inc(job_done, 1)

            pe.wait_ge(ones_set, 1)
            with pe.Fori(0, NB) as tb:
                w0 = tb * N_TILE
                with pe.Fori(0, N_GLU // 4) as b:
                    pe.wait_ge(copied, N_BY_DVE * tb + 4)
                    pe.wait_ge(gated, N_BY_ACT * tb + 1)
                    for j in range(4):
                        pe.wait_ge(raw_free, w0 + 4 * b + (j + 3))
                        pe.wait_ge(mix_done if j % 2 else sg_done, 16 * tb + 2 * b + (j // 2 + 1))
                        job(j, KD, *tile(j % 2), AH, AL,
                            wait_half=(lambda n: pe.wait_ge(ld_y[n], 32 * tb + 32)) if j == 0 else None)
                stat(JOB_STAT1 % 4, 32 * tb + 8)
                with pe.Fori(0, F_GROUPS) as fg:
                    w1 = w0 + fg * (2 * F_TILES) + TILE_MLP
                    x1 = N_XADD * tb + KD * fg
                    for f in range(F_TILES):
                        pe.wait_ge(raw_free, w1 + (f + 3))
                        pe.wait_ge(xadd, x1 + (f + 5 + 2))
                        job((JOB_MLP + f) % 4, KD, *tile(f % 2), AH, AL,
                            (lambda k: pe.wait_ge(al_done, 24 * tb + (k + 1))) if f == 0 else None)
                    for m in range(KD):
                        if m % 2 == 0:
                            pe.wait_ge(raw_free, w1 + (F_TILES + m // 2 + 3))
                        if m < 4:
                            pe.wait_ge(relu_done, 32 * tb + 4 * fg + (m + 1))
                        else:
                            pe.wait_ge(xadd, x1 + (KD + m - 3 + 2))
                        job((JOB_MLP + F_TILES + m) % 4, F_TILES, *tile(m // 2 % 2, m % 2 * F_TILES), FH, FL,
                            (lambda k: pe.wait_ge(fl_done, 32 * tb + 4 * fg + (k + 1 + 2))) if m == 0 else None)
                stat(JOB_STAT2 % 4, 32 * tb + 16)
                with pe.Fori(0, N_PLE // 4) as b:
                    for j in range(4):
                        pe.wait_ge(raw_free, w0 + 4 * b + (TILE_PLE + j + 3))
                        pe.wait_ge(mix_done if j % 2 else sg_done, 16 * tb + 2 * b + (KD + j // 2 + 1))
                        if j % 2:
                            pe.wait_ge(pl_done, 2 * tb + 2)
                            job((JOB_PLE + j) % 4, 2, *tile(j % 2), FH, FL)
                        else:
                            job((JOB_PLE + j) % 4, KD, *tile(j % 2), AH, AL,
                                (lambda k: pe.wait_ge(al_done, 24 * tb + (8 + k + 1))) if j == 0 else None)
                stat(JOB_STAT3 % 4, 32 * tb + 24)
                stat((JOB_STAT3 + 1) % 4, 32 * tb + 32)

                def slot_read(j):
                    if j >= 4:
                        by_act = BY_ACT[j - 4]
                        done = before(j - 4, by_act) + 1
                        if by_act:
                            pe.wait_ge(gated, N_BY_ACT * tb + (done + 1))
                        else:
                            pe.wait_ge(copied, N_BY_DVE * tb + (done + 4))

                for j in range(N_FM):
                    pe.wait_ge(raw_free, w0 + (TILE_FM + j + 3))
                    slot_read(j)
                    job((JOB_FM + j) % 4, KD, *tile(j % 2), AH, AL,
                        (lambda k: pe.wait_ge(al_done, 24 * tb + (16 + k + 1))) if j == 0 else None)
                pe.wait_ge(gl_done, 1)
                for n in range(2):
                    t = slice(n * (TB // 2), (n + 1) * (TB // 2))
                    slot_read(GI_AT + n)
                    product(ps4[(JOB_GI + n) % 4][0:8, 0], KD,
                            lambda k: ((gwh[:, k], AH[:, k, t]), (gwh[:, k], AL[:, k, t]), (gwl[:, k], AH[:, k, t]))
                            ).then_inc(job_done, 1)
                c, tiles = TM_AT, 0
                for g in range(4):
                    n = TM_COLS[g]
                    tiles += n // P
                    pe.wait_ge(raw_free, w0 + (TILE_TM + tiles + 2))
                    per = TB // P // TM_JOBS[g]
                    for j in range(TM_JOBS[g]):
                        slot_read(c)
                        out = ps4[(JOB_FM + c) % 4][:].rearrange("p a b -> p (a b)")
                        for i in range(per):
                            t = slice((j * per + i) * P, (j * per + i + 1) * P)
                            last = product(out[:, i * n:(i + 1) * n], KD,
                                           lambda k: ((AH[:, k, t], GH[g % 2][:, k, 0:n]), (AL[:, k, t], GH[g % 2][:, k, 0:n]),
                                                      (AH[:, k, t], GL[g % 2][:, k, 0:n])))
                        last.then_inc(job_done, 1)
                        c += 1


A_HEADS, A_DIM = 4, 64
A_TILES = A_HEADS * A_DIM // P
QB = 128
N_QB = SEQ // QB
WIN = 512 + QB
KT = WIN // QB
NEG = -1e30
NQ4 = 4
QC = SEQ // NQ4


def attention(nc, env, d, ctx):
    sb, ps, sem = tools(nc, ctx)
    ident, eps = env["ident"], env["eps"]
    qk = sb("at_qk", [P, 2 * A_TILES, SEQ])
    z = sb("at_z", [P, A_TILES, SEQ])
    v = sb("at_v", [P, N_QB, A_HEADS * A_DIM])
    bias = sb("at_bias", [P, A_HEADS, WIN])
    gain = sb("at_gain", [P, 2])
    blk = sb("at_blk", [P, P])
    half = sb("at_half", [P, 2])
    sq = sb("at_sq", [P, 2, QC])
    lnv, rr = sb("at_ln", [P, 2, QC]), sb("at_r", [P, 2, QC])
    qs = sb("at_qs", [P, 2, 2, A_TILES, QB])
    sbv = sb("at_sb", [P, 2, WIN])
    e = sb("at_e", [P, 2, WIN])
    pT = sb("at_pT", [P, 2, KT, QB])
    mx, ng, sm, rc = (sb(f"at_{n}", [P, 2]) for n in ("mx", "ng", "sm", "rc"))
    o = sb("at_o", [P, 2, A_HEADS * A_DIM])
    om = sb("at_om", [P, 2, A_TILES, QB])
    s_ps = [ps(f"at_s_ps{i}", [P, 2, 512]) for i in range(2)]
    t_ps = ps("at_t_ps", [P, 2 * 512])
    o_ps = [ps(f"at_o_ps{i}", [P, 512]) for i in range(2)]
    x_ps = o_ps[1][:, 256:512].rearrange("p (t n) -> p t n", n=QB)
    ld_qk, ld_z, ld_v, ld_b, ld_g = (sem(f"at_ld_{n}") for n in ("qk", "z", "v", "b", "g"))
    blk_set, bias_set, g_done = sem("at_blk_set"), sem("at_bias_set"), sem("at_g_done")
    sq_done, ms_done, ln_done, r_done, qk_done = (sem(f"at_{n}_done") for n in ("sq", "ms", "ln", "r", "qk"))
    qs_done, s_done, b_done, n_done, e_done, t_done, p_done, pv_done, rc_done, o_done, x_done, m_done = (
        sem(f"at_{n}_done") for n in ("qs", "s", "b", "neg", "e", "t", "p", "pv", "rc", "o", "x", "m"))
    may_add = sem("at_may_add")
    st = [sem("at_st0"), sem("at_st1")]
    N_NORM = 2 * A_TILES * NQ4

    def schedule(engine, stages):
        def step(b, par, h, inside):
            for off, stage in stages:
                db, hh = (h + off) // A_HEADS, (h + off) % A_HEADS
                if inside:
                    stage(b + db, (par + db) % 2, hh, KT)
                elif 0 <= b + db < N_QB:
                    stage(b + db, (par + db) % 2, hh, min(b + db + 1, KT))

        for u in range(-2, 6 * A_HEADS):
            step(u // A_HEADS, u // A_HEADS % 2, u % A_HEADS, False)
        with engine.Fori(3, N_QB // 2 - 1) as b2:
            for par in range(2):
                for h in range(A_HEADS):
                    step(2 * b2 + par, par, h, True)
        for u in range((N_QB - 2) * A_HEADS, N_QB * A_HEADS + 2):
            step(u // A_HEADS, u // A_HEADS % 2, u % A_HEADS, False)

    def need(engine, semaphore, value):
        if not isinstance(value, int) or value > 0:
            engine.wait_ge(semaphore, value)

    with nc.Block() as block:
        @block.sync
        def _(sp):
            sp.dma_start(qk[:], d["fm"][A_QK].rearrange("k p n -> p k n")).then_inc(ld_qk, 16)
            sp.dma_start(gain[:], d["att_gain"]).then_inc(ld_g, 16)
            sp.dma_start(z[:], d["fm"][A_Z].rearrange("k p n -> p k n")).then_inc(ld_z, 16)
            sp.dma_start(v[:], d["tm"][:, 0:A_HEADS * A_DIM].rearrange("(t p) n -> p t n", p=P)).then_inc(ld_v, 16)
            sp.dma_start(bias[:], d["att_bias"]).then_inc(ld_b, 16)

            def store(b, s):
                dst = d["mixed"][0:A_TILES, :, bass.ds(sp.snap(b * QB, min_val=0, max_val=SEQ - QB), QB)]
                sp.wait_ge(m_done, b + 1 + 2)
                sp.dma_start(dst.rearrange("k p n -> p k n"), om[:, s]).then_inc(st[s], 16)

            with sp.Fori(0, N_QB // 2) as b2:
                for s in range(2):
                    store(2 * b2 + s, s)
            for s in range(2):
                sp.wait_ge(st[s], 16 * (N_QB // 2))

        @block.gpsimd
        def _(pool):
            pool.wait_ge(ld_g, 16)
            pool.tensor_scalar(gain[:, 0:1], gain[:, 0:1], A_DIM ** -0.5, None, ALU.mult).then_inc(g_done, 1)
            pool.sem_inc(qs_done, 2)
            pool.wait_ge(blk_set, 8)

            def queries(b, s, wait):
                if wait:
                    pool.wait_ge(s_done, A_HEADS * b - A_HEADS)
                for hh in range(2):
                    pool.tensor_tensor(qs[:, s, hh], qk[:, 0:A_TILES, bass.ds(b * QB, QB)],
                                       half[:, hh:hh + 1, None].to_broadcast([P, A_TILES, QB]), ALU.mult).then_inc(qs_done, 1)

            pool.wait_ge(qk_done, A_TILES * NQ4)
            for s in range(2):
                queries(s, s, False)
            with pool.Fori(1, N_QB // 2) as b2:
                for s in range(2):
                    queries(2 * b2 + s, s, True)

        @block.scalar
        def _(act):
            act.preload_act_table_set("natural_log_exp_and_others")
            act.wait_ge(ld_qk, 16)
            for i in range(N_NORM):
                t, c = i // NQ4, slice(i % NQ4 * QC, (i % NQ4 + 1) * QC)
                if i >= 2:
                    act.wait_ge(ms_done, i - 1)
                act.activation(sq[:, i % 2], qk[:, t, c], ACT.Square).then_inc(sq_done, 1)
                act.wait_ge(ms_done, i + 1)
                act.activation(lnv[:, i % 2], s_ps[i % 2][:, 0], ACT.Ln, bias=eps[:]).then_inc(ln_done, 1)
                act.wait_ge(ln_done, i + 1)
                if i >= 2:
                    act.wait_ge(qk_done, i - 1)
                act.activation(rr[:, i % 2], lnv[:, i % 2], ACT.Exp, scale=-0.5).then_inc(r_done, 1)


            def weigh(b, s, h, nb):
                u, i = A_HEADS * b + h, h % 2
                w = slice(WIN - nb * QB, WIN)
                act.wait_ge(n_done, u + 1)
                need(act, t_done, u - 1)
                need(act, rc_done, u - 1)
                act.activation(e[:, i, w], sbv[:, i, w], ACT.Exp, bias=ng[:, i:i + 1], accum_out=sm[:, i:i + 1]).then_inc(e_done, 1)

            def copy(b, s, h, nb):
                u = A_HEADS * b + h
                act.wait_ge(t_done, u + 1)
                need(act, pv_done, u - 1)
                act.copy(pT[:, h % 2, 0:nb], t_ps[:, 0:nb * QB].rearrange("p (t n) -> p t n", n=QB)).then_inc(p_done, 1)

            schedule(act, [(1, weigh), (0, copy)])

        @block.vector
        def _(dve):
            dve.memset(om[:, 0, 0, 0:1], 0.0).then_inc(m_done, 2)
            for hh in range(2):
                rows = slice(hh * A_DIM, (hh + 1) * A_DIM)
                dve.memset(blk[rows, rows], 1.0 / A_DIM).then_inc(blk_set, 1)
                dve.memset(blk[rows, (1 - hh) * A_DIM:(2 - hh) * A_DIM], 0.0).then_inc(blk_set, 1)
                dve.memset(half[rows, hh:hh + 1], 1.0).then_inc(blk_set, 1)
                dve.memset(half[rows, 1 - hh:2 - hh], 0.0).then_inc(blk_set, 1)
            dve.wait_ge(ld_b, 16)
            dve.memset(bias[0:64, :, WIN - 64:WIN], NEG).then_inc(bias_set, 1)
            dve.memset(bias[64:P, :, 0:64], NEG).then_inc(bias_set, 1)
            dve.wait_ge(m_done, 2)
            dve.wait_ge(g_done, 1)
            for i in range(N_NORM):
                t, c = i // NQ4, slice(i % NQ4 * QC, (i % NQ4 + 1) * QC)
                dve.wait_ge(r_done, i + 1)
                dve.scalar_tensor_tensor(qk[:, t, c], qk[:, t, c], gain[:, t // A_TILES:t // A_TILES + 1], rr[:, i % 2],
                                         ALU.mult, ALU.mult).then_inc(qk_done, 1)
            dve.wait_ge(bias_set, 2)
            dve.wait_ge(ld_z, 16)

            def scores(b, s, h, nb):
                u, i = A_HEADS * b + h, h % 2
                w, hw = slice(WIN - nb * QB, WIN), nb * QB // 2
                two = lambda a: a.rearrange("p (a n) -> p a n", a=2)
                dve.wait_ge(s_done, u + 1)
                need(dve, e_done, u - 1)
                need(dve, n_done, u - 1)
                dve.sem_inc(may_add, 1)
                dve.tensor_tensor_reduce(two(sbv[:, i, w]), s_ps[i][:, :, 0:hw], two(bias[:, h, w]), 1.0, -3e38,
                                         ALU.add, ALU.max, accum_out=mx[:, i:i + 1]).then_inc(b_done, 1)
                dve.wait_ge(b_done, u + 1)
                dve.tensor_scalar(ng[:, i:i + 1], mx[:, i:i + 1], -1.0, None, ALU.mult).then_inc(n_done, 1)

            def invert(b, s, h, nb):
                u, i = A_HEADS * b + h, h % 2
                dve.wait_ge(e_done, u + 1)
                need(dve, o_done, u - 1)
                dve.reciprocal(rc[:, i:i + 1], sm[:, i:i + 1]).then_inc(rc_done, 1)

            def output(b, s, h, nb):
                u, i = A_HEADS * b + h, h % 2
                dve.wait_ge(rc_done, u + 1)
                dve.wait_ge(pv_done, u + 1)
                need(dve, x_done, b - 1)
                dve.tensor_scalar(o[:, s, h * A_DIM:(h + 1) * A_DIM], o_ps[i][:, h // 2 * A_DIM:(h // 2 + 1) * A_DIM],
                                  rc[:, i:i + 1], None, ALU.mult).then_inc(o_done, 1)

            def gate(b, s, h, nb):
                if h == A_HEADS - 1:
                    dve.wait_ge(x_done, b + 1)
                    need(dve, st[s], 8 * b - 8 * s)
                    dve.tensor_tensor(om[:, s], x_ps, z[:, :, bass.ds(b * QB, QB)], ALU.mult).then_inc(m_done, 1)

            schedule(dve, [(2, scores), (0, invert), (-1, output), (-2, gate)])

        @block.tensor
        def _(pe):
            pe.wait_ge(blk_set, 8)
            for i in range(N_NORM):
                pe.wait_ge(sq_done, i + 1)
                if i >= 2:
                    pe.wait_ge(ln_done, i - 1)
                pe.matmul(s_ps[i % 2][:, 0], blk[:], sq[:, i % 2], start=True, stop=True).then_inc(ms_done, 1)
            pe.wait_ge(qk_done, N_NORM)
            pe.wait_ge(ld_v, 16)

            def scores(b, s, h, nb):
                u, hw = A_HEADS * b + h, nb * QB // 2
                pe.wait_ge(qs_done, 2 * b + 4)
                need(pe, b_done, u - 1)
                for n in range(2):
                    last = pe.matmul(s_ps[h % 2][:, n, 0:hw], qs[:, s, h % 2, h // 2],
                                     qk[:, A_TILES + h // 2, bass.ds((b + 1 - nb) * QB + n * hw, hw)], start=True, stop=True)
                last.then_inc(s_done, 1)

            def turn(b, s, h, nb):
                u = A_HEADS * b + h
                pe.wait_ge(e_done, u + 1)
                need(pe, p_done, u)
                for t in range(nb):
                    last = pe.transpose(t_ps[:, t * QB:(t + 1) * QB], e[:, h % 2, WIN - (nb - t) * QB:WIN - (nb - t - 1) * QB], ident[:])
                last.then_inc(t_done, 1)

            def values(b, s, h, nb):
                u = A_HEADS * b + h
                pe.wait_ge(p_done, u + 1)
                need(pe, o_done, u - 1)
                if h == 1:
                    pe.wait_ge(m_done, b + 2)
                for t in range(nb):
                    vt = v[:, bass.ds(b + 1 - nb + t, 1), h * A_DIM:(h + 1) * A_DIM].rearrange("p o n -> p (o n)")
                    last = pe.matmul(o_ps[h % 2][:, h // 2 * A_DIM:(h // 2 + 1) * A_DIM], pT[:, h % 2, t], vt,
                                     start=(t == 0), stop=(t == nb - 1))
                last.then_inc(pv_done, 1)

            def turn_output(b, s, h, nb):
                if h == A_HEADS - 1:
                    pe.wait_ge(o_done, A_HEADS * b + A_HEADS)
                    for t in range(A_TILES):
                        last = pe.transpose(x_ps[:, t], o[:, s, t * P:(t + 1) * P], ident[:])
                    last.then_inc(x_done, 1)

            schedule(pe, [(2, scores), (0, turn), (-1, values), (-2, turn_output)])


M_HEADS = 4
MC = 128
N_MC = SEQ // MC
M_SCALE = float(P) ** -0.5
M_W = M_HEADS * P
CW = P + 1


def mlstm(nc, env, d, ctx):
    sb, ps, sem = tools(nc, ctx)
    env["m_qk"] = sb("m_qk", [P, 2 * M_HEADS, SEQ])
    env["m_oz"] = sb("m_oz", [P, N_MC, 2 * M_W])
    env["m_tok"] = sb("m_tok", [P, N_MC, 3 * M_HEADS])
    env["m_dec"] = sb("m_dec", [P, M_HEADS, N_MC])
    with ExitStack() as c:
        mlstm_prepare(nc, env, d, c)
    with ExitStack() as c:
        mlstm_chunks(nc, env, d, c)


def mlstm_prepare(nc, env, d, ctx):
    sb, ps, sem = tools(nc, ctx)
    ident, eps, qk, oz, tok, dec = (env[n] for n in ("ident", "eps", "m_qk", "m_oz", "m_tok", "m_dec"))
    H = M_HEADS
    rA, rB, rC, rE, rT, rst = (sb(f"m_row_{n}", [H, SEQ]) for n in "ABCETR")
    bif = sb("m_bif", [H, 2])
    mp, dt, dd = sb("m_mp", [H, N_MC]), sb("m_dt", [H, N_MC]), sb("m_dd", [H, H, N_MC])
    one = sb("m_one", [H, P])
    tok_ps = ps("m_tok_ps", [P, 512])
    dec_ps = ps("m_dec_ps", [P, 512])
    ld_g, ld_oz, ld_qk, a_done, v_done = sem("m_ld_g"), sem("m_ld_oz"), sem("m_ld_qk"), sem("m_a_done"), sem("m_v_done")
    turned, spread, st = sem("m_turned"), sem("m_spread"), sem("m_st")
    rst_set, g_made = sem("m_rst_set"), sem("m_g_made")
    by_chunk = lambda v: v.rearrange("p (c n) -> p c n", n=MC)
    last = lambda v: by_chunk(v)[:, :, MC - 1]

    with nc.Block() as block:
        @block.sync
        def _(sp):
            sp.dma_start(rA[:], d["gi"][0:H]).then_inc(ld_g, 16)
            sp.dma_start(rB[:], d["gi"][H:2 * H]).then_inc(ld_g, 16)
            sp.dma_start(bif[:], d["ml_bif"]).then_inc(ld_g, 16)
            sp.dma_start(qk[:], d["fm"][M_QK].rearrange("k p n -> p k n")).then_inc(ld_qk, 16)
            sp.wait_ge(v_done, 8)
            sp.dma_start(d["rows"][0], rT[:]).then_inc(st, 16)
            sp.wait_ge(a_done, 4)
            sp.dma_start(d["rows"][1], rB[:]).then_inc(st, 16)
            sp.wait_ge(st, 32)
            sp.wait_ge(ld_qk, 16)
            sp.wait_ge(ld_oz, 16)

        @block.scalar
        def _(act):
            act.dma_start(oz[:], d["tm"][:, 256 + M_W:256 + 3 * M_W].rearrange("(t p) n -> p t n", p=P)).then_inc(ld_oz, 16)
            act.preload_act_table_set("natural_log_exp_and_others")
            act.wait_ge(ld_g, 48)
            act.activation(rT[:], rB[:], ACT.Abs, bias=bif[:, 1:2]).then_inc(a_done, 1)
            act.wait_ge(a_done, 1)
            act.activation(rT[:], rT[:], ACT.Exp, scale=-1.0).then_inc(a_done, 1)
            act.wait_ge(a_done, 2)
            act.activation(rT[:], rT[:], ACT.Ln, bias=1.0).then_inc(a_done, 1)
            act.wait_ge(v_done, 8)
            act.activation(rB[:], rB[:], ACT.Exp).then_inc(a_done, 1)
            act.activation(rC[:], rC[:], ACT.Exp, scale=-1.0).then_inc(a_done, 1)
            act.wait_ge(v_done, 9)
            act.activation(mp[:], dt[:], ACT.Exp).then_inc(a_done, 1)
            act.wait_ge(v_done, 10)
            act.activation(rE[:], rE[:], ACT.Exp).then_inc(a_done, 1)

        @block.gpsimd
        def _(pool):
            pool.memset(rst[:], 1.0).then_inc(rst_set, 1)
            pool.wait_ge(rst_set, 1)
            pool.memset(by_chunk(rst[:])[:, :, 0:1], 0.0).then_inc(rst_set, 1)
            pool.memset(one[:], 1.0).then_inc(rst_set, 1)

        @block.vector
        def _(dve):
            dve.wait_ge(ld_g, 48)
            dve.tensor_scalar(rA[:], rA[:], bif[:, 0:1], None, ALU.add).then_inc(v_done, 1)
            dve.tensor_scalar(rE[:], rB[:], bif[:, 1:2], 0.0, ALU.add, ALU.min).then_inc(v_done, 1)
            dve.wait_ge(a_done, 3)
            dve.wait_ge(v_done, 2)
            dve.tensor_tensor(rB[:], rE[:], rT[:], ALU.subtract).then_inc(v_done, 1)
            dve.wait_ge(v_done, 3)
            dve.wait_ge(rst_set, 3)
            dve.tensor_tensor_scan(rC[:], rB[:], rA[:], 0.0, ALU.add, ALU.max).then_inc(v_done, 1)
            dve.tensor_tensor_scan(rE[:], rst[:], rB[:], 0.0, ALU.mult, ALU.add).then_inc(v_done, 1)
            dve.memset(mp[:, 0:1], 0.0)
            dve.wait_ge(v_done, 5)
            dve.tensor_copy(mp[:, 1:], by_chunk(rC[:])[:, 0:N_MC - 1, MC - 1]).then_inc(v_done, 1)
            dve.tensor_tensor(rT[:], rE[:], rC[:], ALU.subtract).then_inc(v_done, 1)
            dve.wait_ge(v_done, 7)
            dve.tensor_tensor(by_chunk(rB[:]), by_chunk(rT[:]), mp[:, :, None].to_broadcast([H, N_MC, MC]), ALU.add).then_inc(v_done, 1)
            dve.tensor_tensor(dt[:], last(rT[:]), mp[:], ALU.add).then_inc(v_done, 1)
            dve.tensor_tensor(rA[:], rA[:], rE[:], ALU.subtract).then_inc(g_made, 1)
            dve.wait_ge(g_made, 1)
            dve.tensor_tensor(by_chunk(rE[:]), by_chunk(rA[:]), by_chunk(rT[:])[:, :, MC - 1:MC].to_broadcast([H, N_MC, MC]),
                              ALU.add).then_inc(v_done, 1)
            dve.wait_ge(a_done, 6)
            dve.tensor_tensor(dd[:], mp[:, None, :].to_broadcast([H, H, N_MC]),
                              ident[0:H, 0:H, None].to_broadcast([H, H, N_MC]), ALU.mult).then_inc(spread, 1)
            dve.wait_ge(turned, 1)
            t = tok_ps[:, 0:3 * H * N_MC].rearrange("p (c n) -> p c n", n=3 * H)
            dve.tensor_copy(tok[:, :, 0:2 * H], t[:, :, 0:2 * H])
            dve.tensor_scalar(tok[:, :, 2 * H:], t[:, :, 2 * H:], M_SCALE, None, ALU.mult)
            dve.wait_ge(turned, 2)
            dve.tensor_copy(dec[:], dec_ps[:, 0:H * N_MC].rearrange("p (h c) -> p h c", h=H))

        @block.tensor
        def _(pe):
            pe.wait_ge(spread, 1)
            pe.wait_ge(a_done, 7)
            pe.wait_ge(rst_set, 3)
            for c in range(N_MC):
                for i, r in enumerate((rA, rC, rE)):
                    at = (3 * c + i) * H
                    last_ = pe.transpose(tok_ps[:, at:at + H], r[:, c * MC:(c + 1) * MC], ident[0:H, 0:H])
            last_.then_inc(turned, 1)
            pe.matmul(dec_ps[:, 0:H * N_MC], one[:], dd[:].rearrange("p h c -> p (h c)"), start=True, stop=True).then_inc(turned, 1)


def mlstm_chunks(nc, env, d, ctx):
    sb, ps, sem = tools(nc, ctx)
    ident, eps, qk, oz, tok, dec = (env[n] for n in ("ident", "eps", "m_qk", "m_oz", "m_tok", "m_dec"))
    H = M_HEADS
    va = sb("m_va", [P, 2, H, CW])
    bc = sb("m_bc", [P, 2, 2, H, MC])
    sc = sb("m_sc", [P, 2, 4 * H])
    ks = sb("m_ks", [P, 2, H, MC])
    qp = sb("m_qp", [P, 2, H, MC])
    am = sb("m_am", [P, 2, H, MC])
    dm = sb("m_dm", [P, 2, H, MC])
    sd = sb("m_sd", [P, 2, H, MC])
    kw = sb("m_kw", [P, 2, H, P])
    hb, hm = sb("m_hb", [P, 2, H, P]), sb("m_hm", [P, 2, H, P])
    om = sb("m_om", [P, 2, H, MC])
    junk = sb("m_junk", [P, H, P])
    state = sb("m_state", [P, H, CW])
    mask = sb("m_mask", [P, MC])
    ad, dn, rc = (sb(f"m_{n}", [P, 2, H]) for n in ("ad", "dn", "rc"))
    ssq, ln, rr = (sb(f"m_{n}", [P, 2, H]) for n in ("ssq", "ln", "rr"))
    gain = sb("m_gain", [P, H])
    s_ps = [ps(f"m_s_ps{i}", [P, H, MC]) for i in range(2)]
    kt_ps, x_ps = ps("m_kt_ps", [P, H, P]), ps("m_x_ps", [P, H, P])
    n_ps, u_ps = ps("m_n_ps", [P, 2, 512]), ps("m_u_ps", [P, 2, 512])
    head = lambda v, h: v[:, h // 2, h % 2 * CW:(h % 2 + 1) * CW]
    heads = lambda v: v[:, :, 0:2 * CW].rearrange("p a (b n) -> p a b n", n=CW)
    two = lambda v: v.rearrange("p (a b) n -> p a b n", a=2)
    ld_g, va_ld, bc_ld = sem("m_ld_gain"), [sem("m_va_ld0"), sem("m_va_ld1")], [sem("m_bc_ld0"), sem("m_bc_ld1")]
    st = [sem("m_st0"), sem("m_st1")]
    names = ("ks qp sc am dm s kt sd kw num upd c ad den rec h hm sq rn r h2 h3 x om").split()
    S = {n: sem(f"m_{n}_done") for n in names}
    (ks_done, qp_done, sc_done, am_done, dm_done, s_done, kt_done, sd_done, kw_done, num_done, upd_done, c_done,
     ad_done, den_done, rec_done, h_done, hm_done, sq_done, rn_done, r_done, h2_done, h3_done, x_done, om_done) = S.values()
    ready, va_set, mask_set = sem("m_ready"), sem("m_va_set"), sem("m_mask_set")

    def schedule(engine, s1, s2, s3, s4):
        def step(c, par, full=True):
            for off, stage in ((1, s1), (0, s2), (-1, s3), (-2, s4)):
                if stage and (full or 0 <= c + off < N_MC):
                    stage(c + off, (par + off) % 2)
        for c in range(-1, 2):
            step(c, c % 2, False)
        with engine.Fori(1, N_MC // 2 - 1) as i:
            for par in range(2):
                step(2 * i + par, par)
        for c in range(N_MC - 2, N_MC + 2):
            step(c, c % 2, False)

    with nc.Block() as block:
        @block.sync
        def _(sp):
            for s in range(2):
                sp.sem_inc(st[s], 16)
            sp.dma_start(gain[:], d["ml_gain"]).then_inc(ld_g, 16)

            def load(c, s):
                tok_at = bass.ds(c * MC, MC) if isinstance(c, int) else bass.ds(sp.snap(c * MC, min_val=0, max_val=SEQ - MC), MC)
                src = d["tm"][tok_at, 256:256 + M_W].rearrange("p (h n) -> p h n", h=H)
                rows = d["rows"][:, :, tok_at].partition_broadcast(P)
                sp.wait_ge(num_done, c + 1)
                sp.sem_inc(ready, 1)
                sp.wait_ge(upd_done, c + 1)
                sp.sem_inc(ready, 1)
                sp.dma_start(va[:, s, :, 0:P], src).then_inc(va_ld[s], 16)
                sp.wait_ge(am_done, c + 1)
                sp.sem_inc(ready, 1)
                sp.wait_ge(qp_done, c + 1)
                sp.sem_inc(ready, 1)
                sp.dma_start(bc[:, s], rows).then_inc(bc_ld[s], 16)

            def store(c, s):
                tok_at = bass.ds(c * MC, MC) if isinstance(c, int) else bass.ds(sp.snap(c * MC, min_val=0, max_val=SEQ - MC), MC)
                dst = d["mixed"][2:2 + H, :, tok_at].rearrange("k p n -> p k n")
                sp.wait_ge(om_done, c + 1)
                sp.dma_start(dst, om[:, s]).then_inc(st[s], 16)

            for c in range(2):
                load(c, c)
            load(2, 0)
            load(3, 1)
            with sp.Fori(0, N_MC // 2 - 2) as i:
                for s in range(2):
                    store(2 * i + s, s)
                    load(2 * i + (4 + s), s)
            for c in range(N_MC - 4, N_MC):
                store(c, c % 2)
            for s in range(2):
                sp.wait_ge(st[s], 16 + 16 * (N_MC // 2))

        @block.gpsimd
        def _(pool):
            pool.memset(mask[:], 0.0).then_inc(mask_set, 1)
            pool.wait_ge(mask_set, 1)
            pool.affine_select(out=mask[:], in_=mask[:], compare_op=ALU.is_ge, fill=NEG, base=0,
                               pattern=[[1, MC]], channel_multiplier=-1).then_inc(mask_set, 1)
            pool.sem_inc(qp_done, 2)
            pool.sem_inc(hm_done, 2)
            pool.sem_inc(h3_done, 2)

            def stage1(c, s):
                at = bass.ds(c * MC, MC)
                pool.wait_ge(kt_done, c + 1)
                pool.tensor_copy(ks[:, s], qk[:, H:, at]).then_inc(ks_done, 1)
                pool.wait_ge(kw_done, c + 1)
                pool.wait_ge(den_done, c + 1)
                pool.tensor_copy(sc[:, s, 0:3 * H], tok[:, bass.ds(c, 1)].rearrange("p o n -> p (o n)")).then_inc(sc_done, 1)
                pool.tensor_copy(sc[:, s, 3 * H:], dec[:, :, bass.ds(c, 1)].rearrange("p h o -> p (h o)")).then_inc(sc_done, 1)
                pool.wait_ge(bc_ld[s], 8 * c + (16 - 8 * s))
                pool.wait_ge(num_done, c + 1)
                pool.tensor_tensor(qp[:, s], qk[:, 0:H, at], bc[:, s, 1], ALU.mult).then_inc(qp_done, 1)

            def stage2(c, s):
                pool.wait_ge(h_done, c + 2)
                pool.wait_ge(h2_done, c + 1)
                pool.tensor_tensor(hm[:, s], hb[:, s], oz[:, bass.ds(c, 1), 0:M_W].rearrange("p o (h n) -> p (o h) n", h=H),
                                   ALU.mult).then_inc(hm_done, 1)

            def stage3(c, s):
                pool.wait_ge(h2_done, c + 3)
                pool.tensor_tensor(hb[:, s], hb[:, s], oz[:, bass.ds(c, 1), M_W:].rearrange("p o (h n) -> p (o h) n", h=H),
                                   ALU.mult).then_inc(h3_done, 1)

            schedule(pool, stage1, stage2, stage3, None)

        @block.scalar
        def _(act):
            act.preload_act_table_set("natural_log_exp_and_others")
            act.sem_inc(dm_done, 2)
            act.sem_inc(kw_done, 2)

            def stage1(c, s):
                act.wait_ge(am_done, c + 3)
                act.wait_ge(sc_done, 2 * c + 2)
                act.wait_ge(sd_done, c + 1)
                for h in range(H):
                    step = act.activation(dm[:, s, h], am[:, s, h], ACT.Exp, bias=sc[:, s, h:h + 1])
                step.then_inc(dm_done, 1)
                act.wait_ge(kt_done, c + 3)
                act.wait_ge(upd_done, c + 1)
                for h in range(H):
                    step = act.activation(kw[:, s, h], kt_ps[:, h], ACT.Copy, scale=sc[:, s, 2 * H + h:2 * H + h + 1])
                step.then_inc(kw_done, 1)

            def stage2(c, s):
                act.wait_ge(num_done, c + 3)
                act.wait_ge(den_done, c + 1)
                act.activation(two(ad[:, s, :, None]), heads(n_ps)[:, :, :, P:CW], ACT.Abs).then_inc(ad_done, 1)
                act.wait_ge(hm_done, c + 3)
                for h in range(H):
                    step = act.activation(junk[:, h], hm[:, s, h], ACT.Square, accum_out=ssq[:, s, h:h + 1])
                step.then_inc(sq_done, 1)
                act.wait_ge(sq_done, c + 1)
                act.activation(ln[:, s], ssq[:, s], ACT.Ln, bias=eps[:], scale=1.0 / P).then_inc(rn_done, 1)
                act.wait_ge(rn_done, c + 1)
                act.activation(rr[:, s], ln[:, s], ACT.Exp, scale=-0.5).then_inc(r_done, 1)

            schedule(act, stage1, stage2, None, None)

        @block.vector
        def _(dve):
            for n in ("am", "sd", "den", "h2"):
                dve.sem_inc(S[n], 2)
            dve.memset(va[:, :, :, P:CW], 1.0).then_inc(va_set, 1)
            dve.memset(state[:], 0.0).then_inc(c_done, 1)
            dve.sem_inc(h_done, 1)

            def stage1(c, s):
                dve.wait_ge(bc_ld[s], 8 * c + (16 - 8 * s))
                dve.wait_ge(dm_done, c + 1)
                dve.tensor_tensor(am[:, s], bc[:, s, 0], mask[:, None, :].to_broadcast([P, H, MC]), ALU.add).then_inc(am_done, 1)
                dve.wait_ge(s_done, c + 1)
                dve.wait_ge(dm_done, c + 3)
                dve.wait_ge(num_done, c + 1)
                dve.scalar_tensor_tensor(sd[:, s], s_ps[s][:], M_SCALE, dm[:, s], ALU.mult, ALU.mult).then_inc(sd_done, 1)

            def stage2(c, s):
                dve.wait_ge(upd_done, c + 3)
                dve.wait_ge(sc_done, 2 * c + 2)
                dve.wait_ge(c_done, c + 1)
                for h in range(H):
                    step = dve.scalar_tensor_tensor(state[:, h], state[:, h], sc[:, s, 3 * H + h:3 * H + h + 1], head(u_ps, h),
                                                    ALU.mult, ALU.add)
                step.then_inc(c_done, 1)
                dve.wait_ge(ad_done, c + 1)
                dve.tensor_tensor(dn[:, s], ad[:, s], sc[:, s, H:2 * H], ALU.max).then_inc(den_done, 1)
                dve.wait_ge(den_done, c + 3)
                dve.reciprocal(rc[:, s], dn[:, s]).then_inc(rec_done, 1)
                dve.wait_ge(rec_done, c + 1)
                dve.wait_ge(x_done, c + 1)
                dve.tensor_tensor(two(hb[:, s]), heads(n_ps)[:, :, :, 0:P],
                                  two(rc[:, s, :, None]).to_broadcast([P, 2, 2, P]), ALU.mult).then_inc(h_done, 1)

            def stage3(c, s):
                dve.wait_ge(r_done, c + 1)
                dve.tensor_tensor(hb[:, s], hm[:, s], rr[:, s, :, None].to_broadcast([P, H, P]), ALU.mult).then_inc(h2_done, 1)

            def stage4(c, s):
                dve.wait_ge(x_done, c + 3)
                dve.wait_ge(st[s], 8 * c + (16 - 8 * s))
                dve.tensor_tensor(om[:, s], x_ps[:], gain[:, :, None].to_broadcast([P, H, MC]), ALU.mult).then_inc(om_done, 1)

            dve.wait_ge(ld_g, 16)
            dve.wait_ge(mask_set, 2)
            schedule(dve, stage1, stage2, stage3, stage4)

        @block.tensor
        def _(pe):
            for n in ("kt", "num", "upd", "x"):
                pe.sem_inc(S[n], 2)
            pe.wait_ge(va_set, 1)

            def stage1(c, s):
                pe.wait_ge(ks_done, c + 1)
                pe.wait_ge(sd_done, c + 1)
                for h in range(H):
                    last = pe.matmul(s_ps[s][:, h], ks[:, s, h], qk[:, h, bass.ds(c * MC, MC)], start=True, stop=True)
                last.then_inc(s_done, 1)
                pe.wait_ge(kw_done, c + 2)
                for h in range(H):
                    last = pe.transpose(kt_ps[:, h], ks[:, s, h], ident[:])
                last.then_inc(kt_done, 1)

            def stage2(c, s):
                pe.wait_ge(va_ld[s], 8 * c + (16 - 8 * s))
                pe.wait_ge(sd_done, c + 3)
                pe.wait_ge(qp_done, c + 3)
                pe.wait_ge(c_done, c + 1)
                pe.wait_ge(h_done, c + 1)
                for h in range(H):
                    pe.matmul(head(n_ps, h), sd[:, s, h], va[:, s, h], start=True, stop=False)
                    last = pe.matmul(head(n_ps, h), qp[:, s, h], state[:, h], start=False, stop=True)
                last.then_inc(num_done, 1)
                pe.wait_ge(kw_done, c + 3)
                for h in range(H):
                    last = pe.matmul(head(u_ps, h), kw[:, s, h], va[:, s, h], start=True, stop=True)
                last.then_inc(upd_done, 1)

            def stage3(c, s):
                pe.wait_ge(h3_done, c + 3)
                pe.wait_ge(om_done, c) if not isinstance(c, int) or c > 0 else None
                for h in range(H):
                    last = pe.transpose(x_ps[:, h], hb[:, s, h], ident[:])
                last.then_inc(x_done, 1)

            schedule(pe, stage1, stage2, stage3, None)


C_TILES = 2
CN = 512


def conv_mixer(nc, env, d, ctx):
    sb, ps, sem = tools(nc, ctx)
    eps = env["eps"]
    z = sb("cv_z", [P, C_TILES, SEQ])
    acc = sb("cv_acc", [P, C_TILES, SEQ])
    par = sb("cv_par", [P, 2, C_TILES])
    ones = sb("cv_ones", [P, P])
    xc, sq, ln, rr = (sb(f"cv_{n}", [P, C_TILES, CN]) for n in ("xc", "sq", "ln", "rr"))
    m_ps, v_ps = ps("cv_m_ps", [P, 2, CN]), ps("cv_v_ps", [P, 2, CN])
    ld_a, ld_z, ld_w = (sem(f"cv_ld_{n}") for n in "azw")
    ones_set = sem("cv_ones_set")
    mean, xc_done, sq_done, var, ln_done, r_done, y_done, s_done, out_done, st = (
        sem(f"cv_{n}") for n in ("mean", "xc_done", "sq_done", "var", "ln_done", "r_done", "y_done", "s_done", "out_done", "st"))
    steps = SEQ // CN

    with nc.Block() as block:
        @block.sync
        def _(sp):
            sp.dma_start(acc[:], d["cva"].rearrange("k p n -> p k n")).then_inc(ld_a, 16)
            sp.dma_start(par[:], d["cv_par"]).then_inc(ld_w, 16)
            sp.dma_start(z[:], d["fm"][C_Z].rearrange("k p n -> p k n")).then_inc(ld_z, 16)
            sp.wait_ge(out_done, steps)
            sp.dma_start(d["mixed"][6:6 + C_TILES].rearrange("k p n -> p k n"), acc[:]).then_inc(st, 16)
            sp.wait_ge(st, 16)

        @block.gpsimd
        def _(pool):
            pool.memset(ones[:], 1.0 / (C_TILES * P)).then_inc(ones_set, 1)

        @block.scalar
        def _(act):
            act.wait_ge(ld_w, 16)
            for i in range(steps):
                act.wait_ge(xc_done, 2 * i + 2)
                if i:
                    act.wait_ge(var, i)
                act.activation(sq[:], xc[:], ACT.Square).then_inc(sq_done, 1)
                act.wait_ge(var, i + 1)
                act.activation(ln[:, 0], v_ps[:, i % 2], ACT.Ln, bias=eps[:]).then_inc(ln_done, 1)
                act.wait_ge(ln_done, i + 1)
                act.activation(rr[:, 0], ln[:, 0], ACT.Exp, scale=-0.5).then_inc(r_done, 1)
                act.wait_ge(y_done, 2 * i + 2)
                for t in range(C_TILES):
                    act.activation(xc[:, t], xc[:, t], ACT.Silu, bias=par[:, 1, t:t + 1], scale=par[:, 0, t:t + 1]).then_inc(s_done, 1)

        @block.vector
        def _(dve):
            dve.wait_ge(ld_z, 16)
            for i in range(steps):
                at = slice(i * CN, (i + 1) * CN)
                dve.wait_ge(mean, i + 1)
                if i:
                    dve.wait_ge(out_done, i)
                for t in range(C_TILES):
                    dve.tensor_tensor(xc[:, t], acc[:, t, at], m_ps[:, i % 2], ALU.subtract).then_inc(xc_done, 1)
                dve.wait_ge(r_done, i + 1)
                dve.wait_ge(xc_done, 2 * i + 2)
                for t in range(C_TILES):
                    dve.tensor_tensor(xc[:, t], xc[:, t], rr[:, 0], ALU.mult).then_inc(y_done, 1)
                dve.wait_ge(s_done, 2 * i + 2)
                dve.tensor_tensor(acc[:, :, at], xc[:], z[:, :, at], ALU.mult).then_inc(out_done, 1)

        @block.tensor
        def _(pe):
            pe.wait_ge(ones_set, 1)
            pe.wait_ge(ld_a, 16)
            for i in range(steps):
                if i >= 2:
                    pe.wait_ge(xc_done, 2 * i - 2)
                for t in range(C_TILES):
                    last = pe.matmul(m_ps[:, i % 2], ones[:], acc[:, t, i * CN:(i + 1) * CN], start=(t == 0), stop=(t == C_TILES - 1))
                last.then_inc(mean, 1)
                pe.wait_ge(sq_done, i + 1)
                if i >= 2:
                    pe.wait_ge(ln_done, i - 1)
                for t in range(C_TILES):
                    last = pe.matmul(v_ps[:, i % 2], ones[:], sq[:, t], start=(t == 0), stop=(t == C_TILES - 1))
                last.then_inc(var, 1)


OT = P
N_OT = SEQ // OT


def final(nc, env, d, ctx):
    sb, ps, sem = tools(nc, ctx)
    ident = env["ident"]
    wr = sb("o_wr", [P, 2, D])
    wh, wl = sb("o_wh", [P, KD, D], F32R), sb("o_wl", [P, KD, D], F32R)
    m = sb("o_m", [P, 2, KD, OT])
    mh, ml = sb("o_mh", [P, 2, KD, OT], F32R), sb("o_ml", [P, 2, KD, OT], F32R)
    x = sb("o_x", [P, 2, KD, OT])
    y = sb("o_y", [P, 2, D])
    y_ps = [ps(f"o_y_ps{i}", [P, 2, D // 2]) for i in range(2)]
    x_ps = [ps(f"o_x_ps{i}", [P, 2, D // 2]) for i in range(2)]
    ld_w, ld_m, ld_x, st = ([sem(f"o_{n}{s}") for s in range(2)] for n in ("ld_w", "ld_m", "ld_x", "st"))
    wh_done, wl_done, mh_done, ml_done, y_done, add_done, turned = (
        sem(f"o_{n}") for n in ("wh_done", "wl_done", "mh_done", "ml_done", "y_done", "add_done", "turned"))
    ready, xs_copied = sem("o_ready"), sem("o_xs_copied")

    with nc.Block() as block:
        @block.sync
        def _(sp):
            for s in range(2):
                sp.sem_inc(st[s], 16)
            w = d["w_out"].rearrange("(k p) n -> k p n", p=P)

            def load(c, s):
                at = bass.ds(c * OT if isinstance(c, int) else sp.snap(c * OT, min_val=0, max_val=SEQ - OT), OT)
                src_m, src_x = (d[n][:, :, at].rearrange("k p n -> p k n") for n in ("mixed", "x2"))
                sp.wait_ge(ml_done, c + 1)
                sp.sem_inc(ready, 1)
                sp.dma_start(m[:, s], src_m).then_inc(ld_m[s], 16)
                sp.wait_ge(turned, c + 1)
                sp.sem_inc(ready, 1)
                sp.dma_start(x[:, s], src_x).then_inc(ld_x[s], 16)

            def store(c, s):
                dst = d["out"][bass.ds(c * OT if isinstance(c, int) else sp.snap(c * OT, min_val=0, max_val=SEQ - OT), OT)]
                sp.wait_ge(add_done, c + 1 + 2)
                sp.sem_inc(ready, 1)
                sp.dma_start(dst, y[:, s]).then_inc(st[s], 16)

            for c in range(2):
                load(c, c)
            for k in range(KD):
                if k >= 2:
                    sp.wait_ge(wl_done, k - 1)
                sp.dma_start(wr[:, k % 2], w[k]).then_inc(ld_w[k % 2], 16)
            with sp.Fori(0, N_OT // 2 - 1) as i:
                for s in range(2):
                    load(2 * i + (2 + s), s)
                    store(2 * i + s, s)
            for s in range(2):
                store(N_OT - 2 + s, s)
            for s in range(2):
                sp.wait_ge(st[s], 16 + 16 * (N_OT // 2))

        @block.scalar
        def _(act):
            def split(c, s):
                act.wait_ge(ld_m[s], 8 * c + (16 - 8 * s))
                act.wait_ge(y_done, c + 1)
                act.copy(mh[:, s], m[:, s]).then_inc(mh_done, 1)

            split(0, 0)
            for k in range(KD):
                act.wait_ge(ld_w[k % 2], 16 * (k // 2) + 16)
                act.copy(wh[:, k], wr[:, k % 2]).then_inc(wh_done, 1)
            split(1, 1)
            with act.Fori(1, N_OT // 2) as i:
                for s in range(2):
                    split(2 * i + s, s)

        @block.gpsimd
        def _(pool):
            pool.sem_inc(ml_done, 2)

            def split(c, s):
                pool.wait_ge(mh_done, c + 1)
                pool.tensor_tensor(ml[:, s], m[:, s], mh[:, s].bitcast(F32), ALU.subtract).then_inc(ml_done, 1)

            split(0, 0)
            for k in range(KD):
                pool.wait_ge(wh_done, k + 1)
                pool.tensor_tensor(wl[:, k], wr[:, k % 2], wh[:, k].bitcast(F32), ALU.subtract).then_inc(wl_done, 1)
            split(1, 1)
            with pool.Fori(1, N_OT // 2) as i:
                for s in range(2):
                    split(2 * i + s, s)

        @block.vector
        def _(dve):
            dve.memset(y[:, 0, 0:1], 0.0).then_inc(add_done, 2)
            dve.wait_ge(add_done, 2)

            def add(c, s):
                dve.wait_ge(turned, c + 1 + 2)
                dve.wait_ge(st[s], 8 * c + (16 - 8 * s))
                dve.tensor_copy(y[:, s].rearrange("p (a n) -> p a n", a=2), x_ps[s][:]).then_inc(xs_copied, 1)
                dve.wait_ge(y_done, c + 1 + 2)
                dve.wait_ge(xs_copied, c + 1)
                ys = y[:, s].rearrange("p (a n) -> p a n", a=2)
                dve.tensor_tensor(ys, ys, y_ps[s][:], ALU.add).then_inc(add_done, 1)

            with dve.Fori(0, N_OT // 2) as i:
                for s in range(2):
                    add(2 * i + s, s)

        @block.tensor
        def _(pe):
            pe.sem_inc(y_done, 2)
            pe.sem_inc(turned, 2)

            def step(c, s, split_wait):
                pe.wait_ge(ld_x[s], 8 * c + (16 - 8 * s))
                pe.wait_ge(add_done, c + 1)
                for k in range(KD):
                    last = pe.transpose(x_ps[s][:, k // 4, k % 4 * P:(k % 4 + 1) * P], x[:, s, k], ident[:])
                last.then_inc(turned, 1)
                pe.wait_ge(ml_done, c + 1 + 2)
                for n in range(2):
                    cols = slice(n * (D // 2), (n + 1) * (D // 2))
                    for k in range(KD):
                        if split_wait and n == 0:
                            pe.wait_ge(wl_done, k + 1)
                        for i, (l, r) in enumerate(((mh, wh), (ml, wh), (mh, wl))):
                            last = pe.matmul(y_ps[s][:, n], l[:, s, k], r[:, k, cols], start=(k == 0 and i == 0),
                                             stop=(k == KD - 1 and i == 2))
                last.then_inc(y_done, 1)

            for s in range(2):
                step(s, s, s == 0)
            with pe.Fori(1, N_OT // 2) as i:
                for s in range(2):
                    step(2 * i + s, s, False)


def layouts(a):
    import numpy as np
    c = np.ascontiguousarray
    x = a["x"][0]
    pair = lambda v: v.reshape(NP, 2 * 64, *v.shape[2:]).swapaxes(0, 1)
    out = {}
    out["x_chunk"] = c(x.reshape(NCH, T, D))
    out["x_group"] = c(x.reshape(NCH, 2, S8, 2 * NP, H).transpose(2, 4, 1, 3, 0).reshape(P, 2, 2 * NP, NCH))
    dt = np.repeat(a["ssm_log_dt"][0][:, None], 64, 1)
    out["s5_prm"] = c(np.stack([pair(a["ssm_lam_re"][0]), pair(a["ssm_lam_im"][0]), pair(dt)], 1))
    cT = lambda v: pair(v.swapaxes(1, 2))
    out["s5_bc"] = c(np.stack([pair(a["ssm_b_re"][0]), pair(a["ssm_b_im"][0]),
                               cT(a["ssm_c_re"][0]), cT(a["ssm_c_im"][0])], 1))
    g = a["norm_mix"][0].reshape(NP, 2, 1, H)
    out["s5_gain"] = c(np.repeat(g, 64, 2).reshape(NP, P, H).swapaxes(0, 1))
    out["s5_skip"] = c(np.stack([a["ssm_d"][0].reshape(NP, 2 * H).T, a["norm_mix"][0].reshape(NP, 2 * H).T], 1))
    return out


def tiles(w, cols, k_tiles=None):
    import numpy as np
    w = w[:, cols]
    k = w.shape[0] // P
    return np.ascontiguousarray(w.reshape(k, P, -1, P).transpose(2, 1, 0, 3).reshape(-1, P, k * P))


FM_COLS = [(3848, 4104), (3592, 3848), (4104, 4360), (768, 1024), (1024, 2048), (0, 512)]
TM_SRC = [(512, 768), (2048, 3584)]
GI_COLS = (3584, 3592)


def layouts2(a):
    import numpy as np
    c = np.ascontiguousarray
    out = {}
    by_feat = lambda v: c(v.T.reshape(-1, P, SEQ))
    out["x_feat"], out["p_feat"] = by_feat(a["x"][0]), by_feat(a["p"][0, 0])
    out["gains"] = c(np.stack([a[k].reshape(KD, P).T for k in ("norm_ffn", "norm_ple", "norm_final", "norm_g_2")], 1))
    glu, w1, w2 = a["ssm_w_glu"][0], a["mlp_w1"][0], a["mlp_w2"][0]
    order = lambda spans: np.concatenate([np.arange(*s) for s in spans])
    glu_t = tiles(glu, slice(None))
    parts = [glu_t[i] for m in range(KD) for i in (KD + m, m)]
    w1_t = tiles(w1, slice(None))
    w2_t = tiles(w2, slice(None)).reshape(KD // 2, 2, P, F_GROUPS, F_TILES * P)
    for fg in range(F_GROUPS):
        parts += [w1_t[fg * F_TILES + f] for f in range(F_TILES)]
        parts += [w2_t[m2, :, :, fg].transpose(1, 0, 2).reshape(P, -1) for m2 in range(KD // 2)]
    gate_t, ple_t = tiles(a["ple_gate_w"][0], slice(None)), tiles(a["ple_w"][0], slice(None))
    for m in range(KD):
        parts += [gate_t[m], np.tile(ple_t[m], (1, 4))]
    w_in = a["w_in_2"][0]
    parts += list(tiles(w_in, order(FM_COLS))) + list(tiles(w_in, order(TM_SRC)))
    out["wall"] = c(np.stack(parts))
    out["w_gi"] = c(w_in[:, GI_COLS[0]:GI_COLS[1]].reshape(KD, P, 8).transpose(1, 0, 2))
    return out


def layouts3(a):
    import numpy as np
    c = np.ascontiguousarray
    out = {}
    out["att_gain"] = c(np.stack([np.tile(a[k][0], P // A_DIM) for k in ("att_q_g_2", "att_k_g_2")], 1))
    rel = np.clip(np.arange(QB)[:, None] - np.arange(WIN)[None, :] + (WIN - QB), -128, 128) + 128
    out["att_bias"] = c(a["att_rel_bias_2"][0][:, rel].swapaxes(0, 1))
    per = lambda v, n: v.reshape(*v.shape[:-1], n, P)
    out["ml_cw"] = c(per(a["ml_qk_conv_w_2"][0], 2 * M_HEADS).transpose(2, 1, 0))
    out["ml_cb"] = c(per(a["ml_qk_conv_b_2"][0], 2 * M_HEADS).T)
    out["ml_bif"] = c(np.stack([a["ml_b_i_2"][0], a["ml_b_f_2"][0]], 1))
    out["ml_gain"] = c(per(a["ml_out_g_2"][0], M_HEADS).T)
    out["cv_w"] = c(per(a["cv_dw_w_2"][0], C_TILES).transpose(2, 1, 0))
    out["cv_par"] = c(np.stack([per(a[k][0], C_TILES).T for k in ("cv_ln_g_2", "cv_ln_b_2")], 1))
    out["cv_b"] = c(per(a["cv_dw_b_2"][0], C_TILES).T)
    out["w_out"] = c(a["w_out_2"][0])
    return out


def scratch(nc, d):
    shapes = {
        "ca": (P, NQ, 2 * QP * (T + 1) * H), "z": (1, 2 * NP * H, (S8 - 1) * H + T * H),
        "y_hi": (KD, P, SEQ), "y_lo": (KD, P, SEQ),
        "x2": (KD, P, SEQ),
        "fm": (N_FM, P, SEQ), "cva": (2, P, SEQ), "gi": (2 * M_HEADS, SEQ), "tm": (SEQ, sum(TM_COLS)),
        "rows": (2, M_HEADS, SEQ), "mixed": (KD, P, SEQ),
    }
    for name, shape in shapes.items():
        if name not in d:
            d[name] = nc.dram_tensor(name + "_scratch", shape, F32).ap()


def program(nc, d):
    scratch(nc, d)
    env = {}
    with ExitStack() as ctx:
        constants(nc, env, ctx)
        s5_stage(nc, env, d)
        for stage in (dense, attention, mlstm, conv_mixer, final):
            with ExitStack() as c:
                stage(nc, env, d, c)


def kernel(**inputs):
    import numpy as np
    import concourse.bacc as bacc
    from concourse.bass_utils import run_bass_kernel_spmd
    a = {k: np.asarray(v) for k, v in inputs.items()}
    arrays = {"in_" + k: v for part in (layouts, layouts2, layouts3) for k, v in part(a).items()}
    nc = bacc.Bacc("TRN2", target_bir_lowering=False, num_devices=1)
    d = {k[3:]: nc.dram_tensor(k, v.shape, F32, kind="ExternalInput").ap() for k, v in arrays.items()}
    d["out"] = nc.dram_tensor("out", (SEQ, D), F32, kind="ExternalOutput").ap()
    program(nc, d)
    r = run_bass_kernel_spmd(nc, [arrays], core_ids=[0])
    return r.results[0]["out"].reshape(1, SEQ, D)
```

```python
from contextlib import ExitStack

import concourse.bass as bass
from concourse import mybir

ALU = mybir.AluOpType
ACT = mybir.ActivationFunctionType
AX = mybir.AxisListType
F32 = mybir.dt.float32
F32R = mybir.dt.float32r

P = 128
SEQ = 2048
D = 1024
EPS = 1e-6
TWO_PI = 6.283185307179586
PI_LOW = 3.1415925
PI2_A, PI2_B = 6.28125, 0.0019350051879882812
PI2_C = TWO_PI - PI2_A - PI2_B
ROUND = 1.5 * 2.0 ** 23


def tools(nc, ctx):
    held = []

    def release():
        nc.clear_and_free_semaphores(held)
        nc.all_engine_barrier()

    ctx.callback(release)

    def sb(name, shape, dt=F32):
        return ctx.enter_context(nc.sbuf_tensor(name, shape, dt))

    def ps(name, shape):
        return ctx.enter_context(nc.psum_tensor(name, shape, F32))

    def sem(name):
        held.append(nc.alloc_semaphore(name))
        return held[-1]

    return sb, ps, sem


T = 16
NCH = SEQ // T
NP = 32
H = 16
S8 = 8
QP = 4
NQ = NP // QP
QS = 2
NS = NP // QS


def s5_setup(nc, env, d, ctx):
    sb, ps, sem = tools(nc, ctx)
    U, Win, ident = env["U"], env["Win"], env["ident"]
    aT, eps = env["aT"], env["eps"]
    prm = sb("s5_prm", [P, 3, NP])
    bc = sb("s5_bc", [P, 4, NP, H])
    gain = sb("s5_gain", [P, NP, H])
    skip = sb("s5_skip", [2 * H, 2, NP])
    xin = sb("s5_xin", [P, 2, D])
    ss = sb("s5_ss", [P, T])
    rms = sb("s5_rms", [P, T])
    rexp = sb("s5_rexp", [P, 2, S8, H])
    rtile = sb("s5_rtile", [P, 2, NCH])
    w = sb("s5_w", [P, 16, NP])
    pw = sb("s5_pw", [P, 2, NP, T + 1])
    pwr = sb("s5_pwr", [P, 2, NP, T])
    bb = sb("s5_bb", [P, 2, NP, H])
    bbd = sb("s5_bbd", [P, 2, NP, 2, H])
    cas = [sb(f"s5_ca{i}", [P, 2, QS, T + 1, H]) for i in range(2)]
    cat = sb("s5_cat", [P, 2, QS, T + 1, H])
    ab = sb("s5_ab", [P, 2, QS, T, H])
    tmp = sb("s5_tmp", [P, 4, NP, H])
    bt, pt = tmp, tmp
    abt = sb("s5_abt", [P, 2, QS, T, H])
    zss = [sb(f"s5_zs{i}", [2 * H, QS, T * H]) for i in range(2)]
    zz = sb("s5_zz", [2 * H, NP, H])
    eyeh = sb("s5_eyeh", [2 * H, H])
    zero = sb("s5_zero", [P, (S8 - 1) * H])
    pst = ps("s5_pst", [P, 4, NCH])
    psz = [ps(f"s5_psz{i}", [2 * H, 2, T * H]) for i in range(2)]
    psw = [ps(f"s5_psw{i}", [P, 4, P]) for i in range(2)]
    ld_prm, ld_u = sem("s5_ld_prm"), sem("s5_ld_u")
    ld_x = [sem("s5_ld_x0"), sem("s5_ld_x1")]
    act_prm, sq_done, rms_sqrt = sem("s5_act_prm"), sem("s5_sq_done"), sem("s5_rms_sqrt")
    dve_prm, dve_rms, r_copied = sem("s5_dve_prm"), sem("s5_dve_rms"), sem("s5_r_copied")
    rexp_done, r_turned = sem("s5_rexp_done"), sem("s5_r_turned")
    chain, pchain = sem("s5_chain"), sem("s5_pchain")
    bb_ready, ca_ready, ab_ready = sem("s5_bb_ready"), sem("s5_ca_ready"), sem("s5_ab_ready")
    z_mm, ab_turned, z_ready, win_ready = sem("s5_z_mm"), sem("s5_ab_turned"), sem("s5_z_ready"), sem("s5_win_ready")
    st_ca, st_z = [sem("s5_st_ca0"), sem("s5_st_ca1")], [sem("s5_st_z0"), sem("s5_st_z1")]
    st_zero, zero_set, pool_set = sem("s5_st_zero"), sem("s5_zero_set"), sem("s5_pool_set")
    pw_ready, ca_free, u_done = sem("s5_pw_ready"), sem("s5_ca_free"), sem("s5_u_done")

    with nc.Block() as block:
        @block.sync
        def _(sp):
            sp.dma_start(prm[:], d["s5_prm"]).then_inc(ld_prm, 16)
            sp.dma_start(bc[:], d["s5_bc"]).then_inc(ld_prm, 16)
            sp.dma_start(gain[:], d["s5_gain"]).then_inc(ld_prm, 16)
            sp.dma_start(skip[:], d["s5_skip"]).then_inc(ld_prm, 16)
            for i in range(T):
                if i >= 2:
                    sp.wait_ge(sq_done, i - 1)
                sp.dma_start(xin[:, i % 2], d["x_chunk"][:, i]).then_inc(ld_x[i % 2], 16)
            for hf in range(2):
                sp.dma_start(U[:, hf], d["x_group"][:, hf]).then_inc(ld_u, 16)
            sp.wait_ge(zero_set, 1)
            for i in range(2):
                sp.dma_start(d["z"][:, i * 512:(i + 1) * 512, 0:(S8 - 1) * H].rearrange("o (a b) n -> (o a) b n", a=P),
                             zero[:, None, :].to_broadcast([P, 4, (S8 - 1) * H])).then_inc(st_zero, 16)
            def store_taps(q):
                sp.wait_ge(z_ready, q + 1)
                sp.dma_start(d["z"][0].rearrange("(j g) n -> g j n", g=2 * H)[:, q * QS:(q + 1) * QS, (S8 - 1) * H:],
                             zss[q % 2][:]).then_inc(st_z[q % 2], 16)

            for q in range(NS):
                sp.wait_ge(ca_ready, q + 1)
                lo = q % (QP // QS) * QS
                sp.dma_start(d["ca"][:, q // (QP // QS)].rearrange("p (r j n) -> p r j n", r=2, j=QP)[:, :, lo:lo + QS],
                             cas[q % 2][:].rearrange("p r j t h -> p r j (t h)")).then_inc(st_ca[q % 2], 16)
                if q:
                    store_taps(q - 1)
            store_taps(NS - 1)
            for i in range(2):
                sp.wait_ge(st_ca[i], 16 * (NS // 2))
                sp.wait_ge(st_z[i], 16 * (NS // 2))
            sp.wait_ge(st_zero, 32)

        @block.scalar
        def _(act):
            act.wait_ge(ld_prm, 64)
            act.activation(w[:, 0], prm[:, 2], ACT.Exp).then_inc(act_prm, 1)
            act.wait_ge(dve_prm, 1)
            act.activation(w[:, 2], w[:, 1], ACT.Exp).then_inc(act_prm, 1)
            act.wait_ge(dve_prm, 2)
            act.activation(w[:, 8], w[:, 7], ACT.Sin).then_inc(act_prm, 1)
            act.activation(w[:, 9], w[:, 7], ACT.Abs).then_inc(act_prm, 1)
            act.wait_ge(act_prm, 4)
            act.activation(w[:, 10], w[:, 9], ACT.Sin, scale=-1.0, bias=env["halfpi"][:]).then_inc(act_prm, 1)
            for i in range(T):
                act.wait_ge(ld_x[i % 2], 16 * (i // 2 + 1))
                act.activation(xin[:, i % 2], xin[:, i % 2], ACT.Square, accum_out=ss[:, i:i + 1]).then_inc(sq_done, 1)
            act.wait_ge(sq_done, T)
            act.activation(rms[:], ss[:], ACT.Sqrt, scale=1.0 / D, bias=eps[:]).then_inc(rms_sqrt, 1)
            act.wait_ge(r_turned, 2)
            act.copy(rtile[:], pst[:, 0:2]).then_inc(r_copied, 1)
            for j in range(NP):
                act.wait_ge(ab_turned, j + 1)
                act.copy(Win[:, j].rearrange("p a b m -> p (a b) m"), psw[j % 2][:]).then_inc(win_ready, 1)

        @block.vector
        def _(dve):
            n = [0]

            def then(ins):
                n[0] += 1
                ins.then_inc(chain, 1)
                dve.wait_ge(chain, n[0])

            dve.wait_ge(ld_prm, 64)
            dve.wait_ge(act_prm, 1)
            dve.tensor_tensor(w[:, 1], prm[:, 0], w[:, 0], ALU.mult).then_inc(dve_prm, 1)
            then(dve.tensor_tensor(w[:, 3], prm[:, 1], w[:, 0], ALU.mult))
            then(dve.tensor_scalar(w[:, 4], w[:, 3], 1.0 / TWO_PI, ROUND, ALU.mult, ALU.add))
            then(dve.tensor_scalar(w[:, 5], w[:, 4], ROUND, None, ALU.subtract))
            then(dve.scalar_tensor_tensor(w[:, 6], w[:, 5], -PI2_A, w[:, 3], ALU.mult, ALU.add))
            then(dve.scalar_tensor_tensor(w[:, 3], w[:, 5], -PI2_B, w[:, 6], ALU.mult, ALU.add))
            then(dve.scalar_tensor_tensor(w[:, 6], w[:, 5], -PI2_C, w[:, 3], ALU.mult, ALU.add))
            dve.tensor_scalar(w[:, 7], w[:, 6], PI_LOW, -PI_LOW, ALU.min, ALU.max).then_inc(dve_prm, 1)
            dve.wait_ge(act_prm, 5)
            a1r, a1i = pw[:, 0, :, 1], pw[:, 1, :, 1]
            then(dve.tensor_tensor(a1r, w[:, 2], w[:, 10], ALU.mult))
            then(dve.tensor_tensor(a1i, w[:, 2], w[:, 8], ALU.mult))
            then(dve.memset(pw[:, 0, :, 0:1], 1.0))
            then(dve.memset(pw[:, 1, :, 0:1], 0.0))
            lr, li = prm[:, 0], prm[:, 1]
            then(dve.tensor_scalar(w[:, 0], a1r, -1.0, None, ALU.add))
            then(dve.tensor_tensor(w[:, 3], lr, lr, ALU.mult))
            then(dve.tensor_tensor(w[:, 4], li, li, ALU.mult))
            then(dve.tensor_tensor(w[:, 5], w[:, 3], w[:, 4], ALU.add))
            then(dve.reciprocal(w[:, 6], w[:, 5]))
            then(dve.tensor_tensor(w[:, 3], w[:, 0], lr, ALU.mult))
            then(dve.tensor_tensor(w[:, 4], a1i, li, ALU.mult))
            then(dve.tensor_tensor(w[:, 5], w[:, 3], w[:, 4], ALU.add))
            then(dve.tensor_tensor(w[:, 11], w[:, 5], w[:, 6], ALU.mult))
            then(dve.tensor_tensor(w[:, 3], a1i, lr, ALU.mult))
            then(dve.tensor_tensor(w[:, 4], w[:, 0], li, ALU.mult))
            then(dve.tensor_tensor(w[:, 5], w[:, 3], w[:, 4], ALU.subtract))
            then(dve.tensor_tensor(w[:, 12], w[:, 5], w[:, 6], ALU.mult))
            cr = w[:, 11, :, None].to_broadcast([P, NP, H])
            ci = w[:, 12, :, None].to_broadcast([P, NP, H])
            then(dve.tensor_tensor(bt[:, 0], bc[:, 0], cr, ALU.mult))
            then(dve.tensor_tensor(bt[:, 1], bc[:, 1], ci, ALU.mult))
            then(dve.tensor_tensor(bt[:, 2], bc[:, 1], cr, ALU.mult))
            then(dve.tensor_tensor(bt[:, 3], bc[:, 0], ci, ALU.mult))
            then(dve.tensor_tensor(bt[:, 0], bt[:, 0], bt[:, 1], ALU.subtract))
            then(dve.tensor_tensor(bt[:, 2], bt[:, 2], bt[:, 3], ALU.add))
            then(dve.tensor_tensor(bb[:, 0], bt[:, 0], gain[:], ALU.mult))
            then(dve.tensor_tensor(bb[:, 1], bt[:, 2], gain[:], ALU.mult))
            m = 1
            while m < T:
                lo_r, lo_i = pw[:, 0, :, 1:m + 1], pw[:, 1, :, 1:m + 1]
                tr = pw[:, 0, :, m:m + 1].to_broadcast([P, NP, m])
                ti = pw[:, 1, :, m:m + 1].to_broadcast([P, NP, m])
                then(dve.tensor_tensor(pt[:, 0, :, 0:m], lo_r, tr, ALU.mult))
                then(dve.tensor_tensor(pt[:, 1, :, 0:m], lo_i, ti, ALU.mult))
                then(dve.tensor_tensor(pt[:, 2, :, 0:m], lo_r, ti, ALU.mult))
                then(dve.tensor_tensor(pt[:, 3, :, 0:m], lo_i, tr, ALU.mult))
                then(dve.tensor_tensor(pw[:, 0, :, m + 1:2 * m + 1], pt[:, 0, :, 0:m], pt[:, 1, :, 0:m], ALU.subtract))
                then(dve.tensor_tensor(pw[:, 1, :, m + 1:2 * m + 1], pt[:, 2, :, 0:m], pt[:, 3, :, 0:m], ALU.add))
                m *= 2
            for s in range(T):
                then(dve.tensor_copy(pwr[:, :, :, s], pw[:, :, :, T - 1 - s]))
            then(dve.tensor_copy(aT[:, 0], pw[:, 0, :, T]))
            then(dve.tensor_copy(aT[:, 1], pw[:, 1, :, T]))
            then(dve.memset(bbd[:], 0.0))
            for g in range(2):
                rows = slice(g * 64, (g + 1) * 64)
                then(dve.tensor_copy(bbd[rows, :, :, g, :], bb[rows]))
            dve.tensor_scalar(w[:, 13], w[:, 11], 0.0, None, ALU.add).then_inc(bb_ready, 1)
            dve.wait_ge(pool_set, 2)
            then(dve.tensor_tensor(w[0:2 * H, 14], skip[:, 0], skip[:, 1], ALU.mult))
            then(dve.tensor_tensor(zz[:], eyeh[:, None, :].to_broadcast([2 * H, NP, H]),
                                   w[0:2 * H, 14, :, None].to_broadcast([2 * H, NP, H]), ALU.mult))
            dve.wait_ge(rms_sqrt, 1)
            then(dve.reciprocal(ss[:], rms[:]))
            dve.tensor_copy(rexp[:].rearrange("p a s h -> p (a s) h"),
                            ss[:, :, None].to_broadcast([P, T, H])).then_inc(rexp_done, 1)
            def taps(q):
                js = slice(q * QS, (q + 1) * QS)
                dve.wait_ge(z_mm, q + 1)
                if q >= 2:
                    dve.wait_ge(st_z[q % 2], 16 * (q // 2))
                out = zss[q % 2][:].rearrange("p j (t h) -> p j t h", h=H)
                src = psz[q % 2][:].rearrange("p j (t h) -> p j t h", h=H)
                dve.tensor_copy(out[:, :, 1:], src[:, :, 1:])
                dve.tensor_tensor(out[:, :, 0], src[:, :, 0], zz[:, js], ALU.add).then_inc(z_ready, 1)

            for q in range(NS):
                js = slice(q * QS, (q + 1) * QS)
                shape = [P, QS, T + 1, H]
                c_r = bc[:, 2, js, None, :].to_broadcast(shape)
                c_i = bc[:, 3, js, None, :].to_broadcast(shape)
                p_r = pw[:, 0, js, :, None].to_broadcast(shape)
                p_i = pw[:, 1, js, :, None].to_broadcast(shape)
                ca = cas[q % 2]
                if q >= 2:
                    dve.wait_ge(st_ca[q % 2], 16 * (q // 2))
                    dve.wait_ge(z_mm, q - 1)
                then(dve.tensor_tensor(cat[:, 0], c_r, p_r, ALU.mult))
                then(dve.tensor_tensor(cat[:, 1], c_i, p_i, ALU.mult))
                then(dve.tensor_tensor(ca[:, 0], cat[:, 0], cat[:, 1], ALU.subtract))
                then(dve.tensor_tensor(cat[:, 0], c_r, p_i, ALU.mult))
                then(dve.tensor_tensor(cat[:, 1], c_i, p_r, ALU.mult))
                dve.scalar_tensor_tensor(ca[:, 1], cat[:, 0], -1.0, cat[:, 1], ALU.mult, ALU.subtract).then_inc(ca_ready, 1)
                dve.wait_ge(ca_ready, q + 1)
                if q:
                    taps(q - 1)
                if q in (NS // 4, NS // 2):
                    hf = q // (NS // 2)
                    dve.wait_ge(r_copied, 1)
                    dve.wait_ge(ld_u, 32)
                    dve.tensor_tensor(U[:, hf], U[:, hf], rtile[:, hf, None, :].to_broadcast([P, 2 * NP, NCH]),
                                      ALU.mult).then_inc(u_done, 1)
            taps(NS - 1)

        @block.gpsimd
        def _(pool):
            n = [0]

            def then(ins):
                n[0] += 1
                ins.then_inc(pchain, 1)
                pool.wait_ge(pchain, n[0])

            pool.memset(zero[:], 0.0).then_inc(zero_set, 1)
            pool.memset(eyeh[:], 0.0).then_inc(pool_set, 1)
            pool.wait_ge(pool_set, 1)
            then(pool.affine_select(out=eyeh[:], in_=eyeh[:], compare_op=ALU.not_equal, fill=1.0, base=0,
                                    pattern=[[-1, H]], channel_multiplier=1))
            pool.affine_select(out=eyeh[:], in_=eyeh[:], compare_op=ALU.not_equal, fill=1.0, base=-H,
                               pattern=[[-1, H]], channel_multiplier=1).then_inc(pool_set, 1)
            pool.wait_ge(bb_ready, 1)
            for q in range(NS):
                js = slice(q * QS, (q + 1) * QS)
                shape = [P, QS, T, H]
                b_r = bb[:, 0, js, None, :].to_broadcast(shape)
                b_i = bb[:, 1, js, None, :].to_broadcast(shape)
                p_r = pwr[:, 0, js, :, None].to_broadcast(shape)
                p_i = pwr[:, 1, js, :, None].to_broadcast(shape)
                then(pool.tensor_tensor(abt[:, 0], b_r, p_r, ALU.mult))
                then(pool.tensor_tensor(abt[:, 1], b_i, p_i, ALU.mult))
                if q:
                    pool.wait_ge(ab_turned, QS * q)
                then(pool.tensor_tensor(ab[:, 0], abt[:, 0], abt[:, 1], ALU.subtract))
                then(pool.tensor_tensor(abt[:, 0], b_r, p_i, ALU.mult))
                then(pool.tensor_tensor(abt[:, 1], b_i, p_r, ALU.mult))
                pool.tensor_tensor(ab[:, 1], abt[:, 0], abt[:, 1], ALU.add).then_inc(ab_ready, 1)
                pool.wait_ge(ab_ready, q + 1)

        @block.tensor
        def _(pe):
            pe.wait_ge(rexp_done, 1)
            for hf in range(2):
                pe.transpose(pst[:, hf], rexp[:, hf].rearrange("p s h -> p (s h)"), ident[:]).then_inc(r_turned, 1)
            for q in range(NS):
                pe.wait_ge(ca_ready, q + 1)
                if q >= 2:
                    pe.wait_ge(z_ready, q - 1)
                for jj in range(QS):
                    for ri in range(2):
                        last = pe.matmul(psz[q % 2][:, jj], bbd[:, ri, q * QS + jj].rearrange("p g h -> p (g h)"),
                                         cas[q % 2][:, ri, jj, 0:T].rearrange("p t h -> p (t h)"),
                                         start=(ri == 0), stop=(ri == 1))
                last.then_inc(z_mm, 1)
                pe.wait_ge(ab_ready, q + 1)
                for jj in range(QS):
                    j = q * QS + jj
                    if j >= 2:
                        pe.wait_ge(win_ready, j - 1)
                    for hf in range(2):
                        for ri in range(2):
                            last = pe.transpose(psw[j % 2][:, 2 * hf + ri],
                                                ab[:, ri, jj, hf * S8:(hf + 1) * S8].rearrange("p s h -> p (s h)"), ident[:])
                    last.then_inc(ab_turned, 1)


def s5_load(sp, d, q, mt, ca, ld_m, ld_c):
    for s in range(S8):
        lo = (S8 - 1 - s) * H
        sp.dma_start(mt[s * H:(s + 1) * H],
                     d["z"][0].rearrange("(g h) n -> h g n", h=H)[:, q * 2 * QP:(q + 1) * 2 * QP, lo:lo + T * H]).then_inc(ld_m, 16)
    sp.dma_start(ca[:].rearrange("p r j n -> p (r j n)"), d["ca"][:, q]).then_inc(ld_c, 16)


def s5_states(nc, env, d, ctx):
    sb, ps, sem = tools(nc, ctx)
    U, Win, aT, xs = env["U"], env["Win"], env["aT"], env["xs"]
    SC, SU = 8, NCH // 8
    t1 = sb("s5_t1", [P, 2, NP, SU])
    t2 = sb("s5_t2", [P, 2, NP, SU])
    ap = sb("s5_ap", [P, 2, NP, SU])
    ani = sb("s5_ani", [P, NP])
    psx = [ps(f"s5_psx{i}", [P, 2, 2, NCH]) for i in range(4)]
    ld_first = sem("s5_ld_first")
    x_mm, x_copied, chain, pchain = sem("s5_x_mm"), sem("s5_x_copied"), sem("s5_scan"), sem("s5_pool_scan")
    BY_DVE = 20
    ORDER = [*range(BY_DVE // 2, NP // 2), *range(BY_DVE // 2)]
    with nc.Block() as block:
        @block.sync
        def _(sp):
            s5_load(sp, d, 0, env["mt0"], env["ca0"], ld_first, ld_first)
            sp.wait_ge(ld_first, 16 * (S8 + 1))

        @block.tensor
        def _(pe):
            for i, j2 in enumerate(ORDER):
                if i >= 4:
                    pe.wait_ge(x_copied, i - 3)
                for jj in range(2):
                    j = 2 * j2 + jj
                    for g in range(2):
                        for ri in range(2):
                            for hf in range(2):
                                last = pe.matmul(psx[i % 4][g * 64:(g + 1) * 64, ri, jj],
                                                 Win[:, j, hf, ri, g * 64:(g + 1) * 64], U[:, hf, 2 * j + g],
                                                 start=(hf == 0), stop=(hf == 1))
                last.then_inc(x_mm, 1)

        @block.scalar
        def _(act):
            for i, j2 in enumerate(ORDER):
                act.wait_ge(x_mm, i + 1)
                act.copy(xs[:, :, 2 * j2:2 * j2 + 2, 1:NCH + 1], psx[i % 4][:]).then_inc(x_copied, 1)

        def scan(eng, chain, js, copied):
            n, pairs = [0], js.stop - js.start

            def then(ins):
                n[0] += 1
                ins.then_inc(chain, 1)
                eng.wait_ge(chain, n[0])

            def times(out, v, ar, ai, tmp):
                eng.tensor_tensor(out[0], v[0], ar, ALU.mult).then_inc(chain, 1)
                eng.tensor_tensor(out[1], v[1], ar, ALU.mult).then_inc(chain, 1)
                eng.tensor_tensor(tmp[0], v[1], ai, ALU.mult).then_inc(chain, 1)
                n[0] += 3
                then(eng.tensor_tensor(tmp[1], v[0], ai, ALU.mult))
                eng.tensor_tensor(out[0], out[0], tmp[0], ALU.subtract).then_inc(chain, 1)
                n[0] += 1
                then(eng.tensor_tensor(out[1], out[1], tmp[1], ALU.add))

            eng.memset(xs[:, :, js, 0:1], 0.0)
            then(eng.tensor_copy(ap[:, :, js, 0], aT[:, :, js]))
            m = 1
            while m < SU:
                shape = [P, pairs, m]
                times([ap[:, r, js, m:2 * m] for r in range(2)], [ap[:, r, js, 0:m] for r in range(2)],
                      ap[:, 0, js, m - 1:m].to_broadcast(shape), ap[:, 1, js, m - 1:m].to_broadcast(shape),
                      [t2[:, r, js, 0:m] for r in range(2)])
                m *= 2
            eng.wait_ge(x_copied, copied)
            view = [xs[:, r, js, 1:].rearrange("p j (c u) -> p j c u", u=SU) for r in range(2)]
            shape = [P, pairs, SC]
            ar, ai = (aT[:, r, js, None].to_broadcast(shape) for r in range(2))
            for u in range(1, SU):
                o = [t1[:, r, js, 0:SC] for r in range(2)]
                times(o, [view[r][:, :, :, u - 1] for r in range(2)], ar, ai, [t2[:, r, js, 0:SC] for r in range(2)])
                eng.tensor_tensor(view[0][:, :, :, u], view[0][:, :, :, u], o[0], ALU.add).then_inc(chain, 1)
                n[0] += 1
                then(eng.tensor_tensor(view[1][:, :, :, u], view[1][:, :, :, u], o[1], ALU.add))
            shape = [P, pairs, SU]
            for c in range(1, SC):
                o = [t1[:, r, js] for r in range(2)]
                v = [xs[:, r, js, c * SU:c * SU + 1].to_broadcast(shape) for r in range(2)]
                times(o, v, ap[:, 0, js], ap[:, 1, js], [t2[:, r, js] for r in range(2)])
                eng.tensor_tensor(view[0][:, :, c], view[0][:, :, c], o[0], ALU.add).then_inc(chain, 1)
                n[0] += 1
                then(eng.tensor_tensor(view[1][:, :, c], view[1][:, :, c], o[1], ALU.add))

        @block.vector
        def _(dve):
            scan(dve, chain, slice(0, BY_DVE), NP // 2)

        @block.gpsimd
        def _(pool):
            scan(pool, pchain, slice(BY_DVE, NP), (NP - BY_DVE) // 2)


def s5_outputs(nc, env, d, ctx):
    sb, ps, sem = tools(nc, ctx)
    U, xs, ident = env["U"], env["xs"], env["ident"]
    mt = [env["mt0"], sb("s5_mt1", [P, 2 * QP, T * H])]
    ca = [env["ca0"], sb("s5_ca_out1", [P, 2, QP, (T + 1) * H])]
    yc = sb("s5_yc", [P, 2, T, P])
    yh = sb("s5_yh", [P, 2, SEQ], F32R)
    yl = sb("s5_yl", [P, 2, SEQ], F32R)
    psy = [ps(f"s5_psy{i}", [P, 2, T * H]) for i in range(4)]
    psq = [ps(f"s5_psq{i}", [P, 4, NCH]) for i in range(4)]
    ld_m = [sem("s5_ld_m0"), sem("s5_ld_m1")]
    ld_c = [sem("s5_ld_c0"), sem("s5_ld_c1")]
    y_mm, gelu_done, y_turned, hi_done, lo_done = (sem("s5_" + x) for x in ("y_mm", "gelu_done", "y_turned", "hi_done", "lo_done"))
    st_y = [sem("s5_st_y0"), sem("s5_st_y1")]
    with nc.Block() as block:
        @block.sync
        def _(sp):
            def load(q):
                if q >= 2:
                    sp.wait_ge(y_mm, 2 * (q - 1))
                s5_load(sp, d, q, mt[q % 2], ca[q % 2], ld_m[q % 2], ld_c[q % 2])

            load(1)
            for q in range(NQ):
                if q + 2 < NQ:
                    load(q + 2)
                sp.wait_ge(hi_done, 4 * (q + 1))
                sp.dma_start(d["y_hi"][q], yh[:, q % 2].bitcast(F32)).then_inc(st_y[q % 2], 16)
                sp.wait_ge(lo_done, 4 * (q + 1))
                sp.dma_start(d["y_lo"][q], yl[:, q % 2].bitcast(F32)).then_inc(st_y[q % 2], 16)
            for i in range(2):
                sp.wait_ge(st_y[i], 32 * (NQ // 2))

        @block.tensor
        def _(pe):
            def outputs(q):
                if q:
                    pe.wait_ge(ld_m[q % 2], 16 * S8 * ((q + 1) // 2))
                    pe.wait_ge(ld_c[q % 2], 16 * ((q + 1) // 2))
                for pr in range(2):
                    if q:
                        pe.wait_ge(gelu_done, 4 * (q - 1) + 2 * pr + 2)
                    for jj in (2 * pr, 2 * pr + 1):
                        j = q * QP + jj
                        for g in range(2):
                            o, m = psy[2 * pr + g][:, jj % 2], mt[q % 2][:, 2 * jj + g]
                            rows = slice(g * 64, (g + 1) * 64)
                            pe.matmul(o, U[:, 0, 2 * j + g], m, start=True, stop=False)
                            pe.matmul(o[:, T * H // 2:], U[:, 1, 2 * j + g], m[:, 0:T * H // 2], start=False, stop=False)
                            for ri in range(2):
                                last = pe.matmul(o, xs[rows, ri, j, 0:NCH], ca[q % 2][rows, ri, jj, H:],
                                                 start=False, stop=(ri == 1))
                    last.then_inc(y_mm, 1)

            def turn(q):
                pe.wait_ge(gelu_done, 4 * (q + 1))
                for i in range(4):
                    if q:
                        pe.wait_ge(lo_done, 4 * (q - 1) + i + 1)
                    for t in range(4):
                        last = pe.transpose(psq[i][:, t], yc[:, q % 2, 4 * i + t], ident[:])
                    last.then_inc(y_turned, 1)

            for q in range(NQ + 1):
                if q < NQ:
                    outputs(q)
                if q:
                    turn(q - 1)

        @block.scalar
        def _(act):
            for q in range(NQ + 1):
                if q < NQ:
                    for pr in range(2):
                        act.wait_ge(y_mm, 2 * q + pr + 1)
                        if q >= 2:
                            act.wait_ge(y_turned, 4 * (q - 1))
                        for g in range(2):
                            act.activation(yc[:, q % 2].rearrange("p t (j g h) -> p j g t h", h=H, g=2)[:, 2 * pr:2 * pr + 2, g],
                                           psy[2 * pr + g][:].rearrange("p j (t h) -> p j t h", h=H),
                                           ACT.Gelu_apprx_tanh).then_inc(gelu_done, 1)
                if q:
                    r = q - 1
                    for i in range(4):
                        act.wait_ge(y_turned, 4 * r + i + 1)
                        if r >= 2:
                            act.wait_ge(st_y[r % 2], 32 * (r // 2))
                        act.copy(yh[:, r % 2].rearrange("p (c t) -> p t c", t=T)[:, 4 * i:4 * i + 4],
                                 psq[i][:]).then_inc(hi_done, 1)

        @block.vector
        def _(dve):
            for q in range(NQ):
                for i in range(4):
                    dve.wait_ge(hi_done, 4 * q + i + 1)
                    view = (slice(None), slice(4 * i, 4 * i + 4))
                    dve.tensor_tensor(yl[:, q % 2].rearrange("p (c t) -> p t c", t=T)[view], psq[i][:],
                                      yh[:, q % 2].rearrange("p (c t) -> p t c", t=T)[view].bitcast(F32),
                                      ALU.subtract).then_inc(lo_done, 1)


def constants(nc, env, ctx):
    sb, ps, sem = tools(nc, ctx)
    env["ident"] = ident = sb("ident", [P, P])
    env["eps"] = eps = sb("eps", [P, 1])
    env["halfpi"] = halfpi = sb("halfpi", [P, 1])
    made = sem("consts_made")
    with nc.Block() as block:
        @block.gpsimd
        def _(pool):
            pool.memset(ident[:], 0.0).then_inc(made, 1)
            pool.memset(eps[:], EPS)
            pool.memset(halfpi[:], TWO_PI / 4)
            pool.wait_ge(made, 1)
            pool.affine_select(out=ident[:], in_=ident[:], compare_op=ALU.not_equal, fill=1.0, base=0,
                               pattern=[[-1, P]], channel_multiplier=1)


def s5_stage(nc, env, d):
    with ExitStack() as stage:
        env["U"] = stage.enter_context(nc.sbuf_tensor("s5_U", [P, 2, 2 * NP, NCH], F32))
        env["aT"] = stage.enter_context(nc.sbuf_tensor("s5_aT", [P, 2, NP], F32))
        with ExitStack() as win:
            env["Win"] = win.enter_context(nc.sbuf_tensor("s5_Win", [P, NP, 2, 2, P], F32, side="right"))
            with ExitStack() as ctx:
                s5_setup(nc, env, d, ctx)
            env["xs"] = stage.enter_context(nc.sbuf_tensor("s5_xs", [P, 2, NP, NCH + 1], F32))
            env["mt0"] = stage.enter_context(nc.sbuf_tensor("s5_mt0", [P, 2 * QP, T * H], F32))
            env["ca0"] = stage.enter_context(nc.sbuf_tensor("s5_ca_out0", [P, 2, QP, (T + 1) * H], F32))
            with ExitStack() as ctx:
                s5_states(nc, env, d, ctx)
        with ExitStack() as ctx:
            s5_outputs(nc, env, d, ctx)


NB = 2
TB = SEQ // NB
KD = D // P
F_GROUPS, F_TILES = 8, 4
N_GLU, N_MLP, N_PLE, N_FM, N_TM = 2 * KD, F_GROUPS * 2 * F_TILES, KD + 2, 20, 14
TILE_MLP = N_GLU
TILE_PLE = TILE_MLP + N_MLP
TILE_FM = TILE_PLE + N_PLE
TILE_TM = TILE_FM + N_FM
N_TILE = TILE_TM + N_TM
JOB_STAT1 = N_GLU
JOB_MLP = JOB_STAT1 + 1
JOB_STAT2 = JOB_MLP + F_GROUPS * (F_TILES + KD)
JOB_PLE = JOB_STAT2 + 1
JOB_STAT3 = JOB_PLE + 2 * KD
JOB_FM = JOB_STAT3 + 2
JOB_GI = JOB_FM + N_FM
JOB_TM = JOB_GI + 2
TM_COLS = [256, 512, 512, 512]
TM_JOBS = [2, 4, 4, 4]
N_JOB = JOB_TM + sum(TM_JOBS)
N_COPY = N_JOB - JOB_FM
C_B, C_A, C_Z, A_Z, M_QK, A_QK = (slice(*v) for v in ((0, 2), (2, 4), (4, 6), (6, 8), (8, 16), (16, 20)))
GI_AT, TM_AT = N_FM, N_FM + 2
KINDS = ["c_b"] * 2 + ["c_a"] * 2 + ["silu"] * 4 + ["conv"] * 8 + ["copy"] * 4 + ["gi"] * 2
KINDS += ["tm"] * (TM_JOBS[0] + TM_JOBS[1]) + ["tm_sigmoid"] * TM_JOBS[2] + ["tm_silu"] * TM_JOBS[3]
BY_ACT = [k in ("c_b", "silu", "tm_sigmoid", "tm_silu") for k in KINDS]
before = lambda j, by_act: sum(b == by_act for b in BY_ACT[:j])
N_BY_ACT, N_BY_DVE = before(N_COPY, True), before(N_COPY, False)
FIRST_V = 4
N_STORE = (N_COPY - FIRST_V) // 2
M_TAPS, C_TAPS = 4, 31
N_TAP = 2 * C_TAPS
MC_INC = M_TAPS + 1
TAPS_AT = {j: 3 for j in range(4, 8)} | {j: 2 for j in range(8, 16)} | {j: 3 for j in range(16, N_COPY)}
assert len(KINDS) == N_COPY and sum(TAPS_AT.values()) >= N_TAP
N_XADD = KD + KD * F_GROUPS + KD
assert N_TILE % 2 == 0 and N_JOB % 4 == 0


def dense(nc, env, d, ctx):
    sb, ps, sem = tools(nc, ctx)
    ident, eps = env["ident"], env["eps"]
    halves = lambda v: v.rearrange("p (a b) -> p a b", a=2)
    X = sb("X", [P, KD, TB])
    x_at = nc.sbuf_base - KD * TB * 4
    Tt = sb("Tt", [P, KD, TB])
    t_at = nc.sbuf_base - KD * TB * 4
    AH, AL = sb("AH", [P, KD, TB], F32R), sb("AL", [P, KD, TB], F32R)
    FH, FL = sb("FH", [P, F_TILES, TB], F32R), sb("FL", [P, F_TILES, TB], F32R)
    SQ0 = nc.alloc_sbuf_tensor_at("SQ0", [P, 2, TB], F32, offset=nc.sbuf_base - 2 * F_TILES * TB * 4)
    WR = [sb(f"WR{i}", [P, TB]) for i in range(2)]
    WH = [sb(f"WH{i}", [P, TB], F32R) for i in range(2)]
    WL = [sb(f"WL{i}", [P, TB], F32R) for i in range(2)]
    SG = [sb(f"SG{i}", [P, 2, TB // 2]) for i in range(2)]
    V = [sb(f"V{i}", [P, 2, TB // 2]) for i in range(2)]
    RB = sb("RB", [P, TB])
    ones = sb("ones_d", [P, P])
    cv_n, cu_n = 2 * TB * 4, -(-2 * (C_TAPS - 1 + TB) * 4 // 32) * 32
    CV = nc.alloc_sbuf_tensor_at("CV", [P, 2, TB], F32, offset=x_at)
    CU = nc.alloc_sbuf_tensor_at("CU", [P, 2, C_TAPS - 1 + TB], F32, offset=x_at + cv_n)
    MX = nc.alloc_sbuf_tensor_at("MX", [P, 2, M_TAPS - 1 + TB], F32, offset=x_at + cv_n + cu_n)
    RB1, RB2 = Tt[:, KD - 2], Tt[:, KD - 1]
    square_at = lambda n: halves(SQ0[:, n % 2]) if n < 8 else V[n % 2][:] if n < 16 else halves(Tt[:, 2 + n % 2])
    ple = lambda F, m: (lambda k: F[:, 2 + m // 4, (2 * (m % 4) + k) * P:(2 * (m % 4) + k + 1) * P])
    cu_tail, mx_tail = sb("cu_tail", [P, 2, C_TAPS - 1]), sb("mx_tail", [P, 8, M_TAPS - 1])
    m_w, m_b = sb("d_mw", [P, 8, M_TAPS]), sb("d_mb", [P, 8])
    c_w, c_b = sb("d_cw", [P, 2, C_TAPS]), sb("d_cb", [P, 2])
    gains = sb("gains", [P, 4, KD])
    gwr = sb("gwr", [P, KD, 8])
    gwh, gwl = sb("gwh", [P, KD, 8], F32R), sb("gwl", [P, KD, 8], F32R)
    GH = [FH[:].rearrange("p a b -> p (a b)").rearrange("p (k n) -> p k n", k=KD), None]
    GL = [FL[:].rearrange("p a b -> p (a b)").rearrange("p (k n) -> p k n", k=KD), None]
    GH[1] = nc.alloc_sbuf_tensor_at("TH", [P, KD, 512], F32R, offset=t_at)[:]
    GL[1] = nc.alloc_sbuf_tensor_at("TL", [P, KD, 512], F32R, offset=t_at + KD * 512 * 4)[:]
    ps4 = [ps(f"ps_job{i}", [P, 2, TB // 2]) for i in range(4)]

    raw_loaded = [sem("raw_loaded0"), sem("raw_loaded1")]
    hi_done, raw_free = sem("w_hi_done"), sem("w_raw_free")
    job_done, sg_done, mix_done, xadd = sem("job_done"), sem("sg_done"), sem("mix_done"), sem("x_added")
    sq_done, acc_done, ln_done, r_done = sem("sq_done"), sem("acc_done"), sem("ln_done"), sem("r_done")
    t_done, ah_done, al_done, xfin = sem("t_done"), sem("ah_done"), sem("al_done"), sem("x_final")
    relu_done, v_done, fh_done, fl_done = sem("relu_done"), sem("v_done"), sem("fh_done"), sem("fl_done")
    ld_x, ld_y, ld_p, ld_g = sem("ld_x"), [sem("ld_y0"), sem("ld_y1")], sem("ld_p"), sem("ld_gains")
    ph_done, pl_done, gh_done, gl_done, ones_set = sem("ph_done"), sem("pl_done"), sem("gh_done"), sem("gl_done"), sem("ones_set")
    gsc_done, rr_done, ms_done = sem("gsc_done"), sem("rr_done"), sem("ms_done")
    x_stored, gated, conv_out, silu_out = sem("x_stored"), sem("gated"), sem("conv_out"), sem("silu_out")
    mc, tap, cu_done, cu_free, ld_c, st_c, tails_set = (sem(n) for n in ("mc", "tap", "cu_done", "cu_free", "ld_c", "st_c", "tails_set"))
    copied, st_out, st_x = sem("copied"), [sem("st_out0"), sem("st_out1")], sem("st_x")

    with nc.Block() as block:
        @block.sync
        def _(sp):
            sp.dma_start(gains[:], d["gains"]).then_inc(ld_g, 16)
            sp.dma_start(gwr[:], d["w_gi"]).then_inc(ld_g, 16)
            for v, name in ((m_w, "ml_cw"), (m_b, "ml_cb"), (c_w, "cv_w"), (c_b, "cv_b")):
                sp.dma_start(v[:], d[name]).then_inc(ld_c, 16)

            def load(w, tile, s, n):
                free, at = (w + 1, tile) if n == 0 else (sp.snap(w + 1), sp.snap(tile, min_val=0, max_val=N_TILE - 1))
                sp.wait_ge(raw_free, free)
                tile = bass.ds(at, 1)
                sp.dma_start(WR[s][:], d["wall"][tile].rearrange("o p n -> p (o n)")).then_inc(raw_loaded[s], 16)

            for s in range(2):
                load(s, s, s, 0)
            with sp.Fori(0, NB) as tb:
                tok = sp.snap(tb * TB, min_val=0, max_val=SEQ - TB)
                for n in range(2):
                    for a, name in ((AH, "y_hi"), (AL, "y_lo")):
                        src = d[name][:, :, bass.ds(sp.snap(tok + n * (TB // 2), min_val=0, max_val=SEQ - TB // 2), TB // 2)]
                        sp.dma_start(a[:, :, n * (TB // 2):(n + 1) * (TB // 2)].bitcast(F32),
                                     src.rearrange("k p n -> p k n")).then_inc(ld_y[n], 16)
                    sp.wait_ge(ld_y[n], 32 * tb + 32)
                    sp.sem_inc(x_stored, 1)
                sp.dma_start(X[:], d["x_feat"][:, :, bass.ds(tok, TB)].rearrange("k p n -> p k n")).then_inc(ld_x, 16)
                with sp.Fori(1, TILE_PLE // 2 + 1) as i:
                    for s in range(2):
                        load(tb * N_TILE + 2 * i + s, 2 * i + s, s, 1)
                sp.wait_ge(al_done, 24 * tb + 16)
                sp.dma_start(Tt[:, 0:2], d["p_feat"][:, :, bass.ds(tok, TB)].rearrange("k p n -> p k n")).then_inc(ld_p, 16)
                with sp.Fori(TILE_PLE // 2 + 1, N_TILE // 2) as i:
                    for s in range(2):
                        load(tb * N_TILE + 2 * i + s, 2 * i + s, s, 1)
                for s in range(2):
                    load(tb * N_TILE + N_TILE + s, s, s, 0)
                sp.wait_ge(st_x, 16 * tb + 16)
                sp.sem_inc(x_stored, 1)
                sp.wait_ge(st_c, 16 * tb + 16)
                sp.sem_inc(x_stored, 1)
                sp.wait_ge(cu_free, tb + 1)
                sp.sem_inc(x_stored, 1)
                sp.wait_ge(t_done, 24 * tb + 24)
                sp.sem_inc(x_stored, 1)
                sp.wait_ge(job_done, N_JOB * tb + N_JOB)
                sp.sem_inc(x_stored, 1)

        @block.scalar
        def _(act):
            act.sem_inc(sg_done, 2)
            act.sem_inc(gated, 1)
            act.sem_inc(fh_done, 2)
            for s in range(2):
                act.sem_inc(st_out[s], 16)

            def hi(w2, s, dst):
                act.wait_ge(raw_loaded[s], 16 * w2 + 16)
                act.copy(dst, WR[s][:]).then_inc(hi_done, 1)

            def whi(w2, s):
                hi(w2, s, WH[s][:])

            act.wait_ge(ld_g, 32)
            act.copy(gwh[:], gwr[:]).then_inc(gh_done, 1)
            for s in range(2):
                whi(0, s)
            with act.Fori(0, NB) as tb:
                job0, w0 = tb * N_JOB, tb * (N_TILE // 2)

                def gates(b):
                    for j in range(4):
                        act.wait_ge(job_done, job0 + (1 + j) + 4 * b)
                        if j % 2 == 0:
                            act.wait_ge(mix_done, 16 * tb + 2 * b + (j // 2 + 1))
                            act.activation(SG[j // 2][:], ps4[j][:], ACT.Sigmoid).then_inc(sg_done, 1)
                        whi(w0 + 2 * b + (j // 2 + 1), j % 2)

                def ple_gate(m):
                    act.wait_ge(job_done, job0 + (JOB_PLE + 2 * m + 1))
                    whi(w0 + (TILE_PLE + 4 + m) // 2, m % 2)
                    act.wait_ge(gsc_done, 8 * tb + (m + 3))
                    act.activation(SG[m % 2][:], SG[m % 2][:], ACT.Sigmoid).then_inc(sg_done, 1)

                def squares(n, k, count, gain=None):
                    act.wait_ge(xadd, N_XADD * tb + (2 + count))
                    if n % 8 >= 2 or n > 17:
                        act.wait_ge(acc_done, 32 * tb + (n - 1))
                    scale = {} if gain is None else {"scale": gain}
                    act.activation(square_at(n), halves(X[:, k]), ACT.Square, **scale).then_inc(sq_done, 1)

                def inverse_rms(job, n, out):
                    act.wait_ge(job_done, job0 + (job + 1))
                    act.activation(SG[0][:], ps4[job % 4][:], ACT.Ln, bias=eps[:]).then_inc(ln_done, 1)
                    act.wait_ge(ln_done, 4 * tb + n)
                    act.activation(out, SG[0][:], ACT.Exp, scale=-0.5).then_inc(r_done, 1)

                def hi_part(i, k):
                    act.wait_ge(t_done, 24 * tb + (8 * i + k + 1))
                    act.copy(AH[:, k], Tt[:, k]).then_inc(ah_done, 1)

                def last_squares(k):
                    for n, gain in ((16 + 2 * k, None), (17 + 2 * k, gains[:, 2, k:k + 1])):
                        squares(n, k, KD + KD * F_GROUPS + k + 1, gain)

                def last_norms():
                    inverse_rms(JOB_STAT3, 3, SG[1][:])
                    act.wait_ge(ms_done, tb + 1)
                    act.activation(V[1][:], V[0][:], ACT.Ln, bias=eps[:]).then_inc(ln_done, 1)
                    act.wait_ge(ln_done, 4 * tb + 4)
                    act.activation(V[1][:], V[1][:], ACT.Exp, scale=-0.5).then_inc(r_done, 1)

                def split(i):
                    for k in range(KD):
                        hi_part(i, k)

                with act.Fori(0, N_GLU // 4 - 1) as b:
                    gates(b)
                for k in range(KD - 2):
                    squares(k, k, k + 1)
                gates(N_GLU // 4 - 1)
                act.preload_act_table_set("natural_log_exp_and_others")
                for k in range(KD - 2, KD):
                    squares(k, k, k + 1)
                act.wait_ge(job_done, job0 + N_GLU)
                split(0)
                inverse_rms(JOB_STAT1, 1, halves(RB[:]))

                def group(fg, last):
                    w1 = w0 + fg * F_TILES + TILE_MLP // 2
                    for f in range(F_TILES):
                        n = 32 * tb + 4 * fg + f
                        act.wait_ge(job_done, job0 + fg * (F_TILES + KD) + (JOB_MLP + f + 1))
                        whi(w1 + (f // 2 + 1), f % 2)
                        act.wait_ge(relu_done, n + 1)
                        act.activation(halves(FH[:, f]), SG[f % 2][:], ACT.Square).then_inc(fh_done, 1)
                    if last:
                        act.wait_ge(fl_done, 32 * tb + (4 * F_GROUPS + 2))
                    for m2 in range(F_TILES):
                        act.wait_ge(job_done, job0 + fg * (F_TILES + KD) + (JOB_MLP + F_TILES + 2 * m2 + 2))
                        whi(w1 + (F_TILES + m2) // 2 + 1, m2 % 2)
                        for k in (2 * m2, 2 * m2 + 1) if last else ():
                            squares(8 + k, k, KD * F_GROUPS + k + 1)
                            hi_part(1, k)

                with act.Fori(0, F_GROUPS - 1) as fg:
                    group(fg, False)
                group(F_GROUPS - 1, True)
                for i in range(2):
                    hi(w0 + (TILE_PLE + 2) // 2, i, FH[:, 2 + i])
                act.preload_act_table_set("natural_log_exp_and_others")
                inverse_rms(JOB_STAT2, 2, halves(RB[:]))
                act.wait_ge(ld_p, 16 * tb + 16)
                for k in range(2):
                    act.copy(FH[:, k], Tt[:, k]).then_inc(ph_done, 1)
                act.wait_ge(al_done, 24 * tb + 16)
                for m in range(KD):
                    ple_gate(m)
                    if m:
                        last_squares(m - 1)
                act.preload_act_table_set("natural_log_exp_and_others")
                last_squares(KD - 1)
                last_norms()
                split(2)
                act.wait_ge(xfin, 8 * tb + 8)
                act.dma_start(d["x2"][:, :, bass.ds(tb * TB, TB)].rearrange("k p n -> p k n"), X[:]).then_inc(st_x, 16)

                tok = bass.ds(tb * TB, TB)
                flat = lambda v: v.rearrange("p a b -> p (a b)")

                def ghi(i):
                    g = 0 if i < 2 else (i + 2) // 4
                    c = (i if i < 2 else (i - 2) % 4) * P
                    hi(w0 + (TILE_TM + i) // 2, i % 2, GH[g % 2][:, :, c:c + P])

                def take(j):
                    src, fn = ps4[(JOB_FM + j) % 4][:], ACT.Sigmoid if KINDS[j] in ("c_b", "tm_sigmoid") else ACT.Silu
                    if BY_ACT[j]:
                        act.wait_ge(job_done, job0 + (JOB_FM + j + 1))
                        if KINDS[j] == "c_b":
                            act.wait_ge(xfin, 8 * tb + 8)
                            act.wait_ge(t_done, 24 * tb + 24)
                            act.activation(SG[j][:], src, fn).then_inc(gated, 1)
                        else:
                            act.wait_ge(st_out[j % 2], 16 * N_STORE * tb + 16 * ((j - FIRST_V) // 2 + 1))
                            act.activation(V[j % 2][:], src, fn).then_inc(gated, 1)

                def store(j):
                    v = V[j % 2]
                    if BY_ACT[j]:
                        act.wait_ge(gated, N_BY_ACT * tb + (before(j, True) + 2))
                    elif KINDS[j] == "conv":
                        i = j - M_QK.start
                        act.wait_ge(conv_out, 8 * tb + (i + 2))
                        act.activation(v[:], v[:], ACT.Silu).then_inc(silu_out, 1)
                        act.wait_ge(silu_out, 8 * tb + (i + 1))
                    else:
                        act.wait_ge(copied, N_BY_DVE * tb + (before(j, False) + 1 + 4))
                    if j < N_FM:
                        dst, src = d["fm"][j, :, tok], flat(v[:])
                    elif KINDS[j] == "gi":
                        n = j - GI_AT
                        dst, src = d["gi"][:, bass.ds(tb * TB + n * (TB // 2), TB // 2)], v[0:8, 0]
                    else:
                        g = [i for i in range(4) if TM_AT + sum(TM_JOBS[:i]) <= j][-1]
                        n = j - TM_AT - sum(TM_JOBS[:g])
                        per = TB // TM_JOBS[g]
                        dst = d["tm"][bass.ds(tb * TB + n * per, per), sum(TM_COLS[:g]):sum(TM_COLS[:g + 1])]
                        dst = dst.rearrange("(t p) n -> p t n", p=P)
                        src = flat(v[:]).rearrange("p (t n) -> p t n", n=TM_COLS[g])
                    act.dma_start(dst, src).then_inc(st_out[j % 2], 16)

                for j in range(N_COPY):
                    if j < N_FM:
                        act.wait_ge(job_done, job0 + (JOB_FM + j + 1))
                        if j < N_FM - 2:
                            whi(w0 + (TILE_FM + j + 2) // 2, j % 2)
                        else:
                            ghi(j - (N_FM - 2))
                    for g in range(3):
                        if j == TM_AT + sum(TM_JOBS[:g]):
                            act.wait_ge(job_done, job0 + (JOB_FM + j))
                            for i in range(2 + 4 * g, 6 + 4 * g):
                                ghi(i)
                    take(j)
                    if j > FIRST_V:
                        store(j - 1)
                store(N_COPY - 1)
                act.wait_ge(tap, N_TAP * tb + N_TAP)
                act.dma_start(d["cva"][:, :, tok].rearrange("k p n -> p k n"), CV[:]).then_inc(st_c, 16)
                for s in range(2):
                    whi(w0 + N_TILE // 2, s)
            act.wait_ge(st_x, 16 * NB)
            act.wait_ge(st_c, 16 * NB)
            for s in range(2):
                act.wait_ge(st_out[s], 16 * NB * N_STORE + 16)

        @block.gpsimd
        def _(pool):
            pool.memset(ones[:], 1.0 / D).then_inc(ones_set, 1)
            pool.sem_inc(raw_free, 2)
            pool.sem_inc(fl_done, 2)
            pool.wait_ge(gh_done, 1)
            pool.tensor_tensor(gwl[:], gwr[:], gwh[:].bitcast(F32), ALU.subtract).then_inc(gl_done, 1)

            def lo(w, s, dst, src, raw):
                pool.wait_ge(hi_done, w + 1)
                pool.tensor_tensor(dst, raw, src.bitcast(F32), ALU.subtract).then_inc(raw_free, 1)

            def wlo(w, s):
                lo(w, s, WL[s][:], WH[s][:], WR[s][:])

            for s in range(2):
                wlo(s, s)
            with pool.Fori(0, NB) as tb:
                w0 = tb * N_TILE

                def split(i):
                    for k in range(KD):
                        pool.wait_ge(ah_done, 24 * tb + (8 * i + k + 1))
                        pool.tensor_tensor(AL[:, k], Tt[:, k], AH[:, k].bitcast(F32), ALU.subtract).then_inc(al_done, 1)

                with pool.Fori(0, N_GLU // 2) as b:
                    for s in range(2):
                        wlo(w0 + 2 * b + (s + 2), s)
                split(0)
                with pool.Fori(0, F_GROUPS) as fg:
                    w1 = w0 + fg * (2 * F_TILES) + TILE_MLP
                    for f in range(F_TILES):
                        wlo(w1 + (f + 2), f % 2)
                        pool.wait_ge(fh_done, 32 * tb + 4 * fg + (f + 3))
                        pool.wait_ge(v_done, 32 * tb + 4 * fg + (f + 3))
                        pool.tensor_tensor(halves(FL[:, f]), V[f % 2][:], halves(FH[:, f]).bitcast(F32), ALU.subtract).then_inc(fl_done, 1)
                    for m2 in range(F_TILES):
                        wlo(w1 + (F_TILES + m2 + 2), m2 % 2)
                split(1)
                for i in range(2):
                    lo(w0 + (TILE_PLE + 2 + i), i, FL[:, 2 + i], FH[:, 2 + i], WR[i][:])
                for k in range(2):
                    pool.wait_ge(ph_done, 2 * tb + k + 1)
                    pool.tensor_tensor(FL[:, k], Tt[:, k], FH[:, k].bitcast(F32), ALU.subtract).then_inc(pl_done, 1)
                with pool.Fori(0, KD // 2) as b:
                    for s in range(2):
                        wlo(w0 + 2 * b + (TILE_PLE + 4 + s), s)
                split(2)
                with pool.Fori(0, N_FM // 2 - 1) as b:
                    for s in range(2):
                        wlo(w0 + 2 * b + (TILE_FM + s + 2), s)
                for i in range(N_TM):
                    g = 0 if i < 2 else (i + 2) // 4
                    c = (i if i < 2 else (i - 2) % 4) * P
                    lo(w0 + (TILE_TM + i), i % 2, GL[g % 2][:, :, c:c + P], GH[g % 2][:, :, c:c + P],
                       WR[i % 2][:].rearrange("p (k n) -> p k n", k=KD))
                for s in range(2):
                    wlo(w0 + (N_TILE + s), s)

        @block.vector
        def _(dve):
            dve.memset(V[0][:, 0, 0:1], 0.0).then_inc(mix_done, 2)
            dve.memset(V[0][:, 0, 1:2], 0.0).then_inc(xadd, 2)
            dve.sem_inc(gsc_done, 2)
            dve.sem_inc(v_done, 2)
            dve.memset(V[0][:, 0, 3:4], 0.0).then_inc(copied, 4)
            dve.wait_ge(copied, 4)
            dve.memset(cu_tail[:], 0.0).then_inc(tails_set, 1)
            dve.memset(mx_tail[:], 0.0).then_inc(mc, 1)
            dve.sem_inc(conv_out, 1)
            dve.wait_ge(tails_set, 1)
            dve.wait_ge(ld_c, 64)
            dve.wait_ge(ld_g, 32)
            dve.tensor_tensor(gains[:, 3], gains[:, 2], gains[:, 3], ALU.mult).then_inc(tails_set, 1)
            dve.wait_ge(tails_set, 2)
            with dve.Fori(0, NB) as tb:
                job0 = tb * N_JOB

                def mix(job, base, m, s):
                    dve.wait_ge(sg_done, 16 * tb + base + m + 3)
                    dve.wait_ge(job_done, job0 + 2 * m + (job + 2))
                    dve.wait_ge(xadd, N_XADD * tb + m + (1 + (KD * F_GROUPS + KD if base else 0)))
                    if base == 0:
                        dve.wait_ge(st_out[s], 16 * N_STORE * tb + 16)
                    dve.tensor_tensor(V[s][:], ps4[(job + 2 * s + 1) % 4][:], SG[s][:], ALU.mult).then_inc(mix_done, 1)
                    dve.wait_ge(mix_done, 16 * tb + base + m + 3)
                    xm = X[:, bass.ds(m, 1), :].rearrange("p o (a n) -> p (o a) n", a=2)
                    dve.tensor_tensor(xm, xm, V[s][:], ALU.add).then_inc(xadd, 1)

                def scale_gate(m):
                    dve.wait_ge(r_done, 4 * tb + 2)
                    dve.wait_ge(job_done, job0 + (JOB_PLE + 2 * m + 1))
                    dve.wait_ge(mix_done, 16 * tb + (KD + m + 1))
                    dve.tensor_tensor(SG[m % 2][:], ps4[(JOB_PLE + 2 * m) % 4][:], halves(RB[:]), ALU.mult).then_inc(gsc_done, 1)

                def add_up(n, acc):
                    dve.wait_ge(sq_done, 32 * tb + (n + 1))
                    first = n % 8 == 0 if n < 16 else n < 18
                    if first:
                        dve.tensor_copy(acc, square_at(n)).then_inc(acc_done, 1)
                    else:
                        dve.wait_ge(acc_done, 32 * tb + n)
                        dve.tensor_tensor(acc, acc, square_at(n), ALU.add).then_inc(acc_done, 1)

                def gained(i, count, k):
                    dve.wait_ge(xadd, N_XADD * tb + (2 + count + k + 1))
                    dve.tensor_scalar(Tt[:, k], X[:, k], gains[:, i, k:k + 1], None, ALU.mult).then_inc(t_done, 1)

                def last_sums(k):
                    for n, acc in ((16 + 2 * k, RB1), (17 + 2 * k, RB2)):
                        add_up(n, halves(acc))

                def last_norms():
                    dve.wait_ge(r_done, 4 * tb + 3)
                    dve.wait_ge(acc_done, 32 * tb + 32)
                    dve.tensor_tensor(V[0][:], SG[1][:], SG[1][:], ALU.mult).then_inc(rr_done, 1)
                    dve.wait_ge(rr_done, 2 * tb + 1)
                    dve.wait_ge(job_done, job0 + (JOB_STAT3 + 2))
                    dve.tensor_tensor(V[0][:], ps4[(JOB_STAT3 + 1) % 4][:], V[0][:], ALU.mult).then_inc(ms_done, 1)
                    dve.wait_ge(r_done, 4 * tb + 4)
                    dve.wait_ge(ms_done, tb + 1)
                    dve.tensor_tensor(V[0][:], V[1][:], SG[1][:], ALU.mult).then_inc(rr_done, 1)
                    dve.wait_ge(rr_done, 2 * tb + 2)
                    for k in range(KD):
                        dve.scalar_tensor_tensor(halves(Tt[:, k]), halves(X[:, k]), gains[:, 3, k:k + 1], V[0][:],
                                                 ALU.mult, ALU.mult).then_inc(t_done, 1)
                    for k in range(KD):
                        dve.wait_ge(t_done, 24 * tb + (16 + k + 1))
                        dve.scalar_tensor_tensor(halves(X[:, k]), halves(X[:, k]), gains[:, 2, k:k + 1], SG[1][:],
                                                 ALU.mult, ALU.mult).then_inc(xfin, 1)

                with dve.Fori(0, N_GLU // 4 - 1) as b:
                    dve.wait_ge(ld_x, 16 * tb + 16)
                    for s in range(2):
                        mix(0, 0, 2 * b + s, s)
                for k in range(KD - 2):
                    gained(0, 0, k)
                    add_up(k, halves(RB[:]))
                for k in range(KD - 2, KD):
                    mix(0, 0, k, k % 2)
                for k in range(KD - 2, KD):
                    gained(0, 0, k)
                    add_up(k, halves(RB[:]))

                def group(fg, last):
                    for f in range(F_TILES):
                        n = 32 * tb + 4 * fg + f
                        dve.wait_ge(r_done, 4 * tb + 1)
                        dve.wait_ge(job_done, job0 + fg * (F_TILES + KD) + (JOB_MLP + f + 1))
                        dve.wait_ge(fh_done, n + 1)
                        dve.wait_ge(v_done, n + 1)
                        dve.scalar_tensor_tensor(SG[f % 2][:], ps4[(JOB_MLP + f) % 4][:], 0.0, halves(RB[:]),
                                                 ALU.max, ALU.mult).then_inc(relu_done, 1)
                        dve.wait_ge(relu_done, n + 1)
                        dve.wait_ge(fl_done, n + 1)
                        dve.tensor_tensor(V[f % 2][:], SG[f % 2][:], SG[f % 2][:], ALU.mult).then_inc(v_done, 1)
                    if last:
                        dve.wait_ge(al_done, 24 * tb + 8)
                    for m in range(KD):
                        dve.wait_ge(job_done, job0 + fg * (F_TILES + KD) + (JOB_MLP + F_TILES + m + 1))
                        xm = halves(X[:, m])
                        dve.tensor_tensor(xm, xm, ps4[(JOB_MLP + F_TILES + m) % 4][:], ALU.add).then_inc(xadd, 1)
                        if last:
                            gained(1, KD * F_GROUPS, m)
                            add_up(8 + m, halves(RB[:]))

                with dve.Fori(0, F_GROUPS - 1) as fg:
                    group(fg, False)
                group(F_GROUPS - 1, True)
                for m in range(KD):
                    scale_gate(m)
                    if m:
                        last_sums(m - 1)
                    mix(JOB_PLE, KD, m, m % 2)
                last_sums(KD - 1)
                last_norms()

                def slot_free(j):
                    dve.wait_ge(st_out[j % 2], 16 * N_STORE * tb + 16 * ((j - FIRST_V) // 2 + 1))

                def convolve(j, i):
                    x, out, m0 = MX[:, i % 2], V[j % 2], MC_INC * 8 * tb + MC_INC * i + 1
                    tail = slice(TB, TB + M_TAPS - 1)
                    dve.wait_ge(mc, m0)
                    dve.wait_ge(conv_out, 8 * tb + (i + 1))
                    dve.tensor_copy(halves(x[:, M_TAPS - 1:]), ps4[(JOB_FM + j) % 4][:]).then_inc(copied, 1)
                    dve.tensor_copy(x[:, 0:M_TAPS - 1], mx_tail[:, i]).then_inc(mc, 1)
                    dve.wait_ge(copied, N_BY_DVE * tb + (before(j, False) + 1 + 4))
                    slot_free(j)
                    for k in range(M_TAPS):
                        xk = halves(x[:, k:k + TB])
                        dve.wait_ge(mc, m0 + (k + 1))
                        if k == 0:
                            step = dve.tensor_scalar(out[:], xk, m_w[:, i, 0:1], m_b[:, i:i + 1], ALU.mult, ALU.add)
                        else:
                            step = dve.scalar_tensor_tensor(out[:], xk, m_w[:, i, k:k + 1], out[:], ALU.mult, ALU.add)
                        step.then_inc(conv_out if k == M_TAPS - 1 else mc, 1)
                    dve.tensor_copy(mx_tail[:, i], x[:, tail]).then_inc(mc, 1)

                def add_tap(n):
                    k, t = n // 2, n % 2
                    xk = CU[:, t, k:k + TB]
                    if k == 0:
                        dve.wait_ge(cu_done, 4 * tb + (3 + t))
                        step = dve.tensor_scalar(CV[:, t], xk, c_w[:, t, 0:1], c_b[:, t:t + 1], ALU.mult, ALU.add)
                    else:
                        dve.wait_ge(tap, N_TAP * tb + (n - 1))
                        step = dve.scalar_tensor_tensor(CV[:, t], xk, c_w[:, t, k:k + 1], CV[:, t], ALU.mult, ALU.add)
                    step.then_inc(tap, 1)

                taps = 0
                dve.wait_ge(st_x, 16 * tb + 16)
                dve.wait_ge(t_done, 24 * tb + 24)
                for t in range(2):
                    dve.tensor_copy(CU[:, t, 0:C_TAPS - 1], cu_tail[:, t]).then_inc(cu_done, 1)
                for j in range(N_COPY):
                    if not BY_ACT[j]:
                        dve.wait_ge(job_done, job0 + (JOB_FM + j + 1))
                    src = ps4[(JOB_FM + j) % 4]
                    if KINDS[j] == "c_a":
                        t = j - C_A.start
                        dve.wait_ge(gated, N_BY_ACT * tb + (t + 2))
                        dve.tensor_tensor(halves(CU[:, t, C_TAPS - 1:]), src[:], SG[t][:], ALU.mult).then_inc(copied, 1)
                        dve.wait_ge(copied, N_BY_DVE * tb + (before(j, False) + 1 + 4))
                        dve.sem_inc(cu_done, 1)
                    elif KINDS[j] == "conv":
                        convolve(j, j - M_QK.start)
                    elif KINDS[j] == "gi":
                        slot_free(j)
                        dve.tensor_copy(V[j % 2][0:8, 0], src[0:8, 0]).then_inc(copied, 1)
                    elif not BY_ACT[j]:
                        slot_free(j)
                        dve.tensor_copy(V[j % 2][:], src[:]).then_inc(copied, 1)
                    for n in range(taps, min(taps + TAPS_AT.get(j, 0), N_TAP)):
                        add_tap(n)
                        taps += 1
                dve.wait_ge(tap, N_TAP * tb + N_TAP)
                dve.tensor_copy(cu_tail[:], CU[:, :, TB:]).then_inc(cu_free, 1)

        @block.tensor
        def _(pe):
            def product(out, k_tiles, passes, wait=None):
                for k in range(k_tiles):
                    if wait:
                        wait(k)
                    for i, (l, r) in enumerate(passes(k)):
                        last = pe.matmul(out, l, r, start=(k == 0 and i == 0), stop=(k == k_tiles - 1 and i == 2))
                return last

            def job_by_parts(slot, k_tiles, wh, wl, ah, al, wait):
                for ks in (range(k_tiles - 1), (k_tiles - 1,)):
                    for n in range(2):
                        t = slice(n * (TB // 2), (n + 1) * (TB // 2))
                        for k in ks:
                            if n == 0:
                                wait(k)
                            for i, (l, r) in enumerate(((wh(k), ah[:, k, t]), (wh(k), al[:, k, t]), (wl(k), ah[:, k, t]))):
                                last = pe.matmul(ps4[slot][:, n], l, r, start=(k == 0 and i == 0),
                                                 stop=(k == k_tiles - 1 and i == 2))
                last.then_inc(job_done, 1)

            def job(slot, k_tiles, wh, wl, ah, al, wait=None, wait_half=None):
                for n in range(2):
                    if wait_half:
                        wait_half(n)
                    t = slice(n * (TB // 2), (n + 1) * (TB // 2))
                    last = product(ps4[slot][:, n], k_tiles,
                                   lambda k: ((wh(k), ah[:, k, t]), (wh(k), al[:, k, t]), (wl(k), ah[:, k, t])),
                                   wait if n == 0 else None)
                last.then_inc(job_done, 1)

            def tile(s, at=0):
                return (lambda k: WH[s][:, (at + k) * P:(at + k + 1) * P]), (lambda k: WL[s][:, (at + k) * P:(at + k + 1) * P])

            def stat(slot, count, acc=RB[:]):
                pe.wait_ge(acc_done, count)
                for n in range(2):
                    last = pe.matmul(ps4[slot][:, n], ones[:], acc[:, n * (TB // 2):(n + 1) * (TB // 2)], start=True, stop=True)
                last.then_inc(job_done, 1)

            pe.wait_ge(ones_set, 1)
            with pe.Fori(0, NB) as tb:
                w0 = tb * N_TILE
                with pe.Fori(0, N_GLU // 4) as b:
                    pe.wait_ge(copied, N_BY_DVE * tb + 4)
                    pe.wait_ge(gated, N_BY_ACT * tb + 1)
                    for j in range(4):
                        pe.wait_ge(raw_free, w0 + 4 * b + (j + 3))
                        pe.wait_ge(mix_done if j % 2 else sg_done, 16 * tb + 2 * b + (j // 2 + 1))
                        job(j, KD, *tile(j % 2), AH, AL,
                            wait_half=(lambda n: pe.wait_ge(ld_y[n], 32 * tb + 32)) if j == 0 else None)
                stat(JOB_STAT1 % 4, 32 * tb + 8)
                with pe.Fori(0, F_GROUPS) as fg:
                    w1 = w0 + fg * (2 * F_TILES) + TILE_MLP
                    x1 = N_XADD * tb + KD * fg
                    for f in range(F_TILES):
                        pe.wait_ge(raw_free, w1 + (f + 3))
                        pe.wait_ge(xadd, x1 + (f + 5 + 2))
                        if (JOB_MLP + f) % 4 == JOB_STAT1 % 4:
                            pe.wait_ge(r_done, 4 * tb + 1)
                        job((JOB_MLP + f) % 4, KD, *tile(f % 2), AH, AL,
                            (lambda k: pe.wait_ge(al_done, 24 * tb + (k + 1))) if f == 0 else None)
                    for m in range(KD):
                        if m % 2 == 0:
                            pe.wait_ge(raw_free, w1 + (F_TILES + m // 2 + 3))
                        if m < 4:
                            pe.wait_ge(relu_done, 32 * tb + 4 * fg + (m + 1))
                        else:
                            pe.wait_ge(xadd, x1 + (KD + m - 3 + 2))
                        operands = (JOB_MLP + F_TILES + m) % 4, F_TILES, *tile(m // 2 % 2, m % 2 * F_TILES), FH, FL
                        if m == 0:
                            job_by_parts(*operands, lambda k: pe.wait_ge(fl_done, 32 * tb + 4 * fg + (k + 1 + 2)))
                        else:
                            job(*operands)
                stat(JOB_STAT2 % 4, 32 * tb + 16)
                for m in range(KD):
                    pe.wait_ge(raw_free, w0 + (TILE_PLE + m + (3 if m < 2 else 5)))
                    if (JOB_PLE + 2 * m) % 4 == JOB_STAT2 % 4 or m == 1:
                        pe.wait_ge(r_done, 4 * tb + 2)
                    pe.wait_ge(gsc_done, 8 * tb + (m + 1))
                    job((JOB_PLE + 2 * m) % 4, KD, *tile(m % 2), AH, AL,
                        (lambda k: pe.wait_ge(al_done, 24 * tb + (8 + k + 1))) if m == 0 else None)
                    if m == 0:
                        pe.wait_ge(raw_free, w0 + (TILE_PLE + 6))
                        pe.wait_ge(pl_done, 2 * tb + 2)
                    pe.wait_ge(mix_done, 16 * tb + (KD + m + 1))
                    job((JOB_PLE + 2 * m + 1) % 4, 2, ple(FH, m), ple(FL, m), FH, FL)
                stat(JOB_STAT3 % 4, 32 * tb + 31, RB1)
                stat((JOB_STAT3 + 1) % 4, 32 * tb + 32, RB2)

                def slot_read(j):
                    if j >= 4:
                        by_act = BY_ACT[j - 4]
                        done = before(j - 4, by_act) + 1
                        if by_act:
                            pe.wait_ge(gated, N_BY_ACT * tb + (done + 1))
                        else:
                            pe.wait_ge(copied, N_BY_DVE * tb + (done + 4))

                for j in range(N_FM):
                    pe.wait_ge(raw_free, w0 + (TILE_FM + j + 3))
                    slot_read(j)
                    job((JOB_FM + j) % 4, KD, *tile(j % 2), AH, AL,
                        (lambda k: pe.wait_ge(al_done, 24 * tb + (16 + k + 1))) if j == 0 else None)
                pe.wait_ge(gl_done, 1)
                for n in range(2):
                    t = slice(n * (TB // 2), (n + 1) * (TB // 2))
                    slot_read(GI_AT + n)
                    product(ps4[(JOB_GI + n) % 4][0:8, 0], KD,
                            lambda k: ((gwh[:, k], AH[:, k, t]), (gwh[:, k], AL[:, k, t]), (gwl[:, k], AH[:, k, t]))
                            ).then_inc(job_done, 1)
                c, tiles = TM_AT, 0
                for g in range(4):
                    n = TM_COLS[g]
                    tiles += n // P
                    pe.wait_ge(raw_free, w0 + (TILE_TM + tiles + 2))
                    per = TB // P // TM_JOBS[g]
                    for j in range(TM_JOBS[g]):
                        slot_read(c)
                        out = ps4[(JOB_FM + c) % 4][:].rearrange("p a b -> p (a b)")
                        for i in range(per):
                            t = slice((j * per + i) * P, (j * per + i + 1) * P)
                            last = product(out[:, i * n:(i + 1) * n], KD,
                                           lambda k: ((AH[:, k, t], GH[g % 2][:, k, 0:n]), (AL[:, k, t], GH[g % 2][:, k, 0:n]),
                                                      (AH[:, k, t], GL[g % 2][:, k, 0:n])))
                        last.then_inc(job_done, 1)
                        c += 1


A_HEADS, A_DIM = 4, 64
A_TILES = A_HEADS * A_DIM // P
QB = 128
N_QB = SEQ // QB
WIN = 512 + QB
KT = WIN // QB
NEG = -1e30
NQ4 = 4
ROWS_AT, ROWS_STEP = 4, 2
QC = SEQ // NQ4


def attention(nc, env, d, ctx):
    sb, ps, sem = tools(nc, ctx)
    ident, eps = env["ident"], env["eps"]
    qk = sb("at_qk", [P, 2 * A_TILES, SEQ])
    z = sb("at_z", [P, A_TILES, SEQ])
    v = sb("at_v", [P, N_QB, A_HEADS * A_DIM])
    bias = sb("at_bias", [P, A_HEADS, WIN])
    gain = sb("at_gain", [P, 2])
    blk = sb("at_blk", [P, P])
    half = sb("at_half", [P, 2])
    sq = sb("at_sq", [P, 2, QC])
    lnv, rr = sb("at_ln", [P, 2, QC]), sb("at_r", [P, 2, QC])
    qs = sb("at_qs", [P, 2, 2, A_TILES, QB])
    sbv = sb("at_sb", [P, 2, WIN])
    e = sb("at_e", [P, 2, WIN])
    pT = sb("at_pT", [P, 2, KT, QB])
    mx, ng, sm, rc = (sb(f"at_{n}", [P, 2]) for n in ("mx", "ng", "sm", "rc"))
    o = sb("at_o", [P, 2, A_HEADS * A_DIM])
    om = sb("at_om", [P, 2, A_TILES, QB])
    s_ps = [ps(f"at_s_ps{i}", [P, 2, 512]) for i in range(2)]
    t_ps = ps("at_t_ps", [P, 2 * 512])
    o_ps = [ps(f"at_o_ps{i}", [P, 512]) for i in range(2)]
    x_ps = o_ps[1][:, 256:512].rearrange("p (t n) -> p t n", n=QB)
    ld_z, ld_v, ld_b, ld_g = (sem(f"at_ld_{n}") for n in ("z", "v", "b", "g"))
    ld_qk = [sem(f"at_ld_qk{k}") for k in range(2 * A_TILES)]
    blk_set, bias_set, g_done = sem("at_blk_set"), sem("at_bias_set"), sem("at_g_done")
    sq_done, ms_done, ln_done, r_done, qk_done = (sem(f"at_{n}_done") for n in ("sq", "ms", "ln", "r", "qk"))
    qs_done, s_done, b_done, n_done, e_done, t_done, p_done, pv_done, rc_done, o_done, x_done, m_done = (
        sem(f"at_{n}_done") for n in ("qs", "s", "b", "neg", "e", "t", "p", "pv", "rc", "o", "x", "m"))
    may_add, ld_cv = sem("at_may_add"), sem("at_ld_cv")
    st = [sem("at_st0"), sem("at_st1")]
    N_NORM = 2 * A_TILES * NQ4

    rows = env["rows"]

    def schedule(engine, stages, extra=None):
        def step(b, par, h, inside):
            for off, stage in stages:
                db, hh = (h + off) // A_HEADS, (h + off) % A_HEADS
                if inside:
                    stage(b + db, (par + db) % 2, hh, KT)
                elif 0 <= b + db < N_QB:
                    stage(b + db, (par + db) % 2, hh, min(b + db + 1, KT))

        for u in range(-2, 6 * A_HEADS):
            step(u // A_HEADS, u // A_HEADS % 2, u % A_HEADS, False)
            if extra:
                extra(u)
        with engine.Fori(3, N_QB // 2 - 1) as b2:
            for par in range(2):
                for h in range(A_HEADS):
                    step(2 * b2 + par, par, h, True)
        for u in range((N_QB - 2) * A_HEADS, N_QB * A_HEADS + 2):
            step(u // A_HEADS, u // A_HEADS % 2, u % A_HEADS, False)

    def need(engine, semaphore, value):
        if not isinstance(value, int) or value > 0:
            engine.wait_ge(semaphore, value)

    with nc.Block() as block:
        @block.sync
        def _(sp):
            rows.load(sp)
            sp.dma_start(gain[:], d["att_gain"]).then_inc(ld_g, 16)
            for k in range(2 * A_TILES):
                sp.dma_start(qk[:, k], d["fm"][A_QK.start + k]).then_inc(ld_qk[k], 16)
            sp.wait_ge(ld_qk[2 * A_TILES - 1], 16)
            sp.dma_start(bias[:], d["att_bias"]).then_inc(ld_b, 16)
            sp.dma_start(z[:], d["fm"][A_Z].rearrange("k p n -> p k n")).then_inc(ld_z, 16)
            sp.dma_start(v[:], d["tm"][:, 0:A_HEADS * A_DIM].rearrange("(t p) n -> p t n", p=P)).then_inc(ld_v, 16)

            sp.dma_start(env["cv_acc"][:], d["cva"].rearrange("k p n -> p k n")).then_inc(ld_cv, 16)
            sp.dma_start(env["cv_z"][:], d["fm"][C_Z].rearrange("k p n -> p k n")).then_inc(ld_cv, 16)

            def store(b, s):
                dst = d["mixed"][0:A_TILES, :, bass.ds(sp.snap(b * QB, min_val=0, max_val=SEQ - QB), QB)]
                sp.wait_ge(m_done, b + 1 + 2)
                sp.dma_start(dst.rearrange("k p n -> p k n"), om[:, s]).then_inc(st[s], 16)

            with sp.Fori(0, N_QB // 2) as b2:
                for s in range(2):
                    store(2 * b2 + s, s)
            for s in range(2):
                sp.wait_ge(st[s], 16 * (N_QB // 2))
            sp.wait_ge(ld_cv, 32)

        @block.gpsimd
        def _(pool):
            rows.resets(pool)
            pool.wait_ge(ld_g, 16)
            pool.tensor_scalar(gain[:, 0:1], gain[:, 0:1], A_DIM ** -0.5, None, ALU.mult).then_inc(g_done, 1)
            pool.sem_inc(qs_done, 2)
            for i in range(N_NORM):
                if i % NQ4 == 0:
                    pool.wait_ge(ld_qk[i // NQ4], 16)
                if i >= 2:
                    pool.wait_ge(ms_done, i - 1)
                x = qk[:, i // NQ4, i % NQ4 * QC:(i % NQ4 + 1) * QC]
                pool.tensor_tensor(sq[:, i % 2], x, x, ALU.mult).then_inc(sq_done, 1)
            pool.wait_ge(blk_set, 8)

            def queries(b, s, wait):
                if wait:
                    pool.wait_ge(s_done, A_HEADS * b - A_HEADS)
                for hh in range(2):
                    pool.tensor_tensor(qs[:, s, hh], qk[:, 0:A_TILES, bass.ds(b * QB, QB)],
                                       half[:, hh:hh + 1, None].to_broadcast([P, A_TILES, QB]), ALU.mult).then_inc(qs_done, 1)

            pool.wait_ge(qk_done, A_TILES * NQ4)
            for s in range(2):
                queries(s, s, False)
            with pool.Fori(1, N_QB // 2) as b2:
                for s in range(2):
                    queries(2 * b2 + s, s, True)

        @block.scalar
        def _(act):
            act.preload_act_table_set("natural_log_exp_and_others")
            rows.logs(act)

            for i in range(N_NORM):
                act.wait_ge(ms_done, i + 1)
                if i >= 2:
                    act.wait_ge(qk_done, i - 1)
                act.activation(lnv[:, i % 2], s_ps[i % 2][:, 0], ACT.Ln, bias=eps[:]).then_inc(ln_done, 1)
                act.wait_ge(ln_done, i + 1)
                act.activation(rr[:, i % 2], lnv[:, i % 2], ACT.Exp, scale=-0.5).then_inc(r_done, 1)

            def weigh(b, s, h, nb):
                u, i = A_HEADS * b + h, h % 2
                w = slice(WIN - nb * QB, WIN)
                act.wait_ge(n_done, u + 1)
                need(act, t_done, u - 1)
                need(act, rc_done, u - 1)
                act.activation(e[:, i, w], sbv[:, i, w], ACT.Exp, bias=ng[:, i:i + 1], accum_out=sm[:, i:i + 1]).then_inc(e_done, 1)

            def copy(b, s, h, nb):
                u = A_HEADS * b + h
                act.wait_ge(t_done, u + 1)
                need(act, pv_done, u - 1)
                act.copy(pT[:, h % 2, 0:nb], t_ps[:, 0:nb * QB].rearrange("p (t n) -> p t n", n=QB)).then_inc(p_done, 1)

            schedule(act, [(1, weigh), (0, copy)], lambda u: rows.weights(act) if u == ROWS_AT + ROWS_STEP * GateRows.N_SCANS else None)

        @block.vector
        def _(dve):
            dve.memset(om[:, 0, 0, 0:1], 0.0).then_inc(m_done, 2)
            for hh in range(2):
                part = slice(hh * A_DIM, (hh + 1) * A_DIM)
                dve.memset(blk[part, part], 1.0 / A_DIM).then_inc(blk_set, 1)
                dve.memset(blk[part, (1 - hh) * A_DIM:(2 - hh) * A_DIM], 0.0).then_inc(blk_set, 1)
                dve.memset(half[part, hh:hh + 1], 1.0).then_inc(blk_set, 1)
                dve.memset(half[part, 1 - hh:2 - hh], 0.0).then_inc(blk_set, 1)
            dve.wait_ge(m_done, 2)
            dve.wait_ge(g_done, 1)
            for i in range(N_NORM):
                t, c = i // NQ4, slice(i % NQ4 * QC, (i % NQ4 + 1) * QC)
                dve.wait_ge(r_done, i + 1)
                dve.scalar_tensor_tensor(qk[:, t, c], qk[:, t, c], gain[:, t // A_TILES:t // A_TILES + 1], rr[:, i % 2],
                                         ALU.mult, ALU.mult).then_inc(qk_done, 1)
            dve.wait_ge(ld_b, 16)
            dve.memset(bias[0:64, :, WIN - 64:WIN], NEG).then_inc(bias_set, 1)
            dve.memset(bias[64:P, :, 0:64], NEG).then_inc(bias_set, 1)
            dve.wait_ge(bias_set, 2)
            dve.wait_ge(ld_z, 16)

            def scores(b, s, h, nb):
                u, i = A_HEADS * b + h, h % 2
                w, hw = slice(WIN - nb * QB, WIN), nb * QB // 2
                two = lambda a: a.rearrange("p (a n) -> p a n", a=2)
                dve.wait_ge(s_done, u + 1)
                need(dve, e_done, u - 1)
                need(dve, n_done, u - 1)
                dve.sem_inc(may_add, 1)
                dve.tensor_tensor_reduce(two(sbv[:, i, w]), s_ps[i][:, :, 0:hw], two(bias[:, h, w]), 1.0, -3e38,
                                         ALU.add, ALU.max, accum_out=mx[:, i:i + 1]).then_inc(b_done, 1)
                dve.wait_ge(b_done, u + 1)
                dve.tensor_scalar(ng[:, i:i + 1], mx[:, i:i + 1], -1.0, None, ALU.mult).then_inc(n_done, 1)

            def invert(b, s, h, nb):
                u, i = A_HEADS * b + h, h % 2
                dve.wait_ge(e_done, u + 1)
                need(dve, o_done, u - 1)
                dve.reciprocal(rc[:, i:i + 1], sm[:, i:i + 1]).then_inc(rc_done, 1)

            def output(b, s, h, nb):
                u, i = A_HEADS * b + h, h % 2
                dve.wait_ge(rc_done, u + 1)
                dve.wait_ge(pv_done, u + 1)
                need(dve, x_done, b - 1)
                dve.tensor_scalar(o[:, s, h * A_DIM:(h + 1) * A_DIM], o_ps[i][:, h // 2 * A_DIM:(h // 2 + 1) * A_DIM],
                                  rc[:, i:i + 1], None, ALU.mult).then_inc(o_done, 1)

            def gate(b, s, h, nb):
                if h == A_HEADS - 1:
                    dve.wait_ge(x_done, b + 1)
                    need(dve, st[s], 8 * b - 8 * s)
                    dve.tensor_tensor(om[:, s], x_ps, z[:, :, bass.ds(b * QB, QB)], ALU.mult).then_inc(m_done, 1)

            def extra(u):
                i, off = divmod(u - ROWS_AT, ROWS_STEP)
                if 0 <= i < GateRows.N_SCANS and not off:
                    rows.scans(dve, i, ident)
                elif u == ROWS_AT + ROWS_STEP * GateRows.N_SCANS + 3:
                    rows.scans(dve, GateRows.N_SCANS, ident)

            schedule(dve, [(2, scores), (0, invert), (-1, output), (-2, gate)], extra)

        @block.tensor
        def _(pe):
            pe.wait_ge(blk_set, 8)
            for i in range(N_NORM):
                pe.wait_ge(sq_done, i + 1)
                if i >= 2:
                    pe.wait_ge(ln_done, i - 1)
                pe.matmul(s_ps[i % 2][:, 0], blk[:], sq[:, i % 2], start=True, stop=True).then_inc(ms_done, 1)
            pe.wait_ge(qk_done, N_NORM)
            pe.wait_ge(ld_v, 16)

            def scores(b, s, h, nb):
                u, hw = A_HEADS * b + h, nb * QB // 2
                pe.wait_ge(qs_done, 2 * b + 4)
                need(pe, b_done, u - 1)
                for n in range(2):
                    last = pe.matmul(s_ps[h % 2][:, n, 0:hw], qs[:, s, h % 2, h // 2],
                                     qk[:, A_TILES + h // 2, bass.ds((b + 1 - nb) * QB + n * hw, hw)], start=True, stop=True)
                last.then_inc(s_done, 1)

            def turn(b, s, h, nb):
                u = A_HEADS * b + h
                pe.wait_ge(e_done, u + 1)
                need(pe, p_done, u)
                for t in range(nb):
                    last = pe.transpose(t_ps[:, t * QB:(t + 1) * QB], e[:, h % 2, WIN - (nb - t) * QB:WIN - (nb - t - 1) * QB], ident[:])
                last.then_inc(t_done, 1)

            def values(b, s, h, nb):
                u = A_HEADS * b + h
                pe.wait_ge(p_done, u + 1)
                need(pe, o_done, u - 1)
                if h == 1:
                    pe.wait_ge(m_done, b + 2)
                for t in range(nb):
                    vt = v[:, bass.ds(b + 1 - nb + t, 1), h * A_DIM:(h + 1) * A_DIM].rearrange("p o n -> p (o n)")
                    last = pe.matmul(o_ps[h % 2][:, h // 2 * A_DIM:(h // 2 + 1) * A_DIM], pT[:, h % 2, t], vt,
                                     start=(t == 0), stop=(t == nb - 1))
                last.then_inc(pv_done, 1)

            def turn_output(b, s, h, nb):
                if h == A_HEADS - 1:
                    pe.wait_ge(o_done, A_HEADS * b + A_HEADS)
                    for t in range(A_TILES):
                        last = pe.transpose(x_ps[:, t], o[:, s, t * P:(t + 1) * P], ident[:])
                    last.then_inc(x_done, 1)

            schedule(pe, [(2, scores), (0, turn), (-1, values), (-2, turn_output)])


M_HEADS = 4
MC = 128
N_MC = SEQ // MC
M_SCALE = float(P) ** -0.5
M_W = M_HEADS * P
CW = P + 1


class GateRows:

    def __init__(self, nc, d, ctx):
        sb, ps, sem = tools(nc, ctx)
        H = M_HEADS
        self.d = d
        self.A, self.B, self.C, self.E, self.T, self.reset = (sb(f"m_row_{n}", [H, SEQ]) for n in "ABCETR")
        self.bif = sb("m_bif", [H, 2])
        self.mp, self.dt, self.dd = sb("m_mp", [H, N_MC]), sb("m_dt", [H, N_MC]), sb("m_dd", [H, H, N_MC])
        self.one = sb("m_one", [H, P])
        self.ld, self.a_done, self.v_done, self.spread, self.st, self.set, self.g_made = (
            sem(f"m_{n}") for n in ("ld_gates", "a_done", "v_done", "spread", "st_rows", "rst_set", "g_made"))

    def load(self, sp):
        H = M_HEADS
        sp.dma_start(self.A[:], self.d["gi"][0:H]).then_inc(self.ld, 16)
        sp.dma_start(self.B[:], self.d["gi"][H:2 * H]).then_inc(self.ld, 16)
        sp.dma_start(self.bif[:], self.d["ml_bif"]).then_inc(self.ld, 16)

    def resets(self, pool):
        pool.memset(self.reset[:], 1.0).then_inc(self.set, 1)
        pool.wait_ge(self.set, 1)
        pool.memset(self.reset[:].rearrange("p (c n) -> p c n", n=MC)[:, :, 0:1], 0.0).then_inc(self.set, 1)
        pool.memset(self.one[:], 1.0).then_inc(self.set, 1)

    def logs(self, act):
        t, a_done = self.T, self.a_done
        act.wait_ge(self.ld, 48)
        act.activation(t[:], self.B[:], ACT.Abs, bias=self.bif[:, 1:2]).then_inc(a_done, 1)
        act.wait_ge(a_done, 1)
        act.activation(t[:], t[:], ACT.Exp, scale=-1.0).then_inc(a_done, 1)
        act.wait_ge(a_done, 2)
        act.activation(t[:], t[:], ACT.Ln, bias=1.0).then_inc(a_done, 1)

    def weights(self, act):
        a_done, v_done = self.a_done, self.v_done
        act.wait_ge(v_done, 8)
        act.activation(self.B[:], self.B[:], ACT.Exp).then_inc(a_done, 1)
        act.dma_start(self.d["rows"][0], self.T[:]).then_inc(self.st, 16)
        act.activation(self.C[:], self.C[:], ACT.Exp, scale=-1.0).then_inc(a_done, 1)
        act.wait_ge(v_done, 9)
        act.activation(self.mp[:], self.dt[:], ACT.Exp).then_inc(a_done, 1)
        act.wait_ge(v_done, 10)
        act.activation(self.E[:], self.E[:], ACT.Exp).then_inc(a_done, 1)
        act.wait_ge(a_done, 4)
        act.dma_start(self.d["rows"][1], self.B[:]).then_inc(self.st, 16)

    def scans(self, dve, i, ident):
        H, v_done = M_HEADS, self.v_done
        A, B, C, E, T, mp = (v[:] for v in (self.A, self.B, self.C, self.E, self.T, self.mp))
        by_chunk = lambda v: v.rearrange("p (c n) -> p c n", n=MC)
        if i == 0:
            dve.wait_ge(self.ld, 48)
            dve.tensor_scalar(A, A, self.bif[:, 0:1], None, ALU.add).then_inc(v_done, 1)
            dve.tensor_scalar(E, B, self.bif[:, 1:2], 0.0, ALU.add, ALU.min).then_inc(v_done, 1)
        elif i == 1:
            dve.wait_ge(self.a_done, 3)
            dve.wait_ge(v_done, 2)
            dve.tensor_tensor(B, E, T, ALU.subtract).then_inc(v_done, 1)
        elif i == 2:
            dve.wait_ge(v_done, 3)
            dve.tensor_tensor_scan(C, B, A, 0.0, ALU.add, ALU.max).then_inc(v_done, 1)
        elif i == 3:
            dve.wait_ge(self.set, 3)
            dve.tensor_tensor_scan(E, self.reset[:], B, 0.0, ALU.mult, ALU.add).then_inc(v_done, 1)
        elif i == 4:
            dve.memset(mp[:, 0:1], 0.0)
            dve.wait_ge(v_done, 5)
            dve.tensor_copy(mp[:, 1:], by_chunk(C)[:, 0:N_MC - 1, MC - 1]).then_inc(v_done, 1)
            dve.tensor_tensor(T, E, C, ALU.subtract).then_inc(v_done, 1)
        elif i == 5:
            dve.wait_ge(v_done, 7)
            dve.tensor_tensor(by_chunk(B), by_chunk(T), mp[:, :, None].to_broadcast([H, N_MC, MC]), ALU.add).then_inc(v_done, 1)
            dve.tensor_tensor(self.dt[:], by_chunk(T)[:, :, MC - 1], mp, ALU.add).then_inc(v_done, 1)
        elif i == 6:
            dve.tensor_tensor(A, A, E, ALU.subtract).then_inc(self.g_made, 1)
        elif i == 7:
            dve.wait_ge(self.g_made, 1)
            dve.tensor_tensor(by_chunk(E), by_chunk(A), by_chunk(T)[:, :, MC - 1:MC].to_broadcast([H, N_MC, MC]),
                              ALU.add).then_inc(v_done, 1)
        elif i == 8:
            dve.wait_ge(self.a_done, 6)
            dve.tensor_tensor(self.dd[:], mp[:, None, :].to_broadcast([H, H, N_MC]),
                              ident[0:H, 0:H, None].to_broadcast([H, H, N_MC]), ALU.mult).then_inc(self.spread, 1)

    N_SCANS = 8


def mlstm_chunks(nc, env, d, ctx):
    sb, ps, sem = tools(nc, ctx)
    ident, eps, rows = env["ident"], env["eps"], env["rows"]
    H = M_HEADS
    tok = sb("m_tok", [P, N_MC, 3 * H])
    dec = sb("m_dec", [P, H, N_MC])
    qr = sb("m_qr", [P, 2, H, MC])
    oz = sb("m_oz", [P, 2, 2 * M_W])
    va = sb("m_va", [P, 2, H, CW])
    bc = sb("m_bc", [P, 2, 2, H, MC])
    sc = sb("m_sc", [P, 2, 4 * H])
    ks = sb("m_ks", [P, 2, H, MC])
    qp = sb("m_qp", [P, 2, H, MC])
    am = sb("m_am", [P, 2, H, MC])
    dm = sb("m_dm", [P, 2, H, MC])
    sd = sb("m_sd", [P, 2, H, MC])
    kw = sb("m_kw", [P, 2, H, P])
    hb, hm, hz = (sb(f"m_{n}", [P, 2, H, P]) for n in ("hb", "hm", "hz"))
    om = sb("m_om", [P, 2, H, MC])
    junk = sb("m_junk", [P, H, P])
    state = sb("m_state", [P, H, CW])
    mask = sb("m_mask", [P, MC])
    ad, dn, rc = (sb(f"m_{n}", [P, 2, H]) for n in ("ad", "dn", "rc"))
    ssq, ln, rr = (sb(f"m_{n}", [P, 2, H]) for n in ("ssq", "ln", "rr"))
    gain = sb("m_gain", [P, H])
    s_ps = [ps(f"m_s_ps{i}", [P, H, MC]) for i in range(2)]
    kt_ps, x_ps = ps("m_kt_ps", [P, H, P]), ps("m_x_ps", [P, H, P])
    n_ps, u_ps = ps("m_n_ps", [P, 2, 512]), ps("m_u_ps", [P, 2, 512])
    head = lambda v, h: v[:, h // 2, h % 2 * CW:(h % 2 + 1) * CW]
    heads = lambda v: v[:, :, 0:2 * CW].rearrange("p a (b n) -> p a b n", n=CW)
    two = lambda v: v.rearrange("p (a b) n -> p a b n", a=2)
    ld_g, va_ld, bc_ld = sem("m_ld_gain"), [sem("m_va_ld0"), sem("m_va_ld1")], [sem("m_bc_ld0"), sem("m_bc_ld1")]
    st = [sem("m_st0"), sem("m_st1")]
    kq_ld, oz_ld = [sem("m_kq_ld0"), sem("m_kq_ld1")], [sem("m_oz_ld0"), sem("m_oz_ld1")]
    turned, tok_done = sem("m_turned"), sem("m_tok_done")
    names = ("qp sc am dm s kt sd kw num upd c ad den rec h hm sq rn r h2 h3 x om").split()
    S = {n: sem(f"m_{n}_done") for n in names}
    (qp_done, sc_done, am_done, dm_done, s_done, kt_done, sd_done, kw_done, num_done, upd_done, c_done,
     ad_done, den_done, rec_done, h_done, hm_done, sq_done, rn_done, r_done, h2_done, h3_done, x_done, om_done) = S.values()
    ready, va_set, mask_set = sem("m_ready"), sem("m_va_set"), sem("m_mask_set")

    def schedule(engine, stages):
        def step(c, par, inside):
            for off, stage in stages:
                if inside or 0 <= c + off < N_MC:
                    stage(c + off, (par + off) % 2)

        for c in range(-2, 4):
            step(c, c % 2, False)
        with engine.Fori(2, N_MC // 2 - 1) as i:
            for par in range(2):
                step(2 * i + par, par, True)
        for c in range(N_MC - 2, N_MC + 4):
            step(c, c % 2, False)

    with nc.Block() as block:
        @block.sync
        def _(sp):
            for s in range(2):
                sp.sem_inc(st[s], 16)
            sp.dma_start(gain[:], d["ml_gain"]).then_inc(ld_g, 16)

            sp.wait_ge(rows.st, 32)

            def tokens(c):
                return bass.ds(c * MC if isinstance(c, int) else sp.snap(c * MC, min_val=0, max_val=SEQ - MC), MC)

            def load_values(c, s):
                src = d["tm"][tokens(c), 256:256 + M_W].rearrange("p (h n) -> p h n", h=H)
                sp.wait_ge(num_done, c + 1)
                sp.sem_inc(ready, 1)
                sp.wait_ge(upd_done, c + 1)
                sp.sem_inc(ready, 1)
                sp.dma_start(va[:, s, :, 0:P], src).then_inc(va_ld[s], 16)

            def load_keys(c, s):
                src_k, src_q = (d["fm"][M_QK.start + i * H:M_QK.start + (i + 1) * H, :, tokens(c)].rearrange("k p n -> p k n") for i in (1, 0))
                sp.wait_ge(kt_done, c + 1)
                sp.sem_inc(ready, 1)
                sp.dma_start(ks[:, s], src_k).then_inc(kq_ld[s], 16)
                sp.wait_ge(qp_done, c + 1)
                sp.sem_inc(ready, 1)
                sp.dma_start(qr[:, s], src_q).then_inc(kq_ld[s], 16)

            def load_gates(c, s):
                src = d["tm"][tokens(c), 256 + M_W:256 + 3 * M_W]
                sp.wait_ge(h3_done, c + 1)
                sp.sem_inc(ready, 1)
                sp.dma_start(oz[:, s], src).then_inc(oz_ld[s], 16)

            def load_rows(c, s):
                rows = d["rows"][:, :, tokens(c)].partition_broadcast(P)
                sp.wait_ge(am_done, c + 1)
                sp.sem_inc(ready, 1)
                sp.wait_ge(qp_done, c + 1)
                sp.sem_inc(ready, 1)
                sp.dma_start(bc[:, s], rows).then_inc(bc_ld[s], 16)

            def store(c, s):
                dst = d["mixed"][2:2 + H, :, tokens(c)].rearrange("k p n -> p k n")
                sp.wait_ge(om_done, c + 1)
                sp.dma_start(dst, om[:, s]).then_inc(st[s], 16)

            def step(c, par, inside):
                for off, transfer in ((2, load_values), (3, load_keys), (0, load_gates), (4, load_rows), (-3, store)):
                    if inside or 0 <= c + off < N_MC:
                        transfer(c + off, (par + off) % 2)

            for c in range(-4, 4):
                step(c, c % 2, False)
            with sp.Fori(2, N_MC // 2 - 2) as i:
                for par in range(2):
                    step(2 * i + par, par, True)
            for c in range(N_MC - 4, N_MC + 3):
                step(c, c % 2, False)
            for s in range(2):
                sp.wait_ge(st[s], 16 + 16 * (N_MC // 2))

        @block.gpsimd
        def _(pool):
            pool.memset(mask[:], 0.0).then_inc(mask_set, 1)
            pool.wait_ge(mask_set, 1)
            pool.affine_select(out=mask[:], in_=mask[:], compare_op=ALU.is_ge, fill=NEG, base=0,
                               pattern=[[1, MC]], channel_multiplier=-1).then_inc(mask_set, 1)
            pool.sem_inc(qp_done, 2)
            pool.sem_inc(hm_done, 2)
            pool.sem_inc(h3_done, 2)

            pool.wait_ge(tok_done, 3)

            def scalars(c, s):
                pool.wait_ge(kw_done, c + 1)
                pool.wait_ge(den_done, c + 1)
                pool.tensor_copy(sc[:, s, 0:3 * H], tok[:, bass.ds(c, 1)].rearrange("p o n -> p (o n)")).then_inc(sc_done, 1)
                pool.tensor_copy(sc[:, s, 3 * H:], dec[:, :, bass.ds(c, 1)].rearrange("p h o -> p (h o)")).then_inc(sc_done, 1)

            def queries(c, s):
                pool.wait_ge(bc_ld[s], 8 * c + (16 - 8 * s))
                pool.wait_ge(kq_ld[s], 16 * c + (32 - 16 * s))
                pool.wait_ge(num_done, c + 1)
                pool.tensor_tensor(qp[:, s], qr[:, s], bc[:, s, 1], ALU.mult).then_inc(qp_done, 1)

            def gate_o(c, s):
                pool.wait_ge(h_done, c + 2)
                pool.wait_ge(h2_done, c + 1)
                pool.wait_ge(oz_ld[s], 8 * c + (16 - 8 * s))
                pool.tensor_tensor(hm[:, s], hb[:, s], oz[:, s, 0:M_W].rearrange("p (h n) -> p h n", h=H),
                                   ALU.mult).then_inc(hm_done, 1)

            def gate_z(c, s):
                pool.wait_ge(h2_done, c + 3)
                pool.tensor_tensor(hz[:, s], hz[:, s], oz[:, s, M_W:].rearrange("p (h n) -> p h n", h=H),
                                   ALU.mult).then_inc(h3_done, 1)

            schedule(pool, [(1, scalars), (1, queries), (-1, gate_o), (-2, gate_z)])

        @block.scalar
        def _(act):
            act.preload_act_table_set("natural_log_exp_and_others")
            act.sem_inc(dm_done, 2)
            act.sem_inc(kw_done, 2)

            def weights(c, s):
                act.wait_ge(am_done, c + 3)
                act.wait_ge(sc_done, 2 * c + 2)
                act.wait_ge(sd_done, c + 1)
                for h in range(H):
                    step = act.activation(dm[:, s, h], am[:, s, h], ACT.Exp, bias=sc[:, s, h:h + 1])
                step.then_inc(dm_done, 1)

            def weighted_keys(c, s):
                act.wait_ge(kt_done, c + 3)
                act.wait_ge(upd_done, c + 1)
                for h in range(H):
                    step = act.activation(kw[:, s, h], kt_ps[:, h], ACT.Copy, scale=sc[:, s, 2 * H + h:2 * H + h + 1])
                step.then_inc(kw_done, 1)

            def denominators(c, s):
                act.wait_ge(num_done, c + 3)
                act.wait_ge(den_done, c + 1)
                act.activation(two(ad[:, s, :, None]), heads(n_ps)[:, :, :, P:CW], ACT.Abs).then_inc(ad_done, 1)

            def rms(c, s):
                act.wait_ge(hm_done, c + 3)
                for h in range(H):
                    step = act.activation(junk[:, h], hm[:, s, h], ACT.Square, accum_out=ssq[:, s, h:h + 1])
                step.then_inc(sq_done, 1)
                act.wait_ge(sq_done, c + 1)
                act.activation(ln[:, s], ssq[:, s], ACT.Ln, bias=eps[:], scale=1.0 / P).then_inc(rn_done, 1)
                act.wait_ge(rn_done, c + 1)
                act.activation(rr[:, s], ln[:, s], ACT.Exp, scale=-0.5).then_inc(r_done, 1)

            schedule(act, [(1, weights), (0, denominators), (1, weighted_keys), (-1, rms)])

        @block.vector
        def _(dve):
            for n in ("am", "sd", "den", "h2"):
                dve.sem_inc(S[n], 2)
            dve.memset(va[:, :, :, P:CW], 1.0).then_inc(va_set, 1)
            dve.memset(state[:], 0.0).then_inc(c_done, 1)
            dve.sem_inc(h_done, 1)

            def exponents(c, s):
                dve.wait_ge(bc_ld[s], 8 * c + (16 - 8 * s))
                dve.wait_ge(dm_done, c + 1)
                dve.tensor_tensor(am[:, s], bc[:, s, 0], mask[:, None, :].to_broadcast([P, H, MC]), ALU.add).then_inc(am_done, 1)

            def scores(c, s):
                dve.wait_ge(s_done, c + 1)
                dve.wait_ge(dm_done, c + 3)
                dve.wait_ge(num_done, c + 1)
                dve.scalar_tensor_tensor(sd[:, s], s_ps[s][:], M_SCALE, dm[:, s], ALU.mult, ALU.mult).then_inc(sd_done, 1)

            def quotient(c, s):
                dve.wait_ge(ad_done, c + 1)
                dve.tensor_tensor(dn[:, s], ad[:, s], sc[:, s, H:2 * H], ALU.max).then_inc(den_done, 1)
                dve.wait_ge(den_done, c + 3)
                dve.reciprocal(rc[:, s], dn[:, s]).then_inc(rec_done, 1)
                dve.wait_ge(rec_done, c + 1)
                dve.wait_ge(hm_done, c + 1)
                dve.tensor_tensor(two(hb[:, s]), heads(n_ps)[:, :, :, 0:P],
                                  two(rc[:, s, :, None]).to_broadcast([P, 2, 2, P]), ALU.mult).then_inc(h_done, 1)

            def new_state(c, s):
                dve.wait_ge(upd_done, c + 3)
                dve.wait_ge(sc_done, 2 * c + 2)
                dve.wait_ge(c_done, c + 1)
                for h in range(H):
                    step = dve.scalar_tensor_tensor(state[:, h], state[:, h], sc[:, s, 3 * H + h:3 * H + h + 1], head(u_ps, h),
                                                    ALU.mult, ALU.add)
                step.then_inc(c_done, 1)

            def normalise(c, s):
                dve.wait_ge(r_done, c + 1)
                dve.wait_ge(x_done, c + 1)
                dve.tensor_tensor(hz[:, s], hm[:, s], rr[:, s, :, None].to_broadcast([P, H, P]), ALU.mult).then_inc(h2_done, 1)

            def output(c, s):
                dve.wait_ge(x_done, c + 3)
                dve.wait_ge(st[s], 8 * c + (16 - 8 * s))
                dve.tensor_tensor(om[:, s], x_ps[:], gain[:, :, None].to_broadcast([P, H, MC]), ALU.mult).then_inc(om_done, 1)

            dve.wait_ge(ld_g, 16)
            dve.wait_ge(mask_set, 2)
            dve.wait_ge(turned, 2)
            t = x_ps[:].rearrange("p a b -> p (a b)")[:, 0:3 * H * N_MC].rearrange("p (c n) -> p c n", n=3 * H)
            dve.tensor_copy(tok[:, :, 0:2 * H], t[:, :, 0:2 * H]).then_inc(tok_done, 1)
            dve.tensor_scalar(tok[:, :, 2 * H:], t[:, :, 2 * H:], M_SCALE, None, ALU.mult).then_inc(tok_done, 1)
            dve.tensor_copy(dec[:], kt_ps[:].rearrange("p a b -> p (a b)")[:, 0:H * N_MC].rearrange("p (h c) -> p h c", h=H)).then_inc(tok_done, 1)
            schedule(dve, [(-2, normalise), (2, exponents), (0, new_state), (0, quotient), (1, scores), (-4, output)])

        @block.tensor
        def _(pe):
            for n in ("kt", "num", "upd", "x"):
                pe.sem_inc(S[n], 2)
            pe.wait_ge(va_set, 1)
            pe.wait_ge(rows.spread, 1)
            pe.wait_ge(rows.a_done, 7)
            pe.wait_ge(rows.set, 3)
            tok_ps = x_ps[:].rearrange("p a b -> p (a b)")
            for c in range(N_MC):
                for i, r in enumerate((rows.A, rows.C, rows.E)):
                    at = (3 * c + i) * H
                    last = pe.transpose(tok_ps[:, at:at + H], r[:, c * MC:(c + 1) * MC], ident[0:H, 0:H])
            last.then_inc(turned, 1)
            pe.matmul(kt_ps[:].rearrange("p a b -> p (a b)")[:, 0:H * N_MC], rows.one[:], rows.dd[:].rearrange("p h c -> p (h c)"),
                      start=True, stop=True).then_inc(turned, 1)
            pe.wait_ge(tok_done, 3)

            def key_products(c, s):
                pe.wait_ge(kq_ld[s], 16 * c + (32 - 16 * s))
                pe.wait_ge(sd_done, c + 1)
                for h in range(H):
                    last = pe.matmul(s_ps[s][:, h], ks[:, s, h], qr[:, s, h], start=True, stop=True)
                last.then_inc(s_done, 1)
                pe.wait_ge(kw_done, c + 2)
                for h in range(H):
                    last = pe.transpose(kt_ps[:, h], ks[:, s, h], ident[:])
                last.then_inc(kt_done, 1)

            def numerators(c, s):
                pe.wait_ge(va_ld[s], 8 * c + (16 - 8 * s))
                pe.wait_ge(sd_done, c + 3)
                pe.wait_ge(qp_done, c + 3)
                pe.wait_ge(c_done, c + 1)
                pe.wait_ge(h_done, c + 1)
                for h in range(H):
                    pe.matmul(head(n_ps, h), sd[:, s, h], va[:, s, h], start=True, stop=False)
                    last = pe.matmul(head(n_ps, h), qp[:, s, h], state[:, h], start=False, stop=True)
                last.then_inc(num_done, 1)
                pe.wait_ge(kw_done, c + 3)
                for h in range(H):
                    last = pe.matmul(head(u_ps, h), kw[:, s, h], va[:, s, h], start=True, stop=True)
                last.then_inc(upd_done, 1)

            def turn_output(c, s):
                pe.wait_ge(h3_done, c + 3)
                pe.wait_ge(om_done, c) if not isinstance(c, int) or c > 0 else None
                for h in range(H):
                    last = pe.transpose(x_ps[:, h], hz[:, s, h], ident[:])
                last.then_inc(x_done, 1)

            schedule(pe, [(0, numerators), (1, key_products), (-3, turn_output)])


C_TILES = 2
N_MIXED = KD - C_TILES
CN = 512
N_CN = SEQ // CN
OT = P
N_OT = SEQ // OT


def finish(nc, env, d, ctx):
    sb, ps, sem = tools(nc, ctx)
    ident, eps = env["ident"], env["eps"]
    acc, z = env["cv_acc"], env["cv_z"]
    par = sb("cv_par", [P, 2, C_TILES])
    ones = sb("cv_ones", [P, P])
    sq = sb("cv_sq", [P, 2, C_TILES, CN])
    ln, rr = sb("cv_ln", [P, 2, CN]), sb("cv_rr", [P, 2, CN])
    wr = sb("o_wr", [P, KD, D])
    wh, wl = sb("o_wh", [P, KD, D], F32R), sb("o_wl", [P, KD, D], F32R)
    m = sb("o_m", [P, 2, N_MIXED, OT])
    mh, ml = sb("o_mh", [P, 2, KD, OT], F32R), sb("o_ml", [P, 2, KD, OT], F32R)
    x = sb("o_x", [P, 2, KD, OT])
    y = sb("o_y", [P, 2, D])
    y_ps = [ps(f"o_y_ps{i}", [P, 2, D // 2]) for i in range(2)]
    x_ps = [ps(f"o_x_ps{i}", [P, 2, D // 2]) for i in range(2)]
    m_ps, v_ps = x_ps
    ld_p, ones_set, mean, xc_done, sq_done, var, ln_done, r_done, y_norm, s_done, out_done = (
        sem(f"cv_{n}") for n in "ld_p ones_set mean xc_done sq_done var ln_done r_done y_norm s_done out_done".split())
    ld_w = [sem(f"o_ld_w{k}") for k in range(KD)]
    ld_m, ld_x, st = ([sem(f"o_{n}{s}") for s in range(2)] for n in ("ld_m", "ld_x", "st"))
    wh_done, wl_done, wh2_done, wl2_done, mh_done, ml_done, y_done, add_done, turned, ready, xs_copied = (
        sem(f"o_{n}") for n in ("wh_done", "wl_done", "wh2_done", "wl2_done", "mh_done", "ml_done", "y_done", "add_done", "turned", "ready", "xs_copied"))

    with nc.Block() as block:
        @block.sync
        def _(sp):
            for s in range(2):
                sp.sem_inc(st[s], 16)
            sp.dma_start(par[:], d["cv_par"]).then_inc(ld_p, 16)
            for k in range(KD):
                sp.dma_start(wr[:, k], d["w_out"][k * P:(k + 1) * P]).then_inc(ld_w[k], 16)

            def load(c, s):
                at = bass.ds(c * OT if isinstance(c, int) else sp.snap(c * OT, min_val=0, max_val=SEQ - OT), OT)
                src_m, src_x = (d[n][:, :, at].rearrange("k p n -> p k n") for n in ("mixed", "x2"))
                sp.wait_ge(ml_done, c + 1)
                sp.sem_inc(ready, 1)
                sp.dma_start(m[:, s], src_m).then_inc(ld_m[s], 16)
                sp.wait_ge(turned, c + 1)
                sp.sem_inc(ready, 1)
                sp.dma_start(x[:, s], src_x).then_inc(ld_x[s], 16)

            def store(c, s):
                dst = d["out"][bass.ds(c * OT if isinstance(c, int) else sp.snap(c * OT, min_val=0, max_val=SEQ - OT), OT)]
                sp.wait_ge(add_done, c + 1 + 2)
                sp.sem_inc(ready, 1)
                sp.dma_start(dst, y[:, s]).then_inc(st[s], 16)

            for c in range(2):
                load(c, c)
            with sp.Fori(0, N_OT // 2 - 1) as i:
                for s in range(2):
                    load(2 * i + (2 + s), s)
                    store(2 * i + s, s)
            for s in range(2):
                store(N_OT - 2 + s, s)
            for s in range(2):
                sp.wait_ge(st[s], 16 + 16 * (N_OT // 2))

        @block.scalar
        def _(act):
            def square(i):
                act.wait_ge(xc_done, C_TILES * (i + 1))
                if i >= 2:
                    act.wait_ge(var, i - 1)
                act.activation(sq[:, i % 2], acc[:, :, i * CN:(i + 1) * CN], ACT.Square).then_inc(sq_done, 1)

            def weights(k):
                act.wait_ge(ld_w[k], 16)
                act.copy(wh[:, k], wr[:, k]).then_inc(wh_done, 1)

            def silu(i):
                at = slice(i * CN, (i + 1) * CN)
                for t in range(C_TILES):
                    act.activation(acc[:, t, at], acc[:, t, at], ACT.Silu, bias=par[:, 1, t:t + 1],
                                   scale=par[:, 0, t:t + 1]).then_inc(s_done, 1)

            def split(c, s):
                at = slice(c * OT, (c + 1) * OT) if isinstance(c, int) else bass.ds(c * OT, OT)
                act.wait_ge(ld_m[s], 8 * c + (16 - 8 * s))
                act.wait_ge(y_done, c + 1)
                act.copy(mh[:, s, 0:N_MIXED], m[:, s])
                act.copy(mh[:, s, N_MIXED:], acc[:, :, at]).then_inc(mh_done, 1)

            act.preload_act_table_set("natural_log_exp_and_others")
            for i in range(-1, N_CN):
                if i + 1 < N_CN:
                    square(i + 1)
                if i >= 0:
                    act.wait_ge(var, i + 1)
                    if i >= 2:
                        act.wait_ge(y_norm, C_TILES * (i - 1))
                    act.activation(ln[:, i % 2], v_ps[:, i % 2], ACT.Ln, bias=eps[:]).then_inc(ln_done, 1)
                    act.wait_ge(ln_done, i + 1)
                    act.activation(rr[:, i % 2], ln[:, i % 2], ACT.Exp, scale=-0.5).then_inc(r_done, 1)
                    weights(i)
            act.wait_ge(ld_p, 16)
            act.wait_ge(y_norm, C_TILES * N_CN)
            silu(0)
            act.wait_ge(out_done, C_TILES)
            for s in range(2):
                split(s, s)
            for i in range(1, N_CN):
                silu(i)
            act.wait_ge(out_done, C_TILES * N_CN)
            with act.Fori(1, N_OT // 2) as i:
                for s in range(2):
                    split(2 * i + s, s)

        @block.gpsimd
        def _(pool):
            pool.memset(ones[:], 1.0 / (C_TILES * P)).then_inc(ones_set, 1)
            pool.sem_inc(ml_done, 2)
            for k in range(N_CN):
                pool.wait_ge(wh_done, k + 1)
                pool.tensor_tensor(wl[:, k], wr[:, k], wh[:, k].bitcast(F32), ALU.subtract).then_inc(wl_done, 1)

            def split(c, s):
                pool.wait_ge(mh_done, c + 1)
                pool.tensor_tensor(ml[:, s, 0:N_MIXED], m[:, s], mh[:, s, 0:N_MIXED].bitcast(F32), ALU.subtract)
                pool.tensor_tensor(ml[:, s, N_MIXED:], acc[:, :, bass.ds(c * OT, OT)], mh[:, s, N_MIXED:].bitcast(F32),
                                   ALU.subtract).then_inc(ml_done, 1)

            with pool.Fori(0, N_OT // 2) as i:
                for s in range(2):
                    split(2 * i + s, s)

        @block.vector
        def _(dve):
            dve.sem_inc(add_done, 2)

            def weights(k, n):
                dve.wait_ge(ld_w[k], 16)
                dve.tensor_copy(wh[:, k], wr[:, k]).then_inc(wh2_done, 1)
                dve.wait_ge(wh2_done, n + 1)
                dve.tensor_tensor(wl[:, k], wr[:, k], wh[:, k].bitcast(F32), ALU.subtract).then_inc(wl2_done, 1)

            for i in range(N_CN + 1):
                at, prev = slice(i * CN, (i + 1) * CN), slice((i - 1) * CN, i * CN)
                if i < N_CN:
                    dve.wait_ge(mean, i + 1)
                    for t in range(C_TILES):
                        dve.tensor_tensor(acc[:, t, at], acc[:, t, at], m_ps[:, i % 2], ALU.subtract).then_inc(xc_done, 1)
                if i:
                    dve.wait_ge(r_done, i)
                    dve.wait_ge(xc_done, C_TILES * i)
                    for t in range(C_TILES):
                        dve.tensor_tensor(acc[:, t, prev], acc[:, t, prev], rr[:, (i - 1) % 2], ALU.mult).then_inc(y_norm, 1)
                    if i < N_CN:
                        weights(N_CN + i, i - 1)
            weights(N_CN, KD - N_CN - 1)
            for i in range(N_CN):
                at = slice(i * CN, (i + 1) * CN)
                for t in range(C_TILES):
                    dve.wait_ge(s_done, C_TILES * i + t + 1)
                    dve.tensor_tensor(acc[:, t, at], acc[:, t, at], z[:, t, at], ALU.mult).then_inc(out_done, 1)

            def add(c, s):
                dve.wait_ge(turned, c + 1 + 2)
                dve.wait_ge(st[s], 8 * c + (16 - 8 * s))
                ys = y[:, s].rearrange("p (a n) -> p a n", a=2)
                dve.tensor_copy(ys, x_ps[s][:]).then_inc(xs_copied, 1)
                dve.wait_ge(y_done, c + 1 + 2)
                dve.wait_ge(xs_copied, c + 1)
                dve.tensor_tensor(ys, ys, y_ps[s][:], ALU.add).then_inc(add_done, 1)

            with dve.Fori(0, N_OT // 2) as i:
                for s in range(2):
                    add(2 * i + s, s)

        @block.tensor
        def _(pe):
            pe.sem_inc(y_done, 2)
            pe.sem_inc(turned, 2)
            pe.wait_ge(ones_set, 1)
            for i in range(N_CN + 1):
                if i < N_CN:
                    if i >= 2:
                        pe.wait_ge(xc_done, C_TILES * (i - 1))
                    for t in range(C_TILES):
                        last = pe.matmul(m_ps[:, i % 2], ones[:], acc[:, t, i * CN:(i + 1) * CN], start=(t == 0), stop=(t == C_TILES - 1))
                    last.then_inc(mean, 1)
                if i:
                    pe.wait_ge(sq_done, i)
                    if i >= 3:
                        pe.wait_ge(ln_done, i - 2)
                    for t in range(C_TILES):
                        last = pe.matmul(v_ps[:, (i - 1) % 2], ones[:], sq[:, (i - 1) % 2, t], start=(t == 0), stop=(t == C_TILES - 1))
                    last.then_inc(var, 1)
            pe.wait_ge(ln_done, N_CN)
            pe.wait_ge(xc_done, C_TILES * N_CN)

            def step(c, s, first):
                pe.wait_ge(ld_x[s], 8 * c + (16 - 8 * s))
                pe.wait_ge(add_done, c + 1)
                for k in range(KD):
                    last = pe.transpose(x_ps[s][:, k // 4, k % 4 * P:(k % 4 + 1) * P], x[:, s, k], ident[:])
                last.then_inc(turned, 1)
                if first:
                    pe.wait_ge(wl_done, N_CN)
                    pe.wait_ge(wl2_done, KD - N_CN)
                pe.wait_ge(ml_done, c + 1 + 2)
                for n in range(2):
                    cols = slice(n * (D // 2), (n + 1) * (D // 2))
                    for k in range(KD):
                        for i, (l, r) in enumerate(((mh, wh), (ml, wh), (mh, wl))):
                            last = pe.matmul(y_ps[s][:, n], l[:, s, k], r[:, k, cols], start=(k == 0 and i == 0),
                                             stop=(k == KD - 1 and i == 2))
                last.then_inc(y_done, 1)

            for s in range(2):
                step(s, s, s == 0)
            with pe.Fori(1, N_OT // 2) as i:
                for s in range(2):
                    step(2 * i + s, s, False)


def layouts(a):
    import numpy as np
    c = np.ascontiguousarray
    x = a["x"][0]
    pair = lambda v: v.reshape(NP, 2 * 64, *v.shape[2:]).swapaxes(0, 1)
    out = {}
    out["x_chunk"] = c(x.reshape(NCH, T, D))
    out["x_group"] = c(x.reshape(NCH, 2, S8, 2 * NP, H).transpose(2, 4, 1, 3, 0).reshape(P, 2, 2 * NP, NCH))
    dt = np.repeat(a["ssm_log_dt"][0][:, None], 64, 1)
    out["s5_prm"] = c(np.stack([pair(a["ssm_lam_re"][0]), pair(a["ssm_lam_im"][0]), pair(dt)], 1))
    cT = lambda v: pair(v.swapaxes(1, 2))
    out["s5_bc"] = c(np.stack([pair(a["ssm_b_re"][0]), pair(a["ssm_b_im"][0]),
                               cT(a["ssm_c_re"][0]), cT(a["ssm_c_im"][0])], 1))
    g = a["norm_mix"][0].reshape(NP, 2, 1, H)
    out["s5_gain"] = c(np.repeat(g, 64, 2).reshape(NP, P, H).swapaxes(0, 1))
    out["s5_skip"] = c(np.stack([a["ssm_d"][0].reshape(NP, 2 * H).T, a["norm_mix"][0].reshape(NP, 2 * H).T], 1))
    return out


def tiles(w, cols, k_tiles=None):
    import numpy as np
    w = w[:, cols]
    k = w.shape[0] // P
    return np.ascontiguousarray(w.reshape(k, P, -1, P).transpose(2, 1, 0, 3).reshape(-1, P, k * P))


FM_COLS = [(3848, 4104), (3592, 3848), (4104, 4360), (768, 1024), (1024, 2048), (0, 512)]
TM_SRC = [(512, 768), (2048, 3584)]
GI_COLS = (3584, 3592)


def layouts2(a):
    import numpy as np
    c = np.ascontiguousarray
    out = {}
    by_feat = lambda v: c(v.T.reshape(-1, P, SEQ))
    out["x_feat"], out["p_feat"] = by_feat(a["x"][0]), by_feat(a["p"][0, 0])
    out["gains"] = c(np.stack([a[k].reshape(KD, P).T for k in ("norm_ffn", "norm_ple", "norm_final", "norm_g_2")], 1))
    glu, w1, w2 = a["ssm_w_glu"][0], a["mlp_w1"][0], a["mlp_w2"][0]
    order = lambda spans: np.concatenate([np.arange(*s) for s in spans])
    glu_t = tiles(glu, slice(None))
    parts = [glu_t[i] for m in range(KD) for i in (KD + m, m)]
    w1_t = tiles(w1, slice(None))
    w2_t = tiles(w2, slice(None)).reshape(KD // 2, 2, P, F_GROUPS, F_TILES * P)
    for fg in range(F_GROUPS):
        parts += [w1_t[fg * F_TILES + f] for f in range(F_TILES)]
        parts += [w2_t[m2, :, :, fg].transpose(1, 0, 2).reshape(P, -1) for m2 in range(KD // 2)]
    gate_t, ple_t = tiles(a["ple_gate_w"][0], slice(None)), tiles(a["ple_w"][0], slice(None))
    packed = [ple_t[4 * i:4 * i + 4].transpose(1, 0, 2).reshape(P, -1) for i in range(2)]
    parts += [gate_t[0], gate_t[1], *packed, *gate_t[2:]]
    w_in = a["w_in_2"][0]
    parts += list(tiles(w_in, order(FM_COLS))) + list(tiles(w_in, order(TM_SRC)))
    out["wall"] = c(np.stack(parts))
    out["w_gi"] = c(w_in[:, GI_COLS[0]:GI_COLS[1]].reshape(KD, P, 8).transpose(1, 0, 2))
    return out


def layouts3(a):
    import numpy as np
    c = np.ascontiguousarray
    out = {}
    out["att_gain"] = c(np.stack([np.tile(a[k][0], P // A_DIM) for k in ("att_q_g_2", "att_k_g_2")], 1))
    rel = np.clip(np.arange(QB)[:, None] - np.arange(WIN)[None, :] + (WIN - QB), -128, 128) + 128
    out["att_bias"] = c(a["att_rel_bias_2"][0][:, rel].swapaxes(0, 1))
    per = lambda v, n: v.reshape(*v.shape[:-1], n, P)
    out["ml_cw"] = c(per(a["ml_qk_conv_w_2"][0], 2 * M_HEADS).transpose(2, 1, 0))
    out["ml_cb"] = c(per(a["ml_qk_conv_b_2"][0], 2 * M_HEADS).T)
    out["ml_bif"] = c(np.stack([a["ml_b_i_2"][0], a["ml_b_f_2"][0]], 1))
    out["ml_gain"] = c(per(a["ml_out_g_2"][0], M_HEADS).T)
    out["cv_w"] = c(per(a["cv_dw_w_2"][0], C_TILES).transpose(2, 1, 0))
    out["cv_par"] = c(np.stack([per(a[k][0], C_TILES).T for k in ("cv_ln_g_2", "cv_ln_b_2")], 1))
    out["cv_b"] = c(per(a["cv_dw_b_2"][0], C_TILES).T)
    out["w_out"] = c(a["w_out_2"][0])
    return out


def scratch(nc, d):
    shapes = {
        "ca": (P, NQ, 2 * QP * (T + 1) * H), "z": (1, 2 * NP * H, (S8 - 1) * H + T * H),
        "y_hi": (KD, P, SEQ), "y_lo": (KD, P, SEQ),
        "x2": (KD, P, SEQ),
        "fm": (N_FM, P, SEQ), "cva": (2, P, SEQ), "gi": (2 * M_HEADS, SEQ), "tm": (SEQ, sum(TM_COLS)),
        "rows": (2, M_HEADS, SEQ), "mixed": (N_MIXED, P, SEQ),
    }
    for name, shape in shapes.items():
        if name not in d:
            d[name] = nc.dram_tensor(name + "_scratch", shape, F32).ap()


def program(nc, d):
    scratch(nc, d)
    env = {}
    with ExitStack() as ctx:
        constants(nc, env, ctx)
        s5_stage(nc, env, d)
        with ExitStack() as c:
            dense(nc, env, d, c)
        with ExitStack() as held:
            for name in ("cv_acc", "cv_z"):
                env[name] = held.enter_context(nc.sbuf_tensor(name, [P, 2, SEQ], F32, side="right"))
            with ExitStack() as mixers:
                env["rows"] = GateRows(nc, d, mixers)
                for stage in (attention, mlstm_chunks):
                    with ExitStack() as c:
                        stage(nc, env, d, c)
            with ExitStack() as c:
                finish(nc, env, d, c)


def kernel(**inputs):
    import numpy as np
    import concourse.bacc as bacc
    from concourse.bass_utils import run_bass_kernel_spmd
    a = {k: np.asarray(v) for k, v in inputs.items()}
    arrays = {"in_" + k: v for part in (layouts, layouts2, layouts3) for k, v in part(a).items()}
    nc = bacc.Bacc("TRN2", target_bir_lowering=False, num_devices=1)
    d = {k[3:]: nc.dram_tensor(k, v.shape, F32, kind="ExternalInput").ap() for k, v in arrays.items()}
    d["out"] = nc.dram_tensor("out", (SEQ, D), F32, kind="ExternalOutput").ap()
    program(nc, d)
    r = run_bass_kernel_spmd(nc, [arrays], core_ids=[0])
    return r.results[0]["out"].reshape(1, SEQ, D)
```
